# Optimizing a Trainium2 kernel written in Bass

```python
import jax
import jax.numpy as jnp
from jax import lax
import numpy as np
import math
import jax, jax.numpy as jnp

D_MODEL = 1024
BATCH = 1
SEQ = 512
DEPTH = 1

HEAD_DIM = 64
N_HEADS_A = 4
N_HEADS_C = 4
N_HEADS_D = 4
CONV_CH = 4 * HEAD_DIM
CONV_K = 3
MIX_WIDTH = (N_HEADS_A + N_HEADS_C + N_HEADS_D) * HEAD_DIM + CONV_CH
N_GROUPS = MIX_WIDTH // HEAD_DIM
BLOCK = 128
CMP_LEN = 32
CMP_STRIDE = 16
CMP_HIDDEN = 256
SEL_BLOCK = 64
N_SELECT = 16
NSA_WINDOW = 512
N_NSA_BRANCH = 3
DILATED_CONFIGS = ((128, 1), (512, 4), (2048, 16))
D_FF = -(-(8 * D_MODEL) // (3 * 256)) * 256
A_COLS = N_HEADS_A * HEAD_DIM + 6 * HEAD_DIM + N_NSA_BRANCH * N_HEADS_A
IN_COLS = A_COLS + 3 * CONV_CH + 3 * N_HEADS_C * HEAD_DIM + 3 * N_HEADS_D * HEAD_DIM
COL_WIDTHS = (N_HEADS_A * HEAD_DIM, HEAD_DIM, HEAD_DIM, HEAD_DIM, HEAD_DIM, HEAD_DIM, HEAD_DIM,
              N_NSA_BRANCH * N_HEADS_A,
              CONV_CH, CONV_CH, CONV_CH,
              N_HEADS_C * HEAD_DIM, N_HEADS_C * HEAD_DIM, N_HEADS_C * HEAD_DIM,
              N_HEADS_D * HEAD_DIM, N_HEADS_D * HEAD_DIM, N_HEADS_D * HEAD_DIM)
NEG_INF = -1e30
FORCE_SCORE = 1e6
RMS_EPS = 1e-6


def rms_norm(x, g):
    xf = x.astype(jnp.float32)
    y = xf * lax.rsqrt(jnp.mean(xf * xf, axis=-1, keepdims=True) + RMS_EPS)
    return (y * g.astype(jnp.float32)).astype(x.dtype)

def to_heads(t, n):
    b, s, _ = t.shape
    return t.reshape(b, s, n, HEAD_DIM).transpose(0, 2, 1, 3)

def alibi_slopes(n):
    return jnp.exp2(-8.0 * jnp.arange(1, n + 1, dtype=jnp.float32) / n)

def banded_attention(q, k, v, max_back, dist_scale, slopes):
    n, h, l, hd = q.shape
    g = k.shape[1]
    r = h // g
    nb = l // BLOCK
    n_prev = -(-max_back // BLOCK)
    w = (n_prev + 1) * BLOCK
    qb = q.reshape(n, g, r, nb, BLOCK, hd)

    def band(t):
        tb = t.reshape(n, g, nb, BLOCK, hd)
        tp = jnp.pad(tb, ((0, 0), (0, 0), (n_prev, 0), (0, 0), (0, 0)))
        return jnp.concatenate([tp[:, :, i:i + nb] for i in range(n_prev + 1)], axis=3)

    kb, vb = band(k), band(v)
    rows = jnp.arange(BLOCK)
    diff = rows[:, None] + n_prev * BLOCK - jnp.arange(w)[None, :]
    key_idx = jnp.arange(nb)[:, None, None] * BLOCK + rows[None, :, None] - diff[None]
    mask = (diff >= 0) & (diff <= max_back) & (key_idx >= 0)
    s = jnp.einsum('ngrbqd,ngbkd->ngrbqk', qb, kb).astype(jnp.float32) * (HEAD_DIM ** -0.5)
    s = s - slopes.reshape(g, r)[None, :, :, None, None, None] * (diff * dist_scale).astype(jnp.float32)
    s = jnp.where(mask, s, NEG_INF)
    lse = jax.nn.logsumexp(s, axis=-1)
    p = jnp.exp(s - lse[..., None])
    o = jnp.einsum('ngrbqk,ngbkd->ngrbqd', p.astype(v.dtype), vb)
    return o.reshape(n, h, l, hd), lse.reshape(n, h, l)

def compress_tokens(t, pe, w1, w2):
    b, s, _ = t.shape
    n_cmp = (s - CMP_LEN) // CMP_STRIDE + 1
    idx = jnp.arange(n_cmp)[:, None] * CMP_STRIDE + jnp.arange(CMP_LEN)[None, :]
    blocks = (t[:, idx] + pe).reshape(b, n_cmp, CMP_LEN * HEAD_DIM)
    return jax.nn.gelu(blocks @ w1) @ w2

def nsa_mixer(q_tok, kc_tok, vc_tok, ks_tok, vs_tok, kw_tok, vw_tok, gate_logits, b_gate,
              g_q, g_kc, g_ks, g_kw, pe_k, pe_v, w1_k, w2_k, w1_v, w2_v, slopes):
    b, s, _ = q_tok.shape
    h = N_HEADS_A
    scale = HEAD_DIM ** -0.5
    q = rms_norm(to_heads(q_tok, h), g_q)
    kc = rms_norm(compress_tokens(kc_tok, pe_k, w1_k, w2_k), g_kc)
    vc = compress_tokens(vc_tok, pe_v, w1_v, w2_v)
    n_cmp = kc.shape[1]
    cmp_end = jnp.arange(n_cmp) * CMP_STRIDE + CMP_LEN - 1
    n_sel = s // SEL_BLOCK
    top = min(N_SELECT, n_sel)
    ratio = SEL_BLOCK // CMP_STRIDE
    ks = rms_norm(ks_tok, g_ks).reshape(b, n_sel, SEL_BLOCK, HEAD_DIM)
    vs = vs_tok.reshape(b, n_sel, SEL_BLOCK, HEAD_DIM)
    blk_ids = jnp.arange(n_sel)
    bidx = jnp.arange(b)[:, None, None]
    nc = s // BLOCK
    q_chunks = q.reshape(b, h, nc, BLOCK, HEAD_DIM).transpose(2, 0, 1, 3, 4)

    def chunk(args):
        qi, c = args
        t = c * BLOCK + jnp.arange(BLOCK)
        dist_c = t[:, None] - cmp_end[None, :]
        vis = dist_c >= 0
        sc = jnp.einsum('bhqd,bnd->bhqn', qi, kc).astype(jnp.float32) * scale
        sc = jnp.where(vis, sc - slopes[:, None, None] * dist_c.astype(jnp.float32), NEG_INF)
        p_cmp = jax.nn.softmax(sc, axis=-1) * vis
        o_cmp = jnp.einsum('bhqn,bnd->bhqd', p_cmp.astype(vc.dtype), vc)
        imp = jnp.pad(p_cmp.sum(1), ((0, 0), (0, 0), (0, ratio * n_sel - n_cmp)))
        imp_ov = imp
        for sh in range(1, CMP_LEN // CMP_STRIDE):
            imp_ov = imp_ov + jnp.pad(imp[..., :-sh], ((0, 0), (0, 0), (sh, 0)))
        imp_blk = imp_ov.reshape(b, BLOCK, n_sel, ratio).sum(-1)
        cur = t // SEL_BLOCK
        forced = (blk_ids[None] == 0) | (blk_ids[None] == cur[:, None]) | (blk_ids[None] == cur[:, None] - 1)
        valid = blk_ids[None] * SEL_BLOCK <= t[:, None]
        score = jnp.where(forced, FORCE_SCORE, jnp.where(valid, imp_blk, -FORCE_SCORE))
        _, idx = lax.top_k(score, top)
        kg = ks[bidx, idx]
        vg = vs[bidx, idx]
        pos = idx[..., None] * SEL_BLOCK + jnp.arange(SEL_BLOCK)
        dist_s = t[None, :, None, None] - pos
        ss = jnp.einsum('bhqd,bqkjd->bhqkj', qi, kg).astype(jnp.float32) * scale
        ss = ss - slopes[None, :, None, None, None] * dist_s[:, None].astype(jnp.float32)
        ss = jnp.where((dist_s >= 0)[:, None], ss, NEG_INF)
        p_slc = jax.nn.softmax(ss.reshape(b, h, BLOCK, top * SEL_BLOCK), axis=-1).reshape(ss.shape)
        o_slc = jnp.einsum('bhqkj,bqkjd->bhqd', p_slc.astype(vg.dtype), vg)
        return o_cmp, o_slc

    o_cmp, o_slc = lax.map(chunk, (q_chunks, jnp.arange(nc)))
    o_cmp = o_cmp.transpose(1, 2, 0, 3, 4).reshape(b, h, s, HEAD_DIM)
    o_slc = o_slc.transpose(1, 2, 0, 3, 4).reshape(b, h, s, HEAD_DIM)
    o_win, _ = banded_attention(q, rms_norm(kw_tok, g_kw)[:, None], vw_tok[:, None], NSA_WINDOW - 1, 1, slopes)
    gates = jax.nn.sigmoid(gate_logits + b_gate).reshape(b, s, h, N_NSA_BRANCH).transpose(0, 2, 1, 3)
    return gates[..., 0:1] * o_cmp + gates[..., 1:2] * o_slc + gates[..., 2:3] * o_win

def short_conv_mixer(gate_b, gate_c, u, conv_w):
    y = lax.conv_general_dilated(gate_c * u, conv_w[:, None, :], window_strides=(1,),
                                 padding=[(CONV_K - 1, 0)], dimension_numbers=('NWC', 'WIO', 'NWC'),
                                 feature_group_count=CONV_CH)
    return gate_b * y

def stick_breaking_attention(q, k, v):
    b, h, s, hd = q.shape
    nc = s // BLOCK
    q_chunks = q.reshape(b, h, nc, BLOCK, hd).transpose(2, 0, 1, 3, 4)
    key_pos = jnp.arange(s)

    def chunk(args):
        qi, c = args
        t = c * BLOCK + jnp.arange(BLOCK)
        z = jnp.einsum('bhqd,bhsd->bhqs', qi, k).astype(jnp.float32) * (hd ** -0.5)
        past = key_pos[None, :] < t[:, None]
        neg_log_keep = jnp.where(past, jax.nn.softplus(z), 0.0)
        between = lax.cumsum(neg_log_keep, axis=3, reverse=True) - neg_log_keep
        attn = jnp.where(past, jnp.exp(jax.nn.log_sigmoid(z) - between), 0.0)
        return jnp.einsum('bhqs,bhsd->bhqd', attn.astype(v.dtype), v)

    o = lax.map(chunk, (q_chunks, jnp.arange(nc)))
    return o.transpose(1, 2, 0, 3, 4).reshape(b, h, s, hd)

def dilated_attention(q, k, v, window, dil, slopes):
    b, h, s, hd = q.shape
    span = dil * BLOCK
    sp = -(-s // span) * span
    l = sp // dil

    def fold(t):
        t = jnp.pad(t, ((0, 0), (0, 0), (0, sp - s), (0, 0)))
        return t.reshape(b, h, l, dil, hd).transpose(0, 3, 1, 2, 4).reshape(b * dil, h, l, hd)

    o, lse = banded_attention(fold(q), fold(k), fold(v), window // dil, dil, slopes)
    o = o.reshape(b, dil, h, l, hd).transpose(0, 2, 3, 1, 4).reshape(b, h, sp, hd)[:, :, :s]
    lse = lse.reshape(b, dil, h, l).transpose(0, 2, 3, 1).reshape(b, h, sp)[:, :, :s]
    return o, lse

def hybrid_layer(x, g_mix, w_in, b_gate, g_q_nsa, g_k_cmp, g_k_slc, g_k_win, pe_k_cmp, pe_v_cmp,
                 w1_k_cmp, w2_k_cmp, w1_v_cmp, w2_v_cmp, conv_w, g_q_dil, g_k_dil, g_out, w_out,
                 g_ffn, w_gate, w_up, w_down):
    b, s, _ = x.shape
    hn = rms_norm(x, g_mix)
    proj = hn @ w_in
    cuts = [int(c) for c in np.cumsum(COL_WIDTHS)[:-1]]
    (qa, kca, vca, ksa, vsa, kwa, vwa, gta, cvb, cvc, cvu,
     qc, kc, vc, qd, kd, vd) = jnp.split(proj, cuts, axis=-1)
    slopes = alibi_slopes(N_HEADS_A + N_HEADS_D)
    slopes_a, slopes_d = slopes[0::2], slopes[1::2]
    o_a = nsa_mixer(qa, kca, vca, ksa, vsa, kwa, vwa, gta, b_gate, g_q_nsa, g_k_cmp, g_k_slc, g_k_win,
                    pe_k_cmp, pe_v_cmp, w1_k_cmp, w2_k_cmp, w1_v_cmp, w2_v_cmp, slopes_a)
    o_b = short_conv_mixer(cvb, cvc, cvu, conv_w).reshape(b, s, CONV_CH // HEAD_DIM, HEAD_DIM)
    o_c = stick_breaking_attention(to_heads(qc, N_HEADS_C), to_heads(kc, N_HEADS_C), to_heads(vc, N_HEADS_C))
    qdh = rms_norm(to_heads(qd, N_HEADS_D), g_q_dil)
    kdh = rms_norm(to_heads(kd, N_HEADS_D), g_k_dil)
    vdh = to_heads(vd, N_HEADS_D)
    outs, lses = [], []
    for window, dil in DILATED_CONFIGS:
        o_i, lse_i = dilated_attention(qdh, kdh, vdh, window, dil, slopes_d)
        outs.append(o_i)
        lses.append(lse_i)
    mix_w = jax.nn.softmax(jnp.stack(lses, axis=0), axis=0)
    o_d = jnp.sum(mix_w[..., None].astype(vdh.dtype) * jnp.stack(outs, axis=0), axis=0)
    groups = jnp.concatenate([o_a.transpose(0, 2, 1, 3), o_b, o_c.transpose(0, 2, 1, 3),
                              o_d.transpose(0, 2, 1, 3)], axis=2)
    groups = rms_norm(groups, g_out.reshape(N_GROUPS, HEAD_DIM)).reshape(b, s, MIX_WIDTH)
    x = x + groups @ w_out
    h2 = rms_norm(x, g_ffn)
    return x + (jax.nn.silu(h2 @ w_gate) * (h2 @ w_up)) @ w_down

def first_inputs(seed: int = 0) -> dict:
    key = jax.random.key(seed)
    ks = jax.random.split(key, 23)
    L = DEPTH
    hd = HEAD_DIM

    def nrm(k, shape, scale):
        return jax.random.normal(k, shape, jnp.float32) * scale

    def gain(k, shape):
        return 1.0 + 0.02 * jax.random.normal(k, shape, jnp.float32)

    return {
        'x': nrm(ks[0], (BATCH, SEQ, D_MODEL), 1.0),
        'g_mix': gain(ks[1], (L, D_MODEL)),
        'w_in': nrm(ks[2], (L, D_MODEL, IN_COLS), D_MODEL ** -0.5),
        'b_gate': nrm(ks[3], (L, N_NSA_BRANCH * N_HEADS_A), 0.1),
        'g_q_nsa': gain(ks[4], (L, hd)),
        'g_k_cmp': gain(ks[5], (L, hd)),
        'g_k_slc': gain(ks[6], (L, hd)),
        'g_k_win': gain(ks[7], (L, hd)),
        'pe_k_cmp': nrm(ks[8], (L, CMP_LEN, hd), 0.1),
        'pe_v_cmp': nrm(ks[9], (L, CMP_LEN, hd), 0.1),
        'w1_k_cmp': nrm(ks[10], (L, CMP_LEN * hd, CMP_HIDDEN), (CMP_LEN * hd) ** -0.5),
        'w2_k_cmp': nrm(ks[11], (L, CMP_HIDDEN, hd), CMP_HIDDEN ** -0.5),
        'w1_v_cmp': nrm(ks[12], (L, CMP_LEN * hd, CMP_HIDDEN), (CMP_LEN * hd) ** -0.5),
        'w2_v_cmp': nrm(ks[13], (L, CMP_HIDDEN, hd), CMP_HIDDEN ** -0.5),
        'conv_w': nrm(ks[14], (L, CONV_K, CONV_CH), CONV_K ** -0.5),
        'g_q_dil': gain(ks[15], (L, hd)),
        'g_k_dil': gain(ks[16], (L, hd)),
        'g_out': gain(ks[17], (L, MIX_WIDTH)),
        'w_out': nrm(ks[18], (L, MIX_WIDTH, D_MODEL), MIX_WIDTH ** -0.5),
        'g_ffn': gain(ks[19], (L, D_MODEL)),
        'w_gate': nrm(ks[20], (L, D_MODEL, D_FF), D_MODEL ** -0.5),
        'w_up': nrm(ks[21], (L, D_MODEL, D_FF), D_MODEL ** -0.5),
        'w_down': nrm(ks[22], (L, D_FF, D_MODEL), D_FF ** -0.5),
    }

def first_block(x, g_mix, w_in, b_gate, g_q_nsa, g_k_cmp, g_k_slc, g_k_win, pe_k_cmp, pe_v_cmp,
              w1_k_cmp, w2_k_cmp, w1_v_cmp, w2_v_cmp, conv_w, g_q_dil, g_k_dil, g_out, w_out,
              g_ffn, w_gate, w_up, w_down):
    for l in range(DEPTH):
        x = hybrid_layer(x, g_mix[l], w_in[l], b_gate[l], g_q_nsa[l], g_k_cmp[l], g_k_slc[l], g_k_win[l],
                         pe_k_cmp[l], pe_v_cmp[l], w1_k_cmp[l], w2_k_cmp[l], w1_v_cmp[l], w2_v_cmp[l],
                         conv_w[l], g_q_dil[l], g_k_dil[l], g_out[l], w_out[l], g_ffn[l],
                         w_gate[l], w_up[l], w_down[l])
    return x


DEPTH_2 = 4

N_MIXERS = 4
N_A = (DEPTH_2 + 3) // 4
N_B = (DEPTH_2 + 2) // 4
N_C = (DEPTH_2 + 1) // 4
N_D = DEPTH_2 // 4
A_HEADS = 4
A_DV = D_MODEL // A_HEADS
A_DK = A_DV // 2
A_CHUNK = 64
A_IN = 2 * A_HEADS * A_DK + 2 * A_HEADS * A_DV + 2 * A_HEADS
B_HEAD_DIM = 64
B_Q_HEADS = D_MODEL // B_HEAD_DIM
B_KV_HEADS = B_Q_HEADS // 8
B_WINDOW = 128
B_BLOCK = 128
B_IN = (B_Q_HEADS + 2 * B_KV_HEADS) * B_HEAD_DIM
C_EXPAND = 128
C_HEADS = D_MODEL // C_EXPAND
C_DK = C_EXPAND
C_DV = D_MODEL // C_HEADS
C_CHUNK = 16
C_IN = 2 * C_HEADS * C_DK + 2 * C_HEADS * C_DV
D_HEAD_DIM = 64
D_HEADS = D_MODEL // (2 * D_HEAD_DIM)
D_QBLOCK = 128
D_IN = 3 * D_HEADS * 2 * D_HEAD_DIM
ROPE_THETA = 500000.0
ROT_FRAC = 4
FFN_HIDDEN = -(-8 * D_MODEL // (3 * 256)) * 256
DEEPNORM_ALPHA = (2 * DEPTH_2) ** 0.25
DEEPNORM_BETA = (8 * DEPTH_2) ** -0.25
F32 = jnp.float32


def layer_norm(x, g, b, eps=1e-5):
    xf = x.astype(F32)
    mu = xf.mean(-1, keepdims=True)
    var = jnp.square(xf - mu).mean(-1, keepdims=True)
    return ((xf - mu) * lax.rsqrt(var + eps) * g.astype(F32) + b.astype(F32)).astype(x.dtype)

def head_rms_norm(h, w, eps=1e-6):
    hf = h.astype(F32)
    return hf * lax.rsqrt(jnp.mean(hf * hf, -1, keepdims=True) + eps) * w.astype(F32)

def partial_rope(x, positions):
    hd = x.shape[-1]
    rot = hd // ROT_FRAC
    half = rot // 2
    inv = jnp.power(ROPE_THETA, -jnp.arange(half, dtype=F32) * 2.0 / rot)
    ang = positions.astype(F32)[..., None] * inv
    cos = jnp.cos(ang)[:, :, None, :]
    sin = jnp.sin(ang)[:, :, None, :]
    xf = x.astype(F32)
    x1, x2 = xf[..., :half], xf[..., half:rot]
    out = jnp.concatenate([x1 * cos - x2 * sin, x2 * cos + x1 * sin, xf[..., rot:]], axis=-1)
    return out.astype(x.dtype)

def to_chunks(a, L):
    r = a.reshape(a.shape[0], a.shape[1] // L, L, *a.shape[2:])
    return jnp.swapaxes(jnp.moveaxis(r, 1, 0), 2, 3)

def from_chunks(a):
    r = jnp.moveaxis(jnp.swapaxes(a, 2, 3), 0, 1)
    return r.reshape(r.shape[0], r.shape[1] * r.shape[2], *r.shape[3:])

def mlstm_mixer(h, w_in, b_gate, norm_w, w_out):
    bsz, seq, _ = h.shape
    qk, vw = A_HEADS * A_DK, A_HEADS * A_DV
    proj = (h @ w_in).astype(F32)
    q = proj[..., :qk].reshape(bsz, seq, A_HEADS, A_DK)
    k = proj[..., qk:2 * qk].reshape(bsz, seq, A_HEADS, A_DK) * (A_DK ** -0.5)
    v = proj[..., 2 * qk:2 * qk + vw].reshape(bsz, seq, A_HEADS, A_DV)
    o = jax.nn.sigmoid(proj[..., 2 * qk + vw:2 * qk + 2 * vw]).reshape(bsz, seq, A_HEADS, A_DV)
    gates = proj[..., 2 * qk + 2 * vw:] + b_gate.astype(F32)
    i_pre = gates[..., :A_HEADS]
    log_f = jax.nn.log_sigmoid(gates[..., A_HEADS:])
    causal = jnp.tril(jnp.ones((A_CHUNK, A_CHUNK), bool))

    def step(carry, xs):
        C, n, m = carry
        qc, kc, vc, ic, fc = xs
        b = jnp.cumsum(fc, axis=-1)
        dmat = jnp.where(causal, b[..., :, None] - b[..., None, :] + ic[..., None, :], -jnp.inf)
        m_inter = b + m[..., None]
        m_t = jnp.maximum(m_inter, dmat.max(-1))
        a = jnp.einsum('bhtd,bhsd->bhts', qc, kc) * jnp.exp(dmat - m_t[..., None])
        w_inter = jnp.exp(m_inter - m_t)
        num = jnp.einsum('bhts,bhse->bhte', a, vc) + w_inter[..., None] * jnp.einsum('bhtd,bhde->bhte', qc, C)
        den = a.sum(-1) + w_inter * jnp.einsum('bhtd,bhd->bht', qc, n)
        h_out = num / jnp.maximum(jnp.abs(den), jnp.exp(-m_t))[..., None]
        b_last = b[..., -1]
        g = b_last[..., None] - b + ic
        m_new = jnp.maximum(b_last + m, g.max(-1))
        decay = jnp.exp(b_last + m - m_new)
        ws = jnp.exp(g - m_new[..., None])
        C_new = decay[..., None, None] * C + jnp.einsum('bhs,bhsd,bhse->bhde', ws, kc, vc)
        n_new = decay[..., None] * n + jnp.einsum('bhs,bhsd->bhd', ws, kc)
        return (C_new, n_new, m_new), h_out

    init = (jnp.zeros((bsz, A_HEADS, A_DK, A_DV), F32),
            jnp.zeros((bsz, A_HEADS, A_DK), F32),
            jnp.zeros((bsz, A_HEADS), F32))
    xs = (to_chunks(q, A_CHUNK), to_chunks(k, A_CHUNK), to_chunks(v, A_CHUNK),
          to_chunks(i_pre, A_CHUNK), to_chunks(log_f, A_CHUNK))
    _, ys = lax.scan(step, init, xs)
    hs = from_chunks(ys)
    y = head_rms_norm(hs, norm_w.reshape(A_HEADS, A_DV)) * o
    return y.reshape(bsz, seq, vw).astype(w_out.dtype) @ w_out

def swa_mixer(h, positions, w_in, sinks, w_out):
    bsz, seq, _ = h.shape
    nb = seq // B_BLOCK
    grp = B_Q_HEADS // B_KV_HEADS
    qw, kw = B_Q_HEADS * B_HEAD_DIM, B_KV_HEADS * B_HEAD_DIM
    proj = h @ w_in
    q = partial_rope(proj[..., :qw].reshape(bsz, seq, B_Q_HEADS, B_HEAD_DIM), positions)
    k = partial_rope(proj[..., qw:qw + kw].reshape(bsz, seq, B_KV_HEADS, B_HEAD_DIM), positions)
    v = proj[..., qw + kw:].reshape(bsz, seq, B_KV_HEADS, B_HEAD_DIM)
    qb = jnp.moveaxis(q.reshape(bsz, nb, B_BLOCK, B_KV_HEADS, grp, B_HEAD_DIM), 1, 0)

    def band(a):
        ap = jnp.pad(a, ((0, 0), (B_BLOCK, 0), (0, 0), (0, 0)))
        ap = ap.reshape(bsz, nb + 1, B_BLOCK, B_KV_HEADS, B_HEAD_DIM)
        return jnp.moveaxis(jnp.concatenate([ap[:, :-1], ap[:, 1:]], axis=2), 1, 0)

    kb, vb = band(k), band(v)
    sink = sinks.astype(F32).reshape(1, B_KV_HEADS, grp, 1, 1)
    scale = B_HEAD_DIM ** -0.5

    def block(args):
        qi, ki, vi, n = args
        s = jnp.einsum('bqhgd,bkhd->bhgqk', qi, ki, preferred_element_type=F32) * scale
        qpos = n * B_BLOCK + jnp.arange(B_BLOCK)
        kpos = (n - 1) * B_BLOCK + jnp.arange(2 * B_BLOCK)
        rel = qpos[:, None] - kpos[None, :]
        valid = (rel >= 0) & (rel < B_WINDOW) & (kpos >= 0)[None, :]
        s = jnp.where(valid, s, -jnp.inf)
        mx = jnp.maximum(s.max(-1, keepdims=True), sink)
        p = jnp.exp(s - mx)
        p = p / (p.sum(-1, keepdims=True) + jnp.exp(sink - mx))
        return jnp.einsum('bhgqk,bkhd->bqhgd', p, vi.astype(F32))

    out = lax.map(block, (qb, kb, vb, jnp.arange(nb)))
    out = jnp.moveaxis(out, 0, 1).reshape(bsz, seq, qw)
    return out.astype(w_out.dtype) @ w_out

def hgrn2_mixer(h, lower_bound, w_in, norm_w, w_out):
    bsz, seq, _ = h.shape
    kw, vw = C_HEADS * C_DK, C_HEADS * C_DV
    proj = (h @ w_in).astype(F32)
    q = proj[..., :kw]
    f_pre = proj[..., kw:2 * kw]
    i_in = proj[..., 2 * kw:2 * kw + vw]
    g_out = proj[..., 2 * kw + vw:]
    lb = lower_bound.astype(F32)
    log_f = jnp.logaddexp(jnp.log(lb), jnp.log1p(-lb) + jax.nn.log_sigmoid(f_pre))
    k = (1.0 - lb) * jax.nn.sigmoid(-f_pre)
    heads = lambda a, d: a.reshape(bsz, seq, C_HEADS, d)
    causal = jnp.tril(jnp.ones((C_CHUNK, C_CHUNK), bool))[:, :, None]

    def step(S, xs):
        qc, kc, vc, fc = xs
        cf = jnp.cumsum(fc, axis=2)
        diff = cf[:, :, :, None, :] - cf[:, :, None, :, :]
        decay = jnp.exp(jnp.where(causal, diff, -jnp.inf))
        a = jnp.einsum('bhtd,bhtsd,bhsd->bhts', qc, decay, kc)
        o = jnp.einsum('bhts,bhse->bhte', a, vc) + jnp.einsum('bhtd,bhde->bhte', qc * jnp.exp(cf), S)
        last = cf[:, :, -1:, :]
        S_new = jnp.exp(last[:, :, 0, :])[..., None] * S + jnp.einsum('bhsd,bhse->bhde', kc * jnp.exp(last - cf), vc)
        return S_new, o

    xs = (to_chunks(heads(q, C_DK), C_CHUNK), to_chunks(heads(k, C_DK), C_CHUNK),
          to_chunks(heads(i_in, C_DV), C_CHUNK), to_chunks(heads(log_f, C_DK), C_CHUNK))
    _, ys = lax.scan(step, jnp.zeros((bsz, C_HEADS, C_DK, C_DV), F32), xs)
    o = from_chunks(ys)
    y = head_rms_norm(o, norm_w.reshape(C_HEADS, C_DV)) * jax.nn.silu(heads(g_out, C_DV))
    return y.reshape(bsz, seq, vw).astype(w_out.dtype) @ w_out

def diff_mixer(h, positions, lam_init, w_in, lam_vec, norm_w, w_out):
    bsz, seq, _ = h.shape
    nb = seq // D_QBLOCK
    w = D_HEADS * 2 * D_HEAD_DIM
    proj = h @ w_in
    q = partial_rope(proj[..., :w].reshape(bsz, seq, 2 * D_HEADS, D_HEAD_DIM), positions)
    k = partial_rope(proj[..., w:2 * w].reshape(bsz, seq, 2 * D_HEADS, D_HEAD_DIM), positions)
    q = q.reshape(bsz, seq, D_HEADS, 2, D_HEAD_DIM)
    k = k.reshape(bsz, seq, D_HEADS, 2, D_HEAD_DIM)
    v = proj[..., 2 * w:].reshape(bsz, seq, D_HEADS, 2 * D_HEAD_DIM).astype(F32)
    lv = lam_vec.astype(F32)
    lam = jnp.exp(jnp.sum(lv[0] * lv[1])) - jnp.exp(jnp.sum(lv[2] * lv[3])) + lam_init
    qb = jnp.moveaxis(q.reshape(bsz, nb, D_QBLOCK, D_HEADS, 2, D_HEAD_DIM), 1, 0)
    kpos = jnp.arange(seq)
    scale = D_HEAD_DIM ** -0.5

    def block(args):
        qi, n = args
        s = jnp.einsum('bqhcd,bkhcd->bhcqk', qi, k, preferred_element_type=F32) * scale
        qpos = n * D_QBLOCK + jnp.arange(D_QBLOCK)
        s = jnp.where(kpos[None, :] <= qpos[:, None], s, -jnp.inf)
        p = jax.nn.softmax(s, axis=-1)
        a = p[:, :, 0] - lam * p[:, :, 1]
        return jnp.einsum('bhqk,bkhe->bqhe', a, v)

    out = lax.map(block, (qb, jnp.arange(nb)))
    out = jnp.moveaxis(out, 0, 1).reshape(bsz, seq, D_HEADS, 2 * D_HEAD_DIM)
    out = head_rms_norm(out, norm_w) * (1.0 - lam_init)
    return out.reshape(bsz, seq, w).astype(w_out.dtype) @ w_out

def swiglu(h, w_in, w_out):
    gu = h @ w_in
    return (jax.nn.silu(gu[..., :FFN_HIDDEN]) * gu[..., FFN_HIDDEN:]) @ w_out

def second_inputs(seed: int = 0) -> dict:
    key = jax.random.key(seed)
    ks = jax.random.split(key, 26)
    nrm = lambda k, shape, s: jax.random.normal(k, shape, F32) * s
    D = D_MODEL
    beta = DEEPNORM_BETA
    x = nrm(ks[0], (BATCH, SEQ, D), 1.0)
    c = nrm(ks[1], (BATCH, D), 1.0)
    positions = jnp.broadcast_to(jnp.arange(SEQ, dtype=jnp.int32), (BATCH, SEQ))
    ada_w = nrm(ks[2], (DEPTH_2, 2, D, 3 * D), 0.1 * D ** -0.5)
    ada_b = nrm(ks[3], (DEPTH_2, 2, 3 * D), 0.01)
    ln_g = 1.0 + nrm(ks[4], (DEPTH_2, 2, D), 0.02)
    ln_b = nrm(ks[5], (DEPTH_2, 2, D), 0.01)
    mlstm_w_in = nrm(ks[6], (N_A, D, A_IN), D ** -0.5)
    mlstm_b_gate = jnp.concatenate(
        [nrm(ks[7], (N_A, A_HEADS), 0.1),
         jnp.linspace(3.0, 6.0, A_HEADS, dtype=F32) + nrm(ks[8], (N_A, A_HEADS), 0.1)], axis=-1)
    mlstm_norm = 1.0 + nrm(ks[9], (N_A, A_HEADS * A_DV), 0.02)
    mlstm_w_out = nrm(ks[10], (N_A, A_HEADS * A_DV, D), beta * (A_HEADS * A_DV) ** -0.5)
    swa_w_in = nrm(ks[11], (N_B, D, B_IN), D ** -0.5)
    swa_sinks = nrm(ks[12], (N_B, B_Q_HEADS), 0.5)
    swa_w_out = nrm(ks[13], (N_B, B_Q_HEADS * B_HEAD_DIM, D), beta * (B_Q_HEADS * B_HEAD_DIM) ** -0.5)
    hgrn_w_in = nrm(ks[14], (N_C, D, C_IN), D ** -0.5)
    hgrn_lower_bounds = nrm(ks[15], (DEPTH_2, C_HEADS * C_DK), 0.1)
    hgrn_norm = 1.0 + nrm(ks[16], (N_C, C_HEADS * C_DV), 0.02)
    hgrn_w_out = nrm(ks[17], (N_C, C_HEADS * C_DV, D), beta * (C_HEADS * C_DV) ** -0.5)
    diff_w_in = nrm(ks[18], (N_D, D, D_IN), D ** -0.5)
    diff_lambda = nrm(ks[19], (N_D, 4, D_HEAD_DIM), 0.1)
    diff_norm = 1.0 + nrm(ks[20], (N_D, 2 * D_HEAD_DIM), 0.02)
    diff_w_out = nrm(ks[21], (N_D, D_HEADS * 2 * D_HEAD_DIM, D), beta * (D_HEADS * 2 * D_HEAD_DIM) ** -0.5)
    ffn_w_in = nrm(ks[22], (DEPTH_2, D, 2 * FFN_HIDDEN), D ** -0.5)
    ffn_w_out = nrm(ks[23], (DEPTH_2, FFN_HIDDEN, D), beta * FFN_HIDDEN ** -0.5)
    return {"x": x, "c": c, "positions": positions, "ada_w": ada_w, "ada_b": ada_b,
            "ln_g": ln_g, "ln_b": ln_b,
            "mlstm_w_in": mlstm_w_in, "mlstm_b_gate": mlstm_b_gate, "mlstm_norm": mlstm_norm,
            "mlstm_w_out": mlstm_w_out,
            "swa_w_in": swa_w_in, "swa_sinks": swa_sinks, "swa_w_out": swa_w_out,
            "hgrn_w_in": hgrn_w_in, "hgrn_lower_bounds": hgrn_lower_bounds, "hgrn_norm": hgrn_norm,
            "hgrn_w_out": hgrn_w_out,
            "diff_w_in": diff_w_in, "diff_lambda": diff_lambda, "diff_norm": diff_norm,
            "diff_w_out": diff_w_out,
            "ffn_w_in": ffn_w_in, "ffn_w_out": ffn_w_out}

def second_block(x, c, positions, ada_w, ada_b, ln_g, ln_b,
              mlstm_w_in, mlstm_b_gate, mlstm_norm, mlstm_w_out,
              swa_w_in, swa_sinks, swa_w_out,
              hgrn_w_in, hgrn_lower_bounds, hgrn_norm, hgrn_w_out,
              diff_w_in, diff_lambda, diff_norm, diff_w_out,
              ffn_w_in, ffn_w_out):
    cond = jax.nn.silu(c.astype(F32))
    lbs = jnp.cumsum(jax.nn.softmax(hgrn_lower_bounds.astype(F32), axis=0), axis=0)
    lbs = lbs - lbs[0]
    for i in range(DEPTH_2):
        mixer, j = i % N_MIXERS, i // N_MIXERS
        mod = jnp.einsum('bd,sde->sbe', cond, ada_w[i].astype(F32)) + ada_b[i][:, None, :].astype(F32)
        shift, scale, gate = jnp.split(mod.astype(x.dtype), 3, axis=-1)
        h = x * (1 + scale[0][:, None]) + shift[0][:, None]
        if mixer == 0:
            y = mlstm_mixer(h, mlstm_w_in[j], mlstm_b_gate[j], mlstm_norm[j], mlstm_w_out[j])
        elif mixer == 1:
            y = swa_mixer(h, positions, swa_w_in[j], swa_sinks[j], swa_w_out[j])
        elif mixer == 2:
            y = hgrn2_mixer(h, lbs[i], hgrn_w_in[j], hgrn_norm[j], hgrn_w_out[j])
        else:
            lam_init = 0.8 - 0.6 * math.exp(-0.3 * i)
            y = diff_mixer(h, positions, lam_init, diff_w_in[j], diff_lambda[j], diff_norm[j], diff_w_out[j])
        x = layer_norm(DEEPNORM_ALPHA * x + (1 + gate[0][:, None]) * y.astype(x.dtype), ln_g[i, 0], ln_b[i, 0])
        h = x * (1 + scale[1][:, None]) + shift[1][:, None]
        y = swiglu(h, ffn_w_in[i], ffn_w_out[i])
        x = layer_norm(DEEPNORM_ALPHA * x + (1 + gate[1][:, None]) * y.astype(x.dtype), ln_g[i, 1], ln_b[i, 1])
    return x


def setup_inputs(seed=0):
    out = dict(first_inputs(seed))
    for name, value in second_inputs(seed + 1).items():
        if name != "x":
            out[name + "_2"] = value
    return out


def reference(
    x, g_mix, w_in, b_gate, g_q_nsa, g_k_cmp, g_k_slc, g_k_win, pe_k_cmp, pe_v_cmp, w1_k_cmp,
    w2_k_cmp, w1_v_cmp, w2_v_cmp, conv_w, g_q_dil, g_k_dil, g_out, w_out, g_ffn, w_gate, w_up,
    w_down, c_2, positions_2, ada_w_2, ada_b_2, ln_g_2, ln_b_2, mlstm_w_in_2, mlstm_b_gate_2,
    mlstm_norm_2, mlstm_w_out_2, swa_w_in_2, swa_sinks_2, swa_w_out_2, hgrn_w_in_2,
    hgrn_lower_bounds_2, hgrn_norm_2, hgrn_w_out_2, diff_w_in_2, diff_lambda_2, diff_norm_2,
    diff_w_out_2, ffn_w_in_2, ffn_w_out_2,
):
    x = first_block(
        x, g_mix, w_in, b_gate, g_q_nsa, g_k_cmp, g_k_slc, g_k_win, pe_k_cmp, pe_v_cmp,
        w1_k_cmp, w2_k_cmp, w1_v_cmp, w2_v_cmp, conv_w, g_q_dil, g_k_dil, g_out, w_out, g_ffn,
        w_gate, w_up, w_down,
    )
    return second_block(
        x, c_2, positions_2, ada_w_2, ada_b_2, ln_g_2, ln_b_2, mlstm_w_in_2, mlstm_b_gate_2,
        mlstm_norm_2, mlstm_w_out_2, swa_w_in_2, swa_sinks_2, swa_w_out_2, hgrn_w_in_2,
        hgrn_lower_bounds_2, hgrn_norm_2, hgrn_w_out_2, diff_w_in_2, diff_lambda_2, diff_norm_2,
        diff_w_out_2, ffn_w_in_2, ffn_w_out_2,
    )


_drawn_inputs = setup_inputs


def setup_inputs(seed=0):
    import zlib

    import numpy as np

    out = dict(_drawn_inputs(seed))
    spreads = {}
    factors = {'g_q_nsa': 8.0,
     'g_k_cmp': 8.0,
     'g_k_slc': 8.0,
     'g_k_win': 8.0,
     'pe_k_cmp': 6.171,
     'g_q_dil': 8.0,
     'g_k_dil': 6.82,
     'g_out': 3.294,
     'g_ffn': 4.542,
     'ada_b_2': 5.364,
     'mlstm_norm_2': 64.0,
     'swa_sinks_2': 8.0,
     'hgrn_lower_bounds_2': 5.836,
     'hgrn_norm_2': 8.0,
     'diff_norm_2': 31.824}
    for name, (base, spread) in spreads.items():
        noise = np.random.default_rng([zlib.crc32(name.encode()), seed]).standard_normal(out[name].shape)
        drawn = base * np.exp(spread * noise) if base else spread * noise
        out[name] = jnp.asarray(drawn.astype(out[name].dtype))
    for name, factor in factors.items():
        out[name] = (out[name] * factor).astype(out[name].dtype)
    return out
```

```python
from collections import namedtuple
from contextlib import ExitStack, contextmanager

import numpy as np

import concourse.bass as bass
import concourse.mybir as mybir

F32 = mybir.dt.float32
F32R = mybir.dt.float32r
I32 = mybir.dt.int32
ACT = mybir.ActivationFunctionType
ALU = mybir.AluOpType
AX_X = mybir.AxisListType.X

P = 128
S = 512
D = 1024
DT = D // P
HD = 64
FF = 2816
FT = FF // P
TT = S // P
SLOT = 8 * P
RING = 4
LEAD = 3
ADA_RING = 2
CMP_LEN, CMP_STRIDE = 32, 16
NCMP = (S - CMP_LEN) // CMP_STRIDE + 1
NSA_HEADS = 4
NEG = -1e30
ALPHA = 8 ** 0.25
LAYERS = 4
PARTS = ["first", 0, 1, 2, 3]
LAM_INIT = [0.8 - 0.6 * float(np.exp(-0.3 * i)) for i in range(LAYERS)]
ROPE_THETA = 500000.0
SCALE = HD ** -0.5
SLOPES = [2.0 ** -(i + 1) for i in range(8)]
SLOPES_A, SLOPES_D = SLOPES[0::2], SLOPES[1::2]

W_IN_COLS = np.cumsum([0, 256, 64, 64, 64, 64, 64, 64, 12, 256, 256, 256, 256, 256, 256, 256, 256, 256])
(C_QA, C_KC, C_VC, C_KS, C_VS, C_KW, C_VW, C_GT, C_CB, C_CC, C_CU,
 C_QC, C_KCC, C_VCC, C_QD, C_KD, C_VD) = (int(v) for v in W_IN_COLS[:-1])
FIRST_TILES = ([C_QA, C_QA + P, C_CB, C_CB + P, C_QC, C_QC + P, C_QD, C_QD + P, C_KC, C_KS, C_KW,
                C_CC, C_CC + P, C_CU, C_CU + P, C_KCC, C_KCC + P, C_KD, C_KD + P])
FIRST_VALUES = [C_VCC, C_VCC + P, C_VD, C_VD + P]
MLSTM_TILES = [c for h in range(4) for c in (h * P, 512 + h * P)] + [2048 + j * P for j in range(8)]
MLSTM_VALUES = [1024 + j * P for j in range(8)]
SWA_TILES = [j * P for j in range(9)]
SWA_VALUES = [9 * P]
HGRN_TILES = [j * P for j in range(16)] + [3072 + j * P for j in range(8)]
HGRN_VALUES = [2048 + j * P for j in range(8)]
DIFF_TILES = [j * P for j in range(16)]
DIFF_VALUES = [2048 + j * P for j in range(8)]
IN_PROJ = {"first": (FIRST_TILES, FIRST_VALUES), 0: (MLSTM_TILES, MLSTM_VALUES), 1: (SWA_TILES, SWA_VALUES),
           2: (HGRN_TILES, HGRN_VALUES), 3: (DIFF_TILES, DIFF_VALUES)}

COLS = {}


def _columns():
    at = 0
    for name, width in [("g_mix", 8), ("g_ffn", 8), ("g_out", 8), ("g_q_nsa", 1), ("g_k_slc", 1), ("g_k_win", 1),
                        ("g_k_cmp", 1), ("g_q_dil", 1), ("g_k_dil", 1), ("conv_w", 6), ("pe", 32), ("gate_w", 96),
                        ("b_gate", 12), ("w2", 256), ("c", 8), ("ada_b", 192), ("ln_g", 64), ("ln_b", 64),
                        ("mlstm_gw", 64), ("mlstm_b", 2), ("mlstm_norm", 8), ("sinks", 16), ("lower", 32),
                        ("hgrn_norm", 8), ("diff_norm", 1), ("diff_lambda", 256)]:
        COLS[name] = (at, width)
        at += width
    return at


NCOLS = _columns()

KEPT = {"ident": 128, "ones": 128, "block64": 128, "eps6": 1, "eps5": 1, "tiny": 1}
LAYER_CONST = 1024
BIG_CONST = 3 * S


def constants():
    p, f = np.arange(P)[:, None], np.arange(P)[None, :]
    u = np.arange(S)[None, :]
    ident = (p == f).astype(np.float32)
    kept = np.concatenate([ident, np.ones((P, P)), (p // HD == f // HD) / HD, np.full((P, 1), 1e-6),
                           np.full((P, 1), 1e-5), np.full((P, 1), 1e-19)], 1).astype(np.float32)
    dist = p + (S - P) - u
    causal = np.where(dist >= 0, 0.0, NEG)
    mult = (dist <= 128).astype(int) + (dist % 4 == 0) + (dist % 16 == 0)
    logmult = np.where((dist >= 0) & (mult > 0), np.log(np.maximum(mult, 1)), NEG)
    big = np.concatenate([dist, causal, logmult], 1).astype(np.float32)
    layer = np.zeros((5, P, LAYER_CONST), np.float32)
    t = np.arange(TT)[:, None] * P
    dc = (p[:, :, None] + t[None]) - (np.arange(NCMP) * CMP_STRIDE + CMP_LEN - 1)[None, None, :]
    dc = dc.reshape(P, TT * NCMP)
    layer[0, :, 0:124] = dc
    layer[0, :, 124:248] = dc >= 0
    layer[0, :, 248:372] = np.where(dc >= 0, 0.0, NEG)
    layer[0, :, 384:512] = p >= f
    layer[0, :, 512:640] = p < f
    layer[0, :, 640:768] = np.where(p < f, 0.0, NEG)
    for h in range(4):
        layer[1, h, h * P:(h + 1) * P] = 1.0
    layer[1, :, 512:640] = np.where(p <= f, 0.0, -NEG)
    rope = np.zeros((P, P), np.float32)
    for b in (0, HD):
        for j in range(8):
            rope[b + 8 + j, b + j] = -1.0
            rope[b + j, b + 8 + j] = 1.0
    inv = np.zeros((P, 1), np.float32)
    for b in (0, HD):
        for j in range(16):
            inv[b + j, 0] = np.float32(ROPE_THETA) ** np.float32(-(j % 8) * 2.0 / 16)
    band = (P + p) - np.arange(2 * P)[None, :]
    for at in (2, 4):
        layer[at, :, 0:128] = rope
        layer[at, :, 128:129] = inv
    layer[2, :, 256:512] = np.where((band >= 0) & (band < 128), 0.0, NEG)
    for lv in range(7):
        b = 64 >> lv
        layer[3, :, lv * P:(lv + 1) * P] = (p // (2 * b) == f // (2 * b)) & (p % (2 * b) < b) & (f % (2 * b) >= b)
    layer[4, :, 256:768] = causal
    return kept, big, layer


PARTS_SPLIT = 3 * DT + FT


def mix_steps(part):
    return {"first": 2, 1: 1, 3: 1}.get(part, 0)


def n_groups(part):
    return {"first": 8 * TT, 1: 16 * TT, 3: 8 * TT}.get(part, 0)


def lin_total(parts):
    return sum(len(IN_PROJ[p][0]) + len(IN_PROJ[p][1]) + (4 if p == "first" else 0) + 2 * DT + 2 * FT for p in parts)


class Counts(dict):
    def __missing__(self, key):
        return 0

    def add(self, **more):
        for key, by in more.items():
            self[key] = self[key] + by


@contextmanager
def loop(eng, count):
    if count > 1:
        with eng.Fori(0, count) as i:
            yield i
    else:
        yield 0


def wait(eng, semaphore, value):
    if not isinstance(value, int) or value > 0:
        eng.wait_ge(semaphore, value)


def stream_length(parts):
    n = 0
    for part in parts:
        tiles, values = IN_PROJ[part]
        n += len(tiles) + len(values) + (8 if part == "first" else 0) + DT + 2 * FT + 3 * DT
    return n


def program(nc, xT, wstream, ada, cols, kept, bigc, layerc, pos, yT, parts):
    slots_total = stream_length(parts)
    ctx = ExitStack()
    with ctx:
        base = 16512
        top = [0]

        def place(name, shape, dt, at=None):
            size = int(np.prod(shape[1:]))
            if at is None:
                at = top[0]
                top[0] += -(-size // 8) * 8
            return nc.alloc_sbuf_tensor_at(name, shape, dt, offset=base + 4 * at)

        x = place("x", [P, DT, S], F32)
        h_at = top[0]
        h_hi = place("h_hi", [P, DT, S], F32R)
        h_lo = place("h_lo", [P, DT, S], F32R)
        big = top[0]
        hid_hi = place("hid_hi", [P, FT, S], F32R)
        hid_lo = place("hid_lo", [P, FT, S], F32R)
        raw = [place(f"raw{r}", [P, 8, P], F32) for r in range(RING)]
        w_hi = [place(f"w_hi{r}", [P, 8, P], F32R) for r in range(RING)]
        w_lo = [place(f"w_lo{r}", [P, 8, P], F32R) for r in range(RING)]
        ada_raw = [place(f"ada_raw{r}", [P, SLOT], F32) for r in range(ADA_RING)]
        ada_acc = place("ada_acc", [P, SLOT], F32)
        kp = place("kept", [P, sum(KEPT.values())], F32)
        co = place("cols", [P, NCOLS], F32)
        lc = place("layer_const", [P, LAYER_CONST], F32)
        cond = place("cond", [P, 8], F32)
        mod = [place(f"mod{r}", [P, 48], F32) for r in range(2)]
        small = place("small", [P, 160], F32)
        assert base + 4 * top[0] <= nc.sbuf_usable_end, top[0]

        h_tmp = place("h_tmp", [P, DT, S], F32, big + 16384)
        sq = [place(f"sq{r}", [P, S], F32, big + 20480 + r * S) for r in range(2)]
        rt = [place(f"rt{r}", [P, S], F32, big + 21504 + r * S) for r in range(2)]
        proj = place("proj", [P, 24, S], F32, big)
        first_vc = place("first_vc", [P, TT, 256], F32, big + 19 * S)
        first_vd = place("first_vd", [P, TT, 256], F32, big + 21 * S)
        v_slc = place("v_slc", [P, TT, HD], F32, big + 23 * S)
        v_win = place("v_win", [P, TT, HD], F32, big + 23 * S + 256)
        tables = place("tables", [P, 3, S], F32, big + 12288)
        s1 = big + 12288 + 3 * S
        AT = {}
        for name, at in (("first", s1), ("late", big + 13312)):
            AT[name] = dict(
                s=[place(f"att_s_{name}{r}", [P, 520], F32, at + r * 520) for r in range(2)],
                p=[place(f"att_p_{name}{r}", [P, 520], F32, at + 1040 + r * 520) for r in range(2)],
                pt=[place(f"att_pt_{name}{r}", [P, S], F32, at + 2080 + r * S) for r in range(2)])
        bias = place("bias", [P, 4, S], F32, s1 + 3104)
        cmp_bias = place("cmp_bias", [P, 4, TT * NCMP], F32, s1 + 5152)
        blk = place("blk", [P, 2, 16, 32], F32, s1)
        blk_hi = place("blk_hi", [P, 2, 16, 32], F32R, s1 + 1024)
        blk_lo = place("blk_lo", [P, 2, 16, 32], F32R, s1 + 2048)
        CW = [S - P * j for j in range(TT)]
        CO = [sum(CW[:j]) for j in range(TT)]
        CWS = sum(CW)
        st_z = place("st_z", [P, CWS], F32, s1)
        st_e = place("st_e", [P, CWS], F32, s1 + CWS)
        st_l = place("st_l", [P, CWS], F32, s1 + 2 * CWS)
        st_a = place("st_a", [P, CWS], F32, s1 + 3 * CWS)
        ml_v = place("ml_v", [P, TT, D], F32, big + 16 * S)
        ml_r = place("ml_rows", [8, 8, S], F32, h_at)
        ml_e = place("ml_e", [P, CWS], F32, big + 12288)
        ml_a = place("ml_a", [P, CWS], F32, big + 12288 + CWS)
        ml_d = place("ml_d", [P, S], F32, big + 12288 + 2 * CWS)
        ml_x = place("ml_x", [P, S], F32, big + 12288 + 2 * CWS + S)
        swa_v = place("swa_v", [P, TT, P], F32, big + 9 * S)
        swa_k = place("swa_k", [P, 2, S], F32, big + 10 * S)
        rope_cs = place("rope_cs", [P, 2, S], F32, big + 12288)
        rope_t = [place(f"rope_t{r}", [P, S], F32, big + 13312 + r * S) for r in range(4)]
        rope_i = place("rope_i", [P, S], I32, big + 13312 + 4 * S)
        hg_v = place("hg_v", [P, TT, D], F32, big + 24 * S)
        hg_c = place("hg_cf", [P, S], F32, big + 16384)
        hg_k = place("hg_k", [P, S], F32, big + 16384 + S)
        hg_s = place("hg_s", [P, S], F32, big + 16384 + 2 * S)
        hg_d = [place(f"hg_d{r}", [P, S], F32, h_at + r * S) for r in range(2)]
        hg_q = [place(f"hg_q{r}", [P, S], F32, h_at + (2 + r) * S) for r in range(2)]
        hg_t = [place(f"hg_t{r}", [P, S], F32, h_at + (4 + r) * S) for r in range(2)]
        hg_p = place("hg_p", [P, TT, 640], F32, h_at + 6 * S)
        hg_one = place("hg_one", [P, S], F32, h_at + 11 * S)
        df_v = place("df_v", [P, TT, D], F32, big + 16 * S)

        bank = [ctx.enter_context(nc.psum_tensor(f"bank{b}", [P, S], F32)) for b in range(8)]

        def kept_at(name):
            at = 0
            for k, w in KEPT.items():
                if k == name:
                    return kp[:, at:at + w]
                at += w

        ident, ones, block64 = kept_at("ident"), kept_at("ones"), kept_at("block64")
        eps6, eps5, tiny = kept_at("eps6"), kept_at("eps5"), kept_at("tiny")

        def col(name, j=0, n=1):
            a = COLS[name][0]
            return co[:, a + j:a + j + n]

        dist, causal, logmult = tables[:, 0, :], tables[:, 1, :], tables[:, 2, :]
        gates = small[:, 0:48]
        kcmp = small[:, 48:80]
        vcmp = small[0:32, 80:144]
        att_max = [small[:, 144 + r:145 + r] for r in range(2)]
        att_sum = [small[:, 146 + r:147 + r] for r in range(2)]
        att_inv = [small[:, 148 + r:149 + r] for r in range(2)]
        lam = small[:, 150:151]
        lam_w = small[:, 151:157]
        hid_cmp = place("hid_cmp", [P, 4, 32], F32, s1 + 5648)
        hid_pre = place("hid_pre", [P, 4, 32], F32, s1 + 5776)
        ml_w = small[:, 0:16]
        lb = small[:, 0:8]
        one_lb = small[:, 8:16]
        lb_w = small[:, 16:80]

        names = ["const_loaded", "layer_const_loaded", "pos_loaded", "hi_done", "lo_done", "slot_used", "lin_free",
                 "ada_used", "ada_sum", "ada_mod", "cond_done", "sil_done", "part_hi", "part_lo", "n_sq", "n_sum",
                 "n_root", "h_ready", "ln_mean", "ln_centred", "ln_y", "ln_x", "x_scaled", "g_sq", "g_sum", "g_root",
                 "g_out", "att_scores", "att_ready", "att_exp", "att_normed", "att_turned", "att_copied", "att_pv",
                 "att_out", "gate_in", "gate_pre", "gate_out", "blk_ready", "blk_hi_done", "blk_lo_done", 
                 "cmp_act", "cmp_mm", "cmp_sq", "cmp_root", "cmp_out", "v_turned", "v_out", "mix_ready",
                 "st_scores", "st_scaled", "st_log", "st_keep", "st_suffix", "st_arg", "st_attn", "st_pv", "st_out",
                 "rope_ready", "rope_mm", "rope_out", "rope_ang", "ml_gate", "ml_pre", "ml_log", "ml_rows",
                 "ml_turn", "ml_w", "ml_spread", "ml_diag", "ml_exp", "ml_a", "ml_den", "ml_num", "ml_out", "ml_sig",
                 "hg_lb", "hg_lbe", "hg_sig", "hg_dec", "hg_log", "hg_diff", "hg_e", "hg_qk", "hg_mm", "hg_put",
                 "hg_pv", "hg_out", "hg_gate", "lam_in", "lam_exp", "lam_done", "stored",
                 "act_chain", "dve_chain"]
        sm = namedtuple("Semaphores", names)(*[ctx.enter_context(nc.semaphore(name)) for name in names])
        raw_loaded = [ctx.enter_context(nc.semaphore(f"raw_loaded{r}")) for r in range(RING)]
        ada_loaded = [ctx.enter_context(nc.semaphore(f"ada_loaded{r}")) for r in range(ADA_RING)]

        def half(tile_index, head):
            return proj[HD * (head % 2):HD * (head % 2) + HD, tile_index, :]

        def job(q, k, width, bias_ap, values, **more):
            return dict(q=q, k=k, w=width, bias=bias_ap, v=values, sink=None, vis=None, gate=None, first=True,
                        last=True, dv=HD, row=0, dest=None) | more

        def nsa_jobs():
            jobs = []
            for hd in range(NSA_HEADS):
                b = HD * (hd % 2)
                for i in range(TT):
                    q = half(hd // 2, hd)[:, i * P:(i + 1) * P]
                    w = (i + 1) * P
                    common = dict(row=b, dest=q)
                    tok = dict(bias_ap=bias[:, hd, S - w:S])
                    gate = [gates[:, i * 12 + hd * 3 + br:i * 12 + hd * 3 + br + 1] for br in range(3)]
                    jobs.append(job(q, kcmp[b:b + HD, 0:NCMP], NCMP, cmp_bias[:, hd, i * NCMP:(i + 1) * NCMP],
                                    [(vcmp[0:NCMP, :], NCMP)], vis=lc[:, 124 + i * NCMP:124 + (i + 1) * NCMP],
                                    gate=gate[0], last=False, **common))
                    jobs.append(job(q, half(9, hd)[:, 0:w], w, values=[(v_slc[:, j, :], P) for j in range(i + 1)],
                                    gate=gate[1], first=False, last=False, **tok, **common))
                    jobs.append(job(q, half(10, hd)[:, 0:w], w, values=[(v_win[:, j, :], P) for j in range(i + 1)],
                                    gate=gate[2], first=False, **tok, **common))
            return jobs

        def dil_jobs():
            jobs = []
            for hd in range(4):
                for i in range(TT):
                    q, w = half(6 + hd // 2, hd)[:, i * P:(i + 1) * P], (i + 1) * P
                    jobs.append(job(q, half(17 + hd // 2, hd)[:, 0:w], w, bias[:, hd, S - w:S],
                                    [(first_vd[:, j, hd * HD:(hd + 1) * HD], P) for j in range(i + 1)],
                                    row=HD * (hd % 2), dest=q))
            return jobs

        def swa_jobs():
            jobs = []
            for hd in range(16):
                kv = hd // 8
                b = HD * (hd % 2)
                for i in range(TT):
                    q, lo = half(hd // 2, hd)[:, i * P:(i + 1) * P], max(0, i - 1)
                    w = (i + 1 - lo) * P
                    jobs.append(job(q, swa_k[b:b + HD, kv, lo * P:(i + 1) * P], w, lc[:, 512 - w:512],
                                    [(swa_v[:, j, kv * HD:(kv + 1) * HD], P) for j in range(lo, i + 1)],
                                    sink=col("sinks", hd), row=b, dest=q))
            return jobs

        def diff_jobs():
            jobs = []
            for hd in range(8):
                for i in range(TT):
                    w = (i + 1) * P
                    for c in range(2):
                        jobs.append(job(proj[HD * c:HD * c + HD, hd, i * P:(i + 1) * P],
                                        proj[HD * c:HD * c + HD, 8 + hd, 0:w], w, lc[:, 768 - w:768],
                                        [(df_v[:, j, hd * P:(hd + 1) * P], P) for j in range(i + 1)],
                                        gate=lam if c else None, first=c == 0, last=c == 1, dv=P,
                                        dest=proj[:, hd, i * P:(i + 1) * P]))
            return jobs

        def item(src, mat, scale, gain, out, mul=None):
            return dict(src=src, mat=mat, scale=scale, gain=gain, out=out, mul=mul)

        def first_norms():
            items = []
            for t, g in ((0, "g_q_nsa"), (1, "g_q_nsa"), (6, "g_q_dil"), (7, "g_q_dil"), (17, "g_k_dil"),
                         (18, "g_k_dil")):
                items.append(item([proj[:, t, :]], block64, 1.0, [col(g)], [[proj[:, t, :]]]))
            for t, g in ((9, "g_k_slc"), (10, "g_k_win")):
                items.append(item([proj[0:HD, t, :]], block64[0:HD, 0:HD], 1.0, [col(g)[0:HD, :]],
                                  [[proj[HD:P, t, :], proj[0:HD, t, :]]]))
            return items

        def out_norms(part):
            if part == "first":
                return [item([proj[:, t, :]], block64, 1.0, [col("g_out", t)], [[proj[:, t, :]]]) for t in range(DT)]
            if part == 0:
                return [item([proj[:, 2 * g + e, :] for e in range(2)], ones, 1 / 256,
                             [col("mlstm_norm", 2 * g + e) for e in range(2)],
                             [[proj[:, 2 * g + e, :]] for e in range(2)], [proj[:, 8 + 2 * g + e, :] for e in range(2)])
                        for g in range(4)]
            if part == 2:
                return [item([proj[:, t, :]], ones, 1 / P, [col("hgrn_norm", t)], [[proj[:, t, :]]],
                             [proj[:, 16 + t, :]]) for t in range(DT)]
            if part == 3:
                return [item([proj[:, t, :]], ones, 1 / P, [lam_w[:, 5:6]], [[proj[:, t, :]]]) for t in range(DT)]
            return []

        def mod_col(layer, sub, kind, j, n=1):
            a = sub * 24 + kind * 8 + j
            return mod[layer % 2][:, a:a + n]

        SHIFT, ONE_SCALE, ONE_GATE = range(3)
        LV = [256, 128, 64, 32, 16, 8, 4, 2, 1]
        block = ctx.enter_context(nc.Block())

        @block.sync
        def _(sp):
            n = Counts()

            def load_slot(k, i=0, step=0):
                if k >= RING:
                    sp.wait_ge(sm.lo_done, k - RING + 1 + step * i)
                sp.dma_start(raw[k % RING][:, :, :].rearrange("p a b -> p (a b)"),
                             wstream[k + step * i, :, :]).then_inc(raw_loaded[k % RING], 16)

            def load_ada(a, i=0, step=0):
                if a >= ADA_RING or not isinstance(i, int):
                    sp.wait_ge(sm.ada_used, a - ADA_RING + 1 + step * i)
                sp.dma_start(ada_raw[a % ADA_RING][:, :],
                             ada[a + step * i, :, :]).then_inc(ada_loaded[a % ADA_RING], 16)

            def load_slots(count):
                k = n["slot"]
                n.add(slot=count)
                if k == 0:
                    for q in range(RING):
                        load_slot(q)
                    k, count = RING, count - RING
                with loop(sp, count // RING) as i:
                    for q in range(RING):
                        load_slot(k + q, i, RING)
                for q in range(count // RING * RING, count):
                    load_slot(k + q)

            def load_ffn(with_ada):
                k, a = n["slot"], n["ada"]
                first = 0
                if a == 0 and with_ada:
                    for q in range(8):
                        load_slot(k + q)
                        load_ada(a + q)
                    first = 1
                with sp.Fori(first, 5) as i:
                    for q in range(8):
                        load_slot(k + q, i, 8)
                        if with_ada:
                            load_ada(a + q, i, 8)
                for lot, more in ((range(40, 43), range(40, 46)), (range(43, 45), range(46, 48))):
                    for q in lot:
                        load_slot(k + q)
                    if with_ada:
                        for q in more:
                            load_ada(a + q)
                n.add(slot=2 * FT + 1, ada=48 if with_ada else 0)
                load_slots(3 * DT - 1)

            sp.dma_start(x[:, :, :], xT).then_inc(sm.const_loaded, 16)
            sp.dma_start(co[:, :], cols).then_inc(sm.const_loaded, 16)
            sp.dma_start(kp[:, :], kept).then_inc(sm.const_loaded, 16)
            sp.dma_start(lc[:, :], layerc[0, :, :]).then_inc(sm.layer_const_loaded, 16)
            sp.dma_start(tables[:, :, :].rearrange("p a b -> p (a b)"), bigc).then_inc(sm.const_loaded, 16)
            for at, part in enumerate(parts):
                tiles, values = IN_PROJ[part]
                if part != "first":
                    sp.wait_ge(sm.part_lo, PARTS_SPLIT * at)
                    sp.dma_start(lc[:, :], layerc[1 + part, :, :]).then_inc(sm.layer_const_loaded, 16)
                load_slots(len(tiles) + len(values))
                if part in (1, 3):
                    sp.wait_ge(sm.lin_free, lin_total(parts[:at]))
                    sp.dma_start(rope_i[:, :], pos).then_inc(sm.pos_loaded, 16)
                if part == "first":
                    load_slots(8)
                load_slots(DT)
                load_ffn(at + 1 < len(parts))
            if parts[-1] == "first":
                sp.wait_ge(sm.lin_free, lin_total(parts))
            else:
                sp.wait_ge(sm.ln_x, 2 * DT * (len(parts) - 1))
            sp.dma_start(yT, x[:, :, :]).then_inc(sm.stored, 16)
            sp.wait_ge(sm.stored, 16)

        @block.gpsimd
        def _(pool):
            def low(k, i=0, step=0):
                pool.wait_ge(sm.hi_done, k + 1 + step * i)
                nc.gpsimd.tensor_tensor(w_lo[k % RING][:, :, :], raw[k % RING][:, :, :],
                                        w_hi[k % RING][:, :, :].bitcast(F32), ALU.subtract).then_inc(sm.lo_done, 1)

            with pool.Fori(0, slots_total // RING) as i:
                for q in range(RING):
                    low(q, i, RING)
            for k in range(slots_total // RING * RING, slots_total):
                low(k)

        @block.tensor
        def _(pe):
            n = Counts()
            mm, turn = nc.tensor.matmul, nc.tensor.transpose

            def slot_products(k, i, step, pairs, first, last):
                pe.wait_ge(sm.lo_done, k + 1 + step * i)
                r = k % RING
                for at, (out, w, hi, lo) in enumerate(pairs):
                    begin, end = first and w == 0, last and w == len(pairs) - 1
                    mm(out, w_hi[r][:, at, :], hi, start=first and at == 0, stop=False)
                    mm(out, w_hi[r][:, at, :], lo, start=False, stop=False)
                    op = mm(out, w_lo[r][:, at, :], hi, start=False, stop=last and at == len(pairs) - 1)
                op.then_inc(sm.slot_used, 1)

            def m_tile(k, mt, i, step, mt_step, hi, lo, chunks):
                if mt >= 4:
                    pe.wait_ge(sm.lin_free, mt - 3 + mt_step * i)
                c0 = 0
                for s, m in enumerate(chunks):
                    slot_products(k + s, i, step,
                                  [(bank[mt % 4][:, 0:hi.shape[2]], c, hi[:, c0 + c, :], lo[:, c0 + c, :])
                                   for c in range(m)], s == 0, s == len(chunks) - 1)
                    c0 += m

            def linear(tiles, hi, lo, chunks):
                k, mt, per = n["slot"], n["mt"], len(chunks)
                done = 0
                if mt < 4:
                    for q in range(4):
                        m_tile(k + q * per, mt + q, 0, 0, 0, hi, lo, chunks)
                    done = 4
                count = (tiles - done) // 4
                if count:
                    with loop(pe, count) as i:
                        for q in range(4):
                            m_tile(k + (done + q) * per, mt + done + q, i, 4 * per, 4, hi, lo, chunks)
                for q in range(done + 4 * count, tiles):
                    m_tile(k + q * per, mt + q, 0, 0, 0, hi, lo, chunks)
                n.add(slot=tiles * per, mt=tiles)

            def value_tile(k, mt, i, step):
                pe.wait_ge(sm.lin_free, mt - 3 + step * i)
                pe.wait_ge(sm.lo_done, k + 1 + step * i)
                r = k % RING
                for t in range(TT):
                    out, tok = bank[mt % 4][:, t * P:(t + 1) * P], slice(t * P, (t + 1) * P)
                    for c in range(DT):
                        mm(out, h_hi[:, c, tok], w_hi[r][:, c, :], start=c == 0, stop=False)
                        mm(out, h_hi[:, c, tok], w_lo[r][:, c, :], start=False, stop=False)
                        op = mm(out, h_lo[:, c, tok], w_hi[r][:, c, :], start=False, stop=c == DT - 1)
                op.then_inc(sm.slot_used, 1)

            def value_tiles(count):
                k, mt = n["slot"], n["mt"]
                n.add(slot=count, mt=count)
                if count >= 8:
                    with loop(pe, count // 4) as i:
                        for q in range(4):
                            value_tile(k + q, mt + q, i, 4)
                else:
                    for q in range(count):
                        value_tile(k + q, mt + q, 0, 0)

            def wait_parts(count):
                n.add(part=count)
                pe.wait_ge(sm.part_lo, n["part"])

            def mean_squares():
                for c in range(DT):
                    pe.wait_ge(sm.n_sq, n["sq"] + c + 1)
                    mm(bank[6][:, :], ones, sq[c % 2][:, :], start=c == 0, stop=c == DT - 1).then_inc(sm.n_sum, 1)
                n.add(sq=DT)

            def layer_norm():
                pe.wait_ge(sm.lin_free, n["mt"])
                for c in range(DT):
                    op = mm(bank[5][:, :], ones, x[:, c, :], start=c == 0, stop=c == DT - 1)
                op.then_inc(sm.ln_mean, 1)
                mean_squares()

            def group_norms(items):
                for t, it in enumerate(items):
                    wait(pe, sm.g_root, n["gn"] + t - 1)
                    for u in range(len(it["src"])):
                        n.add(gt=1)
                        pe.wait_ge(sm.g_sq, n["gt"])
                        rows = it["src"][u].shape[0]
                        mm(bank[6 + t % 2][0:rows, :], it["mat"], sq[(n["gt"] - 1) % 2][0:rows, :],
                           start=u == 0, stop=u == len(it["src"]) - 1).then_inc(sm.g_sum, 1)
                n.add(gn=len(items))

            def attention(jobs, bufs):
                a, g = n["att"], n["att_g"]
                for step in range(len(jobs) + 2):
                    if step < len(jobs):
                        j, it = step, jobs[step]
                        wait(pe, sm.att_ready, a + j - 1)
                        mm(bank[j % 2][:, 0:it["w"]], it["q"], it["k"], start=True,
                           stop=True).then_inc(sm.att_scores, 1)
                    if 1 <= step <= len(jobs):
                        j, it = step - 1, jobs[step - 1]
                        pe.wait_ge(sm.att_normed, a + j + 1)
                        wait(pe, sm.att_copied, a + j - 1)
                        at = 0
                        for t, (_, keys) in enumerate(it["v"]):
                            op = turn(bank[2 + j % 2][0:keys, t * P:(t + 1) * P], bufs["p"][j % 2][:, at:at + keys],
                                      ident)
                            at += keys
                        op.then_inc(sm.att_turned, 1)
                    if step >= 2:
                        j, it = step - 2, jobs[step - 2]
                        pe.wait_ge(sm.att_copied, a + j + 1)
                        if it["first"]:
                            g += 1
                            wait(pe, sm.att_out, g - 2)
                        out = bank[4 + g % 2][it["row"]:it["row"] + it["dv"], 0:P]
                        for t, (v, keys) in enumerate(it["v"]):
                            op = mm(out, v, bufs["pt"][j % 2][0:keys, t * P:(t + 1) * P],
                                    start=it["first"] and t == 0, stop=it["last"] and t == len(it["v"]) - 1)
                        op.then_inc(sm.att_pv, 1)
                n.add(att=len(jobs), att_g=sum(it["last"] for it in jobs))

            def first_mixer():
                for kv in range(2):
                    if kv == 0:
                        pe.wait_ge(sm.blk_lo_done, 2)
                    linear(2, blk_hi[:, kv, :, :], blk_lo[:, kv, :, :], [8, 8])
                pe.wait_ge(sm.cmp_act, 2)
                w2 = [col("w2", 128 * kv, 128).rearrange("p (m d) -> p m d", m=2) for kv in range(2)]
                for m in range(2):
                    op = mm(bank[4][0:HD, 0:32], w2[0][:, m, :], hid_cmp[:, m, :], start=m == 0, stop=m == 1)
                for m in range(2):
                    op = mm(bank[5][0:32, 0:HD], hid_cmp[:, 2 + m, :], w2[1][:, m, :], start=m == 0, stop=m == 1)
                op.then_inc(sm.cmp_mm, 1)
                pe.wait_ge(sm.cmp_sq, 1)
                mm(bank[6][0:HD, 0:32], block64[0:HD, 0:HD], hid_pre[0:HD, 0, :], start=True,
                   stop=True).then_inc(sm.cmp_mm, 1)
                for b, tile in ((0, 9), (1, 10)):
                    for t in range(TT):
                        op = turn(bank[7][:, (b * TT + t) * HD:(b * TT + t + 1) * HD],
                                  proj[HD:P, tile, t * P:(t + 1) * P], ident[HD:P, HD:P])
                op.then_inc(sm.v_turned, 1)
                pe.wait_ge(sm.cmp_root, 1)
                pe.wait_ge(sm.v_out, 1)
                group_norms(first_norms())
                pe.wait_ge(sm.mix_ready, 1)
                attention(nsa_jobs(), AT["first"])
                stick_breaking()
                pe.wait_ge(sm.mix_ready, 2)
                attention(dil_jobs(), AT["first"])

            def stick_breaking():
                suffix, every = lc[:, 384:512], ones
                for hd in range(4):
                    q, k = half(4 + hd // 2, hd), half(15 + hd // 2, hd)
                    wait(pe, sm.st_arg, hd)
                    if hd == 0:
                        pe.wait_ge(sm.att_out, n["att_g"])
                    for j in range(TT):
                        op = mm(bank[j][:, 0:CW[j]], k[:, j * P:(j + 1) * P], q[:, j * P:S], start=True, stop=True)
                    op.then_inc(sm.st_scores, 1)
                    pe.wait_ge(sm.st_keep, hd + 1)
                    for j in range(TT):
                        for jj in range(j, TT):
                            op = mm(bank[j][:, P * (jj - j):CW[j]], suffix if jj == j else every,
                                    st_l[:, CO[jj]:CO[jj] + CW[jj]], start=jj == j, stop=jj == TT - 1)
                    op.then_inc(sm.st_suffix, 1)
                    pe.wait_ge(sm.st_attn, hd + 1)
                    b = HD * (hd % 2)
                    wait(pe, sm.st_out, hd - 1)
                    for j in range(TT):
                        op = mm(bank[4 + hd % 2][b:b + HD, j * P:S], first_vc[:, j, hd * HD:(hd + 1) * HD],
                                st_a[:, CO[j]:CO[j] + CW[j]], start=j == 0, stop=j == TT - 1)
                    op.then_inc(sm.st_pv, 1)

            def rope(tiles):
                pe.wait_ge(sm.layer_const_loaded, 16 * n["lc"])
                for t in tiles:
                    wait(pe, sm.rope_out, n["rope"] - 1)
                    mm(bank[4 + n["rope"] % 2][:, :], lc[:, 0:128], proj[:, t, :], start=True,
                       stop=True).then_inc(sm.rope_mm, 1)
                    n.add(rope=1)

            def mlstm_gates():
                gw = col("mlstm_gw", 0, 64).rearrange("p (c g) -> p c g", c=DT)
                for g in range(2):
                    for c in range(DT):
                        op = mm(bank[6 + g][0:4, :], gw[:, c, 4 * g:4 * g + 4], h_tmp[:, c, :], start=c == 0,
                                stop=c == DT - 1)
                op.then_inc(sm.ml_gate, 1)

            def mlstm():
                pe.wait_ge(sm.ml_rows, 1)
                for t in range(TT):
                    op = turn(bank[0][:, 4 * t:4 * t + 4], ml_r[0:4, 4, t * P:(t + 1) * P], ident[0:4, 0:4])
                op.then_inc(sm.ml_turn, 1)
                pe.wait_ge(sm.ml_w, 1)
                for hd in range(4):
                    q, k = proj[:, 2 * hd, :], proj[:, 2 * hd + 1, :]
                    sel = lc[0:4, hd * P:(hd + 1) * P]
                    wait(pe, sm.ml_out, hd)
                    mm(bank[0][:, :], sel, ml_r[0:4, 5, :], start=True, stop=True)
                    mm(bank[1][:, :], sel, ml_r[0:4, 6, :], start=True, stop=True)
                    for j in range(TT):
                        op = mm(bank[2 + j][:, 0:CW[j]], k[:, j * P:(j + 1) * P], q[:, j * P:S], start=True, stop=True)
                    op.then_inc(sm.ml_spread, 1)
                    pe.wait_ge(sm.ml_a, hd + 1)
                    for j in range(TT):
                        op = mm(bank[6][:, j * P:S], ones, ml_a[:, CO[j]:CO[j] + CW[j]], start=j == 0,
                                stop=j == TT - 1)
                    op.then_inc(sm.ml_den, 1)
                    for e in range(2):
                        for j in range(TT):
                            op = mm(bank[7 if e else 0][:, j * P:S], ml_v[:, j, hd * 256 + e * P:hd * 256 + (e + 1) * P],
                                    ml_a[:, CO[j]:CO[j] + CW[j]], start=j == 0, stop=j == TT - 1)
                    op.then_inc(sm.ml_num, 1)

            def hgrn():
                for hd in range(8):
                    for at, b in enumerate(LV + [0]):
                        m = hd * 10 + at
                        pe.wait_ge(sm.hg_qk, m + 1)
                        wait(pe, sm.hg_put, m - 1)
                        kk = hg_t[m % 2] if b else hg_k
                        qq = hg_q[m % 2][:, :] if b else proj[:, hd, :]
                        if b == 256:
                            for j in range(2):
                                op = mm(bank[j][:, 0:256], kk[:, j * P:(j + 1) * P], qq[:, 256:S], start=True, stop=True)
                        elif b == 128:
                            for j in (0, 2):
                                op = mm(bank[2][:, j * 64:j * 64 + P], kk[:, j * P:(j + 1) * P],
                                        qq[:, (j + 1) * P:(j + 2) * P], start=True, stop=True)
                        else:
                            for j in range(TT):
                                op = mm(bank[4 + m % 2][:, j * P:(j + 1) * P], kk[:, j * P:(j + 1) * P],
                                        qq[:, j * P:(j + 1) * P], start=True, stop=True)
                        op.then_inc(sm.hg_mm, 1)
                    pe.wait_ge(sm.hg_put, hd * 10 + 10)
                    wait(pe, sm.hg_out, hd - 1)
                    for j in range(TT):
                        op = mm(bank[6 + hd % 2][:, j * P:S], hg_v[:, j, hd * P:(hd + 1) * P], hg_p[:, j, 0:CW[j]],
                                start=j == 0, stop=j == TT - 1)
                    op.then_inc(sm.hg_pv, 1)

            def ffn(with_ada):
                k, mt, cg, a = n["slot"], n["mt"], n["cg"], n["ada"]

                def up(q, i):
                    for s in range(2):
                        m_tile(k + 2 * q + s, mt + 2 * q + s, i, 8, 8, h_hi, h_lo, [8])

                def ada_sums(g, i):
                    if not with_ada:
                        return
                    pe.wait_ge(sm.ada_used, a + 8 * g + 8 + 8 * i)
                    for j in range(8):
                        op = mm(bank[7][:, j:j + 1], ada_acc[:, j * P:(j + 1) * P], ones[:, 0:1], start=True, stop=True)
                    op.then_inc(sm.ada_sum, 1)

                with pe.Fori(0, 5) as i:
                    for q in range(4):
                        up(q, i)
                    ada_sums(0, i)
                for q in range(20, 22):
                    up(q, 0)
                ada_sums(5, 0)
                n.add(slot=2 * FT, mt=2 * FT, ada=48 if with_ada else 0, cg=6 if with_ada else 0)
                wait_parts(FT)
                linear(DT, hid_hi, hid_lo, [8, 8, 6])

            pe.wait_ge(sm.const_loaded, 64)
            for at, part in enumerate(parts):
                tiles, values = IN_PROJ[part]
                n.add(lc=1)
                if part == "first":
                    mean_squares()
                wait_parts(DT)
                if part == "first":
                    gw = col("gate_w", 0, 96).rearrange("p (c g) -> p c g", c=DT)
                    for t in range(TT):
                        for c in range(DT):
                            op = mm(bank[6][:, t * 12:(t + 1) * 12], h_tmp[:, c, t * P:(t + 1) * P], gw[:, c, :],
                                    start=c == 0, stop=c == DT - 1)
                    op.then_inc(sm.gate_in, 1)
                if part == 0:
                    mlstm_gates()
                linear(len(tiles), h_hi, h_lo, [8])
                value_tiles(len(values))
                pe.wait_ge(sm.layer_const_loaded, 16 * n["lc"])
                pe.wait_ge(sm.lin_free, n["mt"])
                if part == "first":
                    first_mixer()
                elif part == 0:
                    mlstm()
                elif part == 1:
                    rope(range(9))
                    pe.wait_ge(sm.mix_ready, n["mix"] + 1)
                    attention(swa_jobs(), AT["late"])
                elif part == 2:
                    hgrn()
                else:
                    rope(range(16))
                    pe.wait_ge(sm.mix_ready, n["mix"] + 1)
                    attention(diff_jobs(), AT["late"])
                n.add(mix=mix_steps(part))
                group_norms(out_norms(part))
                wait_parts(DT)
                linear(DT, h_hi, h_lo, [8])
                if part == "first":
                    pe.wait_ge(sm.lin_free, n["mt"])
                    mean_squares()
                else:
                    layer_norm()
                wait_parts(DT)
                ffn(at + 1 < len(parts))
                if part != "first":
                    layer_norm()

        @block.scalar
        def _(act):
            n = Counts()
            fn = nc.scalar.activation

            def link(ins):
                n.add(act_chain=1)
                ins.then_inc(sm.act_chain, 1)
                act.wait_ge(sm.act_chain, n["act_chain"])

            def split(t, i=0, step=0):
                if not isinstance(i, int) or t < slots_total:
                    act.wait_ge(raw_loaded[t % RING], 16 * (t // RING + 1) + 16 * step // RING * i)
                    if t >= RING:
                        act.wait_ge(sm.slot_used, t - RING + 1 + step * i)
                    fn(w_hi[t % RING][:, :, :], raw[t % RING][:, :, :], ACT.Copy).then_inc(sm.hi_done, 1)

            def split_ahead(count):
                k = n["slot"]
                n.add(slot=count)
                done = 0
                if k + LEAD < RING:
                    for q in range(RING):
                        split(k + q + LEAD)
                    done = RING
                full = (count - done) // RING
                if k + LEAD + count > slots_total:
                    full = 0
                if full:
                    with loop(act, full) as i:
                        for q in range(RING):
                            split(k + done + q + LEAD, i, RING)
                for q in range(done + full * RING, count):
                    split(k + q + LEAD)

            def mean_squares(eps, ready):
                for c in range(DT):
                    ready(c)
                    wait(act, sm.n_sum, n["sq"] + c - 1)
                    fn(sq[c % 2][:, :], x[:, c, :], ACT.Square).then_inc(sm.n_sq, 1)
                n.add(sq=DT)
                act.wait_ge(sm.n_sum, n["sq"])
                fn(rt[0][:, :], bank[6][:, :], ACT.Sqrt, bias=eps, scale=1 / D).then_inc(sm.n_root, 1)

            def high_parts(sources, ready):
                for c, src in enumerate(sources):
                    ready(c)
                    fn(h_hi[:, c, :], src, ACT.Copy).then_inc(sm.part_hi, 1)
                n.add(part=len(sources))

            def split_input(scaled):
                high_parts([h_tmp[:, c, :] for c in range(DT)],
                           lambda c: act.wait_ge(sm.h_ready, n["h"] + c + 1))
                n.add(h=DT)
                if scaled:
                    for c in range(DT):
                        nc.scalar.mul(x[:, c, :], x[:, c, :], ALPHA).then_inc(sm.x_scaled, 1)

            def layer_norm():
                mean_squares(eps5, lambda c: act.wait_ge(sm.ln_centred, n["ln"] * DT + c + 1))
                for c in range(DT):
                    act.wait_ge(sm.ln_y, n["ln"] * DT + c + 1)
                    fn(x[:, c, :], x[:, c, :], ACT.Identity,
                       bias=col("ln_b", n["ln_at"] * 8 + c)).then_inc(sm.ln_x, 1)
                n.add(ln=1)

            def group_norms(items):
                def root(t):
                    it = items[t]
                    act.wait_ge(sm.g_sum, sums[t])
                    wait(act, sm.g_out, n["gn"] + t - 1)
                    r = it["src"][0].shape[0]
                    fn(rt[t % 2][0:r, :], bank[6 + t % 2][0:r, :], ACT.Sqrt, bias=eps6[0:r, :],
                       scale=it["scale"]).then_inc(sm.g_root, 1)

                sums = []
                for t, it in enumerate(items):
                    for src in it["src"]:
                        wait(act, sm.g_sum, n["gt"] - 1)
                        fn(sq[n["gt"] % 2][0:src.shape[0], :], src, ACT.Square).then_inc(sm.g_sq, 1)
                        n.add(gt=1)
                    sums.append(n["gt"])
                    if t:
                        root(t - 1)
                if items:
                    root(len(items) - 1)
                n.add(gn=len(items))

            def attention(jobs, bufs):
                a = n["att"]
                for step in range(len(jobs) + 1):
                    if step < len(jobs):
                        j, it = step, jobs[step]
                        w = it["w"] + (it["sink"] is not None)
                        act.wait_ge(sm.att_ready, a + j + 1)
                        wait(act, sm.att_turned, a + j - 1)
                        fn(bufs["p"][j % 2][:, 0:w], bufs["s"][j % 2][:, 0:w], ACT.Exp, bias=att_max[j % 2],
                           accum_out=att_sum[j % 2]).then_inc(sm.att_exp, 1)
                    if step >= 1:
                        j, it = step - 1, jobs[step - 1]
                        act.wait_ge(sm.att_turned, a + j + 1)
                        wait(act, sm.att_pv, a + j - 1)
                        r, w = it["v"][0][1], len(it["v"]) * P
                        fn(bufs["pt"][j % 2][0:r, 0:w], bank[2 + j % 2][0:r, 0:w], ACT.Copy).then_inc(sm.att_copied, 1)
                n.add(att=len(jobs))

            def first_mixer():
                act.wait_ge(sm.blk_ready, 2)
                for kv in range(2):
                    fn(blk_hi[:, kv, :, :], blk[:, kv, :, :], ACT.Copy).then_inc(sm.blk_hi_done, 1)
                split_ahead(8)
                for kv in range(2):
                    act.wait_ge(sm.lin_free, n["mt"] + 2 * kv + 2)
                    fn(hid_cmp[:, 2 * kv:2 * kv + 2, :], hid_pre[:, 2 * kv:2 * kv + 2, :],
                       ACT.Gelu_apprx_tanh).then_inc(sm.cmp_act, 1)
                act.wait_ge(sm.cmp_mm, 1)
                fn(hid_pre[0:HD, 0, :], bank[4][0:HD, 0:32], ACT.Square).then_inc(sm.cmp_sq, 1)
                act.wait_ge(sm.cmp_mm, 2)
                fn(hid_pre[0:HD, 1, :], bank[6][0:HD, 0:32], ACT.Sqrt, bias=eps6[0:HD, :]).then_inc(sm.cmp_root, 1)
                group_norms(first_norms())
                attention(nsa_jobs(), AT["first"])
                act.wait_ge(sm.att_out, TT * NSA_HEADS)
                for hd in range(4):
                    act.wait_ge(sm.st_scores, hd + 1)
                    for j in range(TT):
                        op = fn(st_z[:, CO[j]:CO[j] + CW[j]], bank[j][:, 0:CW[j]], ACT.Copy, scale=SCALE)
                    link(op)
                    link(fn(st_e[:, :], st_z[:, :], ACT.Abs))
                    link(fn(st_e[:, :], st_e[:, :], ACT.Exp, scale=-1.0))
                    fn(st_e[:, :], st_e[:, :], ACT.Ln, bias=1.0).then_inc(sm.st_log, 1)
                    act.wait_ge(sm.st_arg, hd + 1)
                    wait(act, sm.st_pv, hd)
                    fn(st_a[:, :], st_e[:, :], ACT.Exp).then_inc(sm.st_attn, 1)
                attention(dil_jobs(), AT["first"])

            def rope_tables():
                n.add(rt=1)
                for f in range(2):
                    act.wait_ge(sm.rope_ang, 2 * n["rt"] - 1 + f)
                    fn(rope_cs[:, 1 - f, :], rope_t[f][:, :], ACT.Sin).then_inc(sm.rope_ready, 1)

            def mlstm():
                act.wait_ge(sm.ml_pre, 1)
                link(fn(ml_r[0:4, 2, :], ml_r[0:4, 1, :], ACT.Abs))
                link(fn(ml_r[0:4, 2, :], ml_r[0:4, 2, :], ACT.Exp, scale=-1.0))
                fn(ml_r[0:4, 2, :], ml_r[0:4, 2, :], ACT.Ln, bias=1.0).then_inc(sm.ml_log, 1)
                act.wait_ge(sm.ml_pre, 2)
                fn(ml_r[0:4, 6, :], ml_r[0:4, 2, :], ACT.Exp, scale=-1.0).then_inc(sm.ml_rows, 1)
                act.wait_ge(sm.ml_w, 1)
                for hd in range(4):
                    act.wait_ge(sm.ml_spread, hd + 1)
                    fn(ml_x[:, :], bank[1][:, :], ACT.Copy)
                    act.wait_ge(sm.ml_diag, hd + 1)
                    for j in range(TT - 1):
                        fn(ml_e[:, CO[j] + P:CO[j] + CW[j]], bank[0][:, (j + 1) * P:S], ACT.Exp, scale=-1.0,
                           bias=ml_w[:, 4 * j + hd:4 * j + hd + 1])
                    for j in range(TT):
                        op = fn(ml_e[:, CO[j]:CO[j] + P], ml_d[:, j * P:(j + 1) * P], ACT.Exp, scale=-1.0,
                                bias=ml_w[:, 4 * j + hd:4 * j + hd + 1])
                    op.then_inc(sm.ml_exp, 1)
                for t in range(8, 16):
                    op = fn(proj[:, t, :], proj[:, t, :], ACT.Sigmoid)
                op.then_inc(sm.ml_sig, 1)
                act.wait_ge(sm.ml_out, 4)

            def hgrn():
                act.wait_ge(sm.hg_lb, 1)
                fn(lb_w[:, 0:32], lb_w[:, 0:32], ACT.Exp).then_inc(sm.hg_lbe, 1)
                for t in range(16, 24):
                    op = fn(proj[:, t, :], proj[:, t, :], ACT.Silu)
                op.then_inc(sm.hg_gate, 1)
                for hd in range(8):
                    wait(act, sm.hg_put, 10 * hd)
                    fn(hg_s[:, :], proj[:, 8 + hd, :], ACT.Sigmoid)
                    fn(hg_k[:, :], proj[:, 8 + hd, :], ACT.Sigmoid, scale=-1.0).then_inc(sm.hg_sig, 1)
                    act.wait_ge(sm.hg_dec, hd + 1)
                    fn(hg_s[:, :], hg_s[:, :], ACT.Ln).then_inc(sm.hg_log, 1)
                    for at in range(9):
                        e = hd * 9 + at
                        act.wait_ge(sm.hg_diff, e + 1)
                        fn(hg_d[e % 2][:, :], hg_d[e % 2][:, :], ACT.Exp).then_inc(sm.hg_e, 1)
                act.wait_ge(sm.hg_out, 8)

            def ffn():
                k, mt, m0, p0 = n["slot"], n["mt"], n["m"], n["part"]

                def up(q, i):
                    split(k + 2 * q + LEAD, i, 8)
                    wait(act, sm.part_lo, p0 + q - 1 + 4 * i)
                    act.wait_ge(sm.slot_used, k + 2 * q + 1 + 8 * i)
                    fn(sil[q % 2], bank[(mt + 2 * q) % 4][:, :], ACT.Silu).then_inc(sm.sil_done, 1)
                    split(k + 2 * q + 1 + LEAD, i, 8)
                    act.wait_ge(sm.lin_free, mt + 2 * q + 2 + 8 * i)
                    act.wait_ge(sm.const_loaded, 64)
                    fn(hid_hi[:, q + 4 * i, :], sil[q % 2], ACT.Copy).then_inc(sm.part_hi, 1)

                with act.Fori(0, 5) as i:
                    for q in range(4):
                        up(q, i)
                for q in range(20, 22):
                    up(q, 0)
                n.add(slot=2 * FT, mt=2 * FT, part=FT)
                split_ahead(3 * DT)
                n.add(mt=DT)

            sil = [lc[:, r * S:(r + 1) * S] for r in range(2)]
            act.wait_ge(sm.const_loaded, 64)
            fn(cond[:, :], col("c", 0, 8), ACT.Silu).then_inc(sm.cond_done, 1)
            for t in range(LEAD):
                split(t)
            for at, part in enumerate(parts):
                tiles, values = IN_PROJ[part]
                n.add(lc=1)
                if part == "first":
                    mean_squares(eps6, lambda c: None)
                split_input(part != "first")
                if part == "first":
                    act.wait_ge(sm.gate_pre, 1)
                    fn(gates, gates, ACT.Sigmoid).then_inc(sm.gate_out, 1)
                split_ahead(len(tiles) + len(values))
                n.add(mt=len(tiles) + len(values))
                act.wait_ge(sm.lin_free, n["mt"])
                act.wait_ge(sm.layer_const_loaded, 16 * n["lc"])
                if part == "first":
                    first_mixer()
                    n.add(mt=4)
                    act.wait_ge(sm.att_out, n_groups("first"))
                    act.wait_ge(sm.mix_ready, 2)
                    n.add(mix=2)
                elif part == 0:
                    mlstm()
                elif part == 1:
                    rope_tables()
                    attention(swa_jobs(), AT["late"])
                    n.add(att_g=64)
                elif part == 2:
                    hgrn()
                else:
                    act.wait_ge(sm.lam_in, 1)
                    fn(lam_w[:, 2:4], lam_w[:, 0:2], ACT.Exp).then_inc(sm.lam_exp, 1)
                    rope_tables()
                    attention(diff_jobs(), AT["late"])
                n.add(out=n_groups(part))
                wait(act, sm.att_out, n["out"])
                group_norms(out_norms(part))
                act.wait_ge(sm.g_out, n["gn"])
                high_parts([proj[:, c, :] for c in range(DT)], lambda c: None)
                split_ahead(DT)
                n.add(mt=DT)
                if part == "first":
                    act.wait_ge(sm.lin_free, n["mt"])
                    mean_squares(eps6, lambda c: None)
                else:
                    n["ln_at"] = 2 * part
                    layer_norm()
                split_input(part != "first")
                ffn()
                if part != "first":
                    n["ln_at"] = 2 * part + 1
                    layer_norm()

        @block.vector
        def _(dve):
            n = Counts()
            v = nc.vector

            def link(ins):
                n.add(dve_chain=1)
                ins.then_inc(sm.dve_chain, 1)
                dve.wait_ge(sm.dve_chain, n["dve_chain"])

            def low_parts(sources):
                for c, src in enumerate(sources):
                    dve.wait_ge(sm.part_hi, n["part"] + c + 1)
                    v.tensor_tensor(h_lo[:, c, :], src, h_hi[:, c, :].bitcast(F32), ALU.subtract).then_inc(sm.part_lo, 1)
                n.add(part=len(sources))

            def root():
                n.add(root=1)
                dve.wait_ge(sm.n_root, n["root"])
                link(v.reciprocal(rt[0][:, :], rt[0][:, :]))

            def rms_input(gain):
                root()
                for c in range(DT):
                    v.scalar_tensor_tensor(h_tmp[:, c, :], x[:, c, :], col(gain, c), rt[0][:, :], ALU.mult,
                                           ALU.mult).then_inc(sm.h_ready, 1)
                low_parts([h_tmp[:, c, :] for c in range(DT)])

            def modulated_input(layer, sub, normed):
                for c in range(DT):
                    if normed:
                        dve.wait_ge(sm.ln_x, n["lx"] * DT + c + 1)
                    v.tensor_scalar(h_tmp[:, c, :], x[:, c, :], mod_col(layer, sub, ONE_SCALE, c),
                                    mod_col(layer, sub, SHIFT, c), ALU.mult, ALU.add).then_inc(sm.h_ready, 1)
                n.add(lx=1 if normed else 0)
                low_parts([h_tmp[:, c, :] for c in range(DT)])

            def layer_norm(gain_at):
                n.add(ln=1)
                dve.wait_ge(sm.ln_mean, n["ln"])
                for c in range(DT):
                    v.scalar_tensor_tensor(x[:, c, :], bank[5][:, :], -1.0 / D, x[:, c, :], ALU.mult,
                                           ALU.add).then_inc(sm.ln_centred, 1)
                root()
                for c in range(DT):
                    v.scalar_tensor_tensor(x[:, c, :], x[:, c, :], col("ln_g", gain_at * 8 + c), rt[0][:, :], ALU.mult,
                                           ALU.mult).then_inc(sm.ln_y, 1)

            def tile_done(slots):
                n.add(slot=slots)
                dve.wait_ge(sm.slot_used, n["slot"])
                n.add(mt=1)
                return bank[(n["mt"] - 1) % 4]

            def keep(tiles, values):
                for t in range(tiles):
                    v.tensor_copy(proj[:, t, :], tile_done(1)[:, :]).then_inc(sm.lin_free, 1)
                for out in values:
                    v.tensor_copy(out, tile_done(1)[:, :].rearrange("p (t d) -> p t d", t=TT)).then_inc(sm.lin_free, 1)
                dve.wait_ge(sm.lin_free, n["mt"])

            def add_residual(slots, layer=None, sub=None):
                if layer is not None:
                    n.add(xs=DT)
                    dve.wait_ge(sm.x_scaled, n["xs"])
                for m in range(DT):
                    b = tile_done(slots)
                    if layer is None:
                        v.tensor_tensor(x[:, m, :], b[:, :], x[:, m, :], ALU.add).then_inc(sm.lin_free, 1)
                    else:
                        v.scalar_tensor_tensor(x[:, m, :], b[:, :], mod_col(layer, sub, ONE_GATE, m), x[:, m, :],
                                               ALU.mult, ALU.add).then_inc(sm.lin_free, 1)
                dve.wait_ge(sm.lin_free, n["mt"])

            def group_norms(items):
                for t, it in enumerate(items):
                    rows = it["src"][0].shape[0]
                    r = rt[t % 2][0:rows, :]
                    dve.wait_ge(sm.g_root, n["gn"] + t + 1)
                    link(v.reciprocal(r, r))
                    for u, src in enumerate(it["src"]):
                        for out in it["out"][u]:
                            op = v.scalar_tensor_tensor(out, src, it["gain"][u], r, ALU.mult, ALU.mult)
                        if it["mul"]:
                            link(op)
                            op = v.tensor_tensor(out, out, it["mul"][u], ALU.mult)
                    op.then_inc(sm.g_out, 1)
                n.add(gn=len(items))

            def attention(jobs, bufs):
                a, g = n["att"], n["att_g"]
                for step in range(len(jobs) + 2):
                    if step < len(jobs):
                        j, it = step, jobs[step]
                        s, w = bufs["s"][j % 2], it["w"]
                        dve.wait_ge(sm.att_scores, a + j + 1)
                        wait(dve, sm.att_exp, a + j - 1)
                        op = v.scalar_tensor_tensor(s[:, 0:w], bank[j % 2][:, 0:w], SCALE, it["bias"], ALU.mult, ALU.add)
                        if it["sink"] is not None:
                            op = v.tensor_copy(s[:, w:w + 1], it["sink"])
                            w += 1
                        link(op)
                        v.tensor_reduce(att_max[j % 2], s[:, 0:w], AX_X, ALU.max, negate=True).then_inc(sm.att_ready, 1)
                    if 1 <= step <= len(jobs):
                        j, it = step - 1, jobs[step - 1]
                        p, w, inv = bufs["p"][j % 2], it["w"], att_inv[j % 2]
                        dve.wait_ge(sm.att_exp, a + j + 1)
                        link(v.reciprocal(inv, att_sum[j % 2]))
                        if it["gate"] is not None:
                            link(v.tensor_tensor(inv, inv, it["gate"], ALU.mult))
                        if it["vis"] is not None:
                            op = v.scalar_tensor_tensor(p[:, 0:w], p[:, 0:w], inv, it["vis"], ALU.mult, ALU.mult)
                        else:
                            op = v.tensor_scalar(p[:, 0:w], p[:, 0:w], inv, None, ALU.mult)
                        op.then_inc(sm.att_normed, 1)
                    if step >= 2 and jobs[step - 2]["last"]:
                        j, it = step - 2, jobs[step - 2]
                        g += 1
                        dve.wait_ge(sm.att_pv, a + j + 1)
                        rows = slice(it["row"], it["row"] + it["dv"])
                        v.tensor_copy(it["dest"], bank[4 + g % 2][rows, 0:P]).then_inc(sm.att_out, 1)
                n.add(att=len(jobs), att_g=sum(it["last"] for it in jobs))

            def first_mixer():
                link(v.memset(blk[:, :, :, :], 0.0))
                pe_cols = col("pe", 0, 32).rearrange("p (a c) -> p a c", a=2)
                for kv in range(2):
                    rows = slice(HD * kv, HD * kv + HD)
                    tok = proj[rows, 8, :].rearrange("p (n r) -> p r n", r=CMP_STRIDE)
                    for par in range(2):
                        for c1 in range(2):
                            op = v.tensor_tensor(blk[HD * par:HD * par + HD, kv, 8 * c1:8 * c1 + 8, 0:NCMP],
                                                 tok[:, par::2, c1:c1 + NCMP],
                                                 pe_cols[rows, par, 8 * c1:8 * c1 + 8].unsqueeze(2).to_broadcast([HD, 8, NCMP]),
                                                 ALU.add)
                            if (kv, par, c1) != (1, 1, 1):
                                link(op)
                op.then_inc(sm.blk_ready, 2)
                for kv in range(2):
                    dve.wait_ge(sm.blk_hi_done, kv + 1)
                    v.tensor_tensor(blk_lo[:, kv, :, :], blk[:, kv, :, :], blk_hi[:, kv, :, :].bitcast(F32),
                                    ALU.subtract).then_inc(sm.blk_lo_done, 1)
                for kv in range(2):
                    for m in range(2):
                        v.tensor_copy(hid_pre[:, 2 * kv + m, :], tile_done(2)[:, 0:32]).then_inc(sm.lin_free, 1)
                dve.wait_ge(sm.cmp_mm, 1)
                v.tensor_copy(vcmp[0:NCMP, :], bank[5][0:NCMP, 0:HD])
                dve.wait_ge(sm.cmp_root, 1)
                link(v.reciprocal(hid_pre[0:HD, 1, :], hid_pre[0:HD, 1, :]))
                for b in (HD, 0):
                    v.scalar_tensor_tensor(kcmp[b:b + HD, :], bank[4][0:HD, 0:32], col("g_k_cmp")[0:HD, :],
                                           hid_pre[0:HD, 1, :], ALU.mult, ALU.mult)
                dve.wait_ge(sm.v_turned, 1)
                v.tensor_copy(v_slc[:, :, :], bank[7][:, 0:256].rearrange("p (t d) -> p t d", t=TT))
                v.tensor_copy(v_win[:, :, :], bank[7][:, 256:512].rearrange("p (t d) -> p t d", t=TT)).then_inc(sm.v_out, 1)
                group_norms(first_norms())
                for hd in range(NSA_HEADS):
                    v.scalar_tensor_tensor(bias[:, hd, :], dist, -SLOPES_A[hd], causal, ALU.mult, ALU.add)
                    op = v.scalar_tensor_tensor(cmp_bias[:, hd, :], lc[:, 0:124], -SLOPES_A[hd], lc[:, 248:372],
                                                ALU.mult, ALU.add)
                dve.wait_ge(sm.gate_out, 1)
                link(op)
                for t in range(2):
                    u, y, w = proj[:, 13 + t, :], proj[:, 11 + t, :], [col("conv_w", 3 * t + i) for i in range(3)]
                    link(v.tensor_tensor(u, u, y, ALU.mult))
                    link(v.tensor_scalar(y, u, w[2], None, ALU.mult))
                    link(v.scalar_tensor_tensor(y[:, 1:S], u[:, 0:S - 1], w[1], y[:, 1:S], ALU.mult, ALU.add))
                    link(v.scalar_tensor_tensor(y[:, 2:S], u[:, 0:S - 2], w[0], y[:, 2:S], ALU.mult, ALU.add))
                    op = v.tensor_tensor(proj[:, 2 + t, :], y, proj[:, 2 + t, :], ALU.mult)
                op.then_inc(sm.mix_ready, 1)
                attention(nsa_jobs(), AT["first"])
                stick_breaking()
                for hd in range(4):
                    op = v.scalar_tensor_tensor(bias[:, hd, :], dist, -SLOPES_D[hd], logmult, ALU.mult, ALU.add)
                op.then_inc(sm.mix_ready, 1)
                dve.wait_ge(sm.mix_ready, 2)
                attention(dil_jobs(), AT["first"])

            def stick_breaking():
                strict, shut = lc[:, 512:640], lc[:, 640:768]
                for hd in range(4):
                    dve.wait_ge(sm.st_log, hd + 1)
                    link(v.scalar_tensor_tensor(st_l[:, :], st_z[:, :], 0.0, st_e[:, :], ALU.max, ALU.add))
                    for j in range(TT):
                        d = st_l[:, CO[j]:CO[j] + P]
                        op = v.tensor_tensor(d, d, strict, ALU.mult)
                    op.then_inc(sm.st_keep, 1)
                    dve.wait_ge(sm.st_suffix, hd + 1)
                    for j in range(TT):
                        d = slice(CO[j], CO[j] + CW[j])
                        op = v.tensor_tensor(st_e[:, d], st_z[:, d], bank[j][:, 0:CW[j]], ALU.subtract)
                    link(op)
                    for j in range(TT):
                        d = st_e[:, CO[j]:CO[j] + P]
                        op = v.tensor_tensor(d, d, shut, ALU.add)
                    op.then_inc(sm.st_arg, 1)
                    dve.wait_ge(sm.st_pv, hd + 1)
                    b = HD * (hd % 2)
                    v.tensor_copy(half(4 + hd // 2, hd), bank[4 + hd % 2][b:b + HD, :]).then_inc(sm.st_out, 1)
                dve.wait_ge(sm.st_out, 4)

            def rope_tables():
                n.add(rt=1, lcw=0)
                ang, y = rope_t[2], rope_t[3]
                dve.wait_ge(sm.pos_loaded, 16 * n["rt"])
                link(v.tensor_copy(y[:, :], rope_i[:, :]))
                link(v.tensor_scalar(ang[:, :], y[:, :], lc[:, 128:129], None, ALU.mult))
                turns = [6.28125, 0.0019350051879882812, 3.0200114160515973e-07]
                for f, shift in enumerate((0.0, 0.25)):
                    r = rope_t[f]
                    link(v.tensor_scalar(y[:, :], ang[:, :], 1 / (2 * np.pi), shift, ALU.mult, ALU.add))
                    link(v.tensor_scalar(y[:, :], y[:, :], 12582912.0, None, ALU.add))
                    link(v.tensor_scalar(y[:, :], y[:, :], 12582912.0, None, ALU.subtract))
                    link(v.scalar_tensor_tensor(r[:, :], y[:, :], -turns[0], ang[:, :], ALU.mult, ALU.add))
                    link(v.scalar_tensor_tensor(r[:, :], y[:, :], -turns[1], r[:, :], ALU.mult, ALU.add))
                    link(v.scalar_tensor_tensor(r[:, :], y[:, :], -turns[2], r[:, :], ALU.mult, ALU.add))
                    if f:
                        link(v.tensor_scalar(r[:, :], r[:, :], float(np.pi / 2), None, ALU.add))
                    v.tensor_scalar(r[:, :], r[:, :], 3.1415925, -3.1415925, ALU.min, ALU.max).then_inc(sm.rope_ang, 1)

            def rope(tiles):
                dve.wait_ge(sm.rope_ready, 2 * n["rt"])
                for t in tiles:
                    n.add(rope=1)
                    a = rope_t[n["rope"] % 2]
                    dve.wait_ge(sm.rope_mm, n["rope"])
                    v.tensor_tensor(a[:, :], bank[4 + (n["rope"] - 1) % 2][:, :], rope_cs[:, 1, :], ALU.mult)
                    link(v.tensor_tensor(proj[:, t, :], proj[:, t, :], rope_cs[:, 0, :], ALU.mult))
                    v.tensor_tensor(proj[:, t, :], proj[:, t, :], a[:, :], ALU.add).then_inc(sm.rope_out, 1)
                dve.wait_ge(sm.rope_out, n["rope"])

            def mlstm():
                b = col("mlstm_b", 0, 2)
                dve.wait_ge(sm.ml_gate, 1)
                v.tensor_scalar(ml_r[0:4, 0, :], bank[6][0:4, :], b[0:4, 0:1], None, ALU.add)
                v.tensor_scalar(ml_r[0:4, 1, :], bank[7][0:4, :], b[0:4, 1:2], None, ALU.add).then_inc(sm.ml_pre, 1)
                link(v.memset(ml_r[0:4, 7, :], 1.0))
                dve.wait_ge(sm.ml_log, 1)
                link(v.scalar_tensor_tensor(ml_r[0:4, 3, :], ml_r[0:4, 1, :], 0.0, ml_r[0:4, 2, :], ALU.min, ALU.subtract))
                link(v.tensor_tensor_scan(ml_r[0:4, 1, :], ml_r[0:4, 7, :], ml_r[0:4, 3, :], 0.0, ALU.mult, ALU.add))
                link(v.tensor_tensor(ml_r[0:4, 4, :], ml_r[0:4, 0, :], ml_r[0:4, 1, :], ALU.subtract))
                link(v.tensor_tensor_scan(ml_r[0:4, 5, :], ml_r[0:4, 4, :], ml_r[0:4, 4, :], 0.0, ALU.max, ALU.max))
                v.tensor_tensor(ml_r[0:4, 2, :], ml_r[0:4, 1, :], ml_r[0:4, 5, :], ALU.add).then_inc(sm.ml_pre, 1)
                dve.wait_ge(sm.ml_turn, 1)
                v.tensor_copy(ml_w, bank[0][:, 0:16]).then_inc(sm.ml_w, 1)
                for hd in range(4):
                    dve.wait_ge(sm.ml_spread, hd + 1)
                    v.tensor_tensor(ml_d[:, :].rearrange("p (t q) -> p t q", t=TT),
                                    bank[0][:, :].rearrange("p (t q) -> p t q", t=TT),
                                    lc[:, 512:640].unsqueeze(1).to_broadcast([P, TT, P]), ALU.add).then_inc(sm.ml_diag, 1)
                    dve.wait_ge(sm.ml_exp, hd + 1)
                    for j in range(TT):
                        d = slice(CO[j], CO[j] + CW[j])
                        op = v.scalar_tensor_tensor(ml_a[:, d], bank[2 + j][:, 0:CW[j]], P ** -0.5, ml_e[:, d], ALU.mult,
                                                    ALU.mult)
                    op.then_inc(sm.ml_a, 1)
                    dve.wait_ge(sm.ml_den, hd + 1)
                    link(v.scalar_tensor_tensor(ml_x[:, :], bank[6][:, :], -1.0, ml_x[:, :], ALU.mult, ALU.max))
                    link(v.scalar_tensor_tensor(ml_d[:, :], bank[6][:, :], 1.0, ml_x[:, :], ALU.mult, ALU.max))
                    link(v.reciprocal(ml_d[:, :], ml_d[:, :]))
                    dve.wait_ge(sm.ml_num, hd + 1)
                    for e in range(2):
                        op = v.tensor_tensor(proj[:, 2 * hd + e, :], bank[7 if e else 0][:, :], ml_d[:, :], ALU.mult)
                    op.then_inc(sm.ml_out, 1)
                dve.wait_ge(sm.ml_out, 4)
                dve.wait_ge(sm.ml_sig, 1)

            def hgrn():
                low = col("lower", 0, 32).rearrange("p (l c) -> p c l", l=4)
                top, e = lb_w[:, 32:40], lb_w[:, 0:32]
                link(v.tensor_reduce(top, low, AX_X, ALU.max))
                v.tensor_tensor(e.rearrange("p (l c) -> p l c", l=4), col("lower", 0, 32).rearrange("p (l c) -> p l c", l=4),
                                top.unsqueeze(1).to_broadcast([P, 4, 8]), ALU.subtract).then_inc(sm.hg_lb, 1)
                v.memset(hg_one[:, :], 1.0)
                v.memset(hg_p[:, :, :], 0.0)
                for r in range(2):
                    v.memset(hg_q[r][:, :], 0.0)
                    op = v.memset(hg_t[r][:, :], 0.0)
                link(op)
                dve.wait_ge(sm.hg_lbe, 1)
                link(v.tensor_reduce(top, e.rearrange("p (l c) -> p c l", l=4), AX_X, ALU.add))
                v.tensor_tensor(lb, e[:, 8:16], e[:, 16:24], ALU.add)
                v.tensor_tensor(one_lb, e[:, 0:8], e[:, 24:32], ALU.add)
                link(v.reciprocal(top, top))
                v.tensor_tensor(lb, lb, top, ALU.mult)
                link(v.tensor_tensor(one_lb, one_lb, top, ALU.mult))
                dve.wait_ge(sm.hg_gate, 1)

                def halves(ap, b):
                    q = ap.rearrange("p (n h b) -> p n h b", h=2, b=b)
                    return q[:, :, 0, :], q[:, :, 1, :]

                def decays(hd, at):
                    b, i = LV[at], hd * 9 + at
                    early, late = halves(hg_c[:, :], b)
                    mid = early[:, :, b - 1:b].to_broadcast([P, S // (2 * b), b])
                    d = halves(hg_d[i % 2][:, :], b)
                    wait(dve, sm.hg_qk, hd * 10 + at - 1)
                    v.tensor_tensor(d[0], mid, early, ALU.subtract)
                    v.tensor_tensor(d[1], late, mid, ALU.subtract).then_inc(sm.hg_diff, 1)

                def put(hd, at):
                    m, b = hd * 10 + at, (LV + [0])[at]
                    dve.wait_ge(sm.hg_mm, m + 1)
                    wait(dve, sm.hg_put, m)
                    if b == 256:
                        wait(dve, sm.hg_pv, hd)
                        v.tensor_copy(hg_p[:, 0, 256:512], bank[0][:, 0:256])
                        op = v.tensor_copy(hg_p[:, 1, 128:384], bank[1][:, 0:256])
                    elif b == 128:
                        v.tensor_copy(hg_p[:, 0, 128:256], bank[2][:, 0:128])
                        op = v.tensor_copy(hg_p[:, 2, 128:256], bank[2][:, 128:256])
                    else:
                        mask = lc[:, (at - 2) * P:(at - 1) * P] if b else ident
                        op = v.copy_predicated(hg_p[:, :, 0:P],
                                               mask.bitcast(I32).unsqueeze(1).to_broadcast([P, TT, P]),
                                               bank[4 + m % 2][:, :].rearrange("p (t q) -> p t q", t=TT))
                    op.then_inc(sm.hg_put, 1)

                for hd in range(8):
                    dve.wait_ge(sm.hg_sig, hd + 1)
                    link(v.tensor_scalar(hg_s[:, :], hg_s[:, :], one_lb[:, hd:hd + 1], lb[:, hd:hd + 1], ALU.mult, ALU.add))
                    v.tensor_scalar(hg_s[:, :], hg_s[:, :], tiny, None, ALU.max)
                    v.tensor_scalar(hg_k[:, :], hg_k[:, :], one_lb[:, hd:hd + 1], None, ALU.mult).then_inc(sm.hg_dec, 1)
                    dve.wait_ge(sm.hg_log, hd + 1)
                    link(v.tensor_tensor_scan(hg_c[:, :], hg_one[:, :], hg_s[:, :], 0.0, ALU.mult, ALU.add))
                    decays(hd, 0)
                    for at in range(9):
                        m, i, b = hd * 10 + at, hd * 9 + at, LV[at]
                        if at < 8:
                            decays(hd, at + 1)
                        dve.wait_ge(sm.hg_e, i + 1)
                        wait(dve, sm.hg_mm, m - 1)
                        d, qq = halves(hg_d[i % 2][:, :], b), halves(proj[:, hd, :], b)[1]
                        v.tensor_tensor(halves(hg_q[m % 2][:, :], b)[1], qq, d[1], ALU.mult)
                        v.tensor_tensor(halves(hg_t[m % 2][:, :], b)[0], halves(hg_k[:, :], b)[0], d[0],
                                        ALU.mult).then_inc(sm.hg_qk, 2 if at == 8 else 1)
                        if at:
                            put(hd, at - 1)
                    put(hd, 8)
                    put(hd, 9)
                    dve.wait_ge(sm.hg_pv, hd + 1)
                    v.tensor_copy(proj[:, hd, :], bank[6 + hd % 2][:, :]).then_inc(sm.hg_out, 1)
                dve.wait_ge(sm.hg_out, 8)

            def lambdas():
                a = col("diff_lambda", 0, 256).rearrange("p (l d) -> p l d", l=4)
                prod = small[:, 0:128].rearrange("p (l d) -> p l d", l=2)
                link(v.tensor_tensor(prod, a[:, 0:4:2, :], a[:, 1:4:2, :], ALU.mult))
                v.tensor_reduce(lam_w[:, 0:2], prod, AX_X, ALU.add).then_inc(sm.lam_in, 1)
                v.tensor_scalar(lam_w[:, 5:6], col("diff_norm"), 1.0 - LAM_INIT[3], None, ALU.mult)
                dve.wait_ge(sm.lam_exp, 1)
                link(v.tensor_tensor(lam, lam_w[:, 3:4], lam_w[:, 2:3], ALU.subtract))
                link(v.tensor_scalar(lam, lam, -LAM_INIT[3], None, ALU.add))

            def ffn(ahead, layer, with_residual):
                k, mt, p0, s0, a0, cg = n["slot"], n["mt"], n["part"], n["sil"], n["ada"], n["cg"]

                def ada_slot(a, kc, i):
                    dve.wait_ge(ada_loaded[a % ADA_RING], 16 * (a // ADA_RING + 1) + 64 * i)
                    if kc == 0:
                        op = v.tensor_scalar(ada_acc[:, :], ada_raw[a % ADA_RING][:, :], cond[:, 0:1], None, ALU.mult)
                    else:
                        dve.wait_ge(sm.ada_used, a + 8 * i)
                        op = v.scalar_tensor_tensor(ada_acc[:, :], ada_raw[a % ADA_RING][:, :], cond[:, kc:kc + 1],
                                                    ada_acc[:, :], ALU.mult, ALU.add)
                    op.then_inc(sm.ada_used, 1)

                def ada_out(g, i):
                    dve.wait_ge(sm.ada_sum, cg + g + 1 + i)
                    v.tensor_tensor(mod[ahead % 2][:, bass.ds(8 * g + 8 * i, 8)], bank[7][:, 0:8],
                                    co[:, bass.ds(COLS["ada_b"][0] + 48 * ahead + 8 * g + 8 * i, 8)],
                                    ALU.add).then_inc(sm.ada_mod, 1)

                def up(q, i):
                    dve.wait_ge(sm.sil_done, s0 + q + 1 + 4 * i)
                    dve.wait_ge(sm.slot_used, k + 2 * q + 2 + 8 * i)
                    v.tensor_tensor(sil[q % 2], bank[(mt + 2 * q + 1) % 4][:, :], sil[q % 2],
                                    ALU.mult).then_inc(sm.lin_free, 2)
                    dve.wait_ge(sm.part_hi, p0 + q + 1 + 4 * i)
                    v.tensor_tensor(hid_lo[:, q + 4 * i, :], sil[q % 2], hid_hi[:, q + 4 * i, :].bitcast(F32),
                                    ALU.subtract).then_inc(sm.part_lo, 1)

                if ahead is not None and a0 == 0:
                    dve.wait_ge(sm.cond_done, 1)
                with dve.Fori(0, 5) as i:
                    for q in range(4):
                        if ahead is not None:
                            ada_slot(a0 + 2 * q, 2 * q, i)
                            ada_slot(a0 + 2 * q + 1, 2 * q + 1, i)
                        up(q, i)
                    if ahead is not None:
                        ada_out(0, i)
                for q in range(20, 22):
                    if ahead is not None:
                        for kc in range(4 * (q - 20), 4 * (q - 20) + 4):
                            ada_slot(a0 + 40 + kc, kc, 0)
                    up(q, 0)
                if ahead is not None:
                    ada_out(5, 0)
                    n.add(ada=48, cg=6)
                    dve.wait_ge(sm.ada_mod, n["cg"])
                    more = mod[ahead % 2][:, :].rearrange("p (s k) -> p s k", s=2)[:, :, 8:24]
                    link(v.tensor_scalar(more, more, 1.0, None, ALU.add))
                n.add(slot=2 * FT, mt=2 * FT, part=FT, sil=FT)
                add_residual(3, layer, 1)

            sil = [lc[:, r * S:(r + 1) * S] for r in range(2)]
            dve.wait_ge(sm.const_loaded, 64)
            for at, part in enumerate(parts):
                tiles, values = IN_PROJ[part]
                layer = None if part == "first" else part
                n.add(lc=1)
                if part == "first":
                    rms_input("g_mix")
                    dve.wait_ge(sm.gate_in, 1)
                    v.tensor_tensor(gates.rearrange("p (t g) -> p t g", t=TT),
                                    bank[6][:, 0:48].rearrange("p (t g) -> p t g", t=TT),
                                    col("b_gate", 0, 12).unsqueeze(1).to_broadcast([P, TT, 12]),
                                    ALU.add).then_inc(sm.gate_pre, 1)
                    keep(len(tiles), [t[:, :, e * P:(e + 1) * P] for t in (first_vc, first_vd) for e in range(2)])
                else:
                    modulated_input(layer, 0, parts[at - 1] != "first")
                    vals = {0: ml_v, 1: swa_v, 2: hg_v, 3: df_v}[part]
                    keep(len(tiles), [vals[:, :, e * P:(e + 1) * P] for e in range(len(values))])
                dve.wait_ge(sm.layer_const_loaded, 16 * n["lc"])
                if part == "first":
                    first_mixer()
                elif part == 0:
                    mlstm()
                elif part == 1:
                    rope_tables()
                    rope(range(9))
                    for g in range(2):
                        for b in (0, HD):
                            op = v.tensor_copy(swa_k[b:b + HD, g, :], proj[HD * g:HD * g + HD, 8, :])
                    op.then_inc(sm.mix_ready, 1)
                    attention(swa_jobs(), AT["late"])
                elif part == 2:
                    hgrn()
                else:
                    lambdas()
                    rope_tables()
                    rope(range(16))
                    v.tensor_copy(lam_w[:, 4:5], eps6).then_inc(sm.mix_ready, 1)
                    attention(diff_jobs(), AT["late"])
                wait(dve, sm.att_out, n["att_g"])
                group_norms(out_norms(part))
                low_parts([proj[:, c, :] for c in range(DT)])
                add_residual(1, layer, 0)
                if part == "first":
                    rms_input("g_ffn")
                else:
                    layer_norm(2 * part)
                    modulated_input(layer, 1, True)
                ffn(parts[at + 1] if at + 1 < len(parts) else None, layer, True)
                if part != "first":
                    layer_norm(2 * part + 1)


def slot_rows(w, columns):
    rows = w.shape[0] // P
    slots = []
    for c in columns:
        t = w[:, c:c + P].reshape(rows, P, P).transpose(1, 0, 2)
        for r in range(0, rows, 8):
            s = np.zeros((P, 8, P), w.dtype)
            s[:, 0:min(8, rows - r), :] = t[:, r:r + 8, :]
            slots.append(s.reshape(P, SLOT))
    return slots


def weight_stream(a, parts):
    out = []
    every = [j * P for j in range(DT)]
    for part in parts:
        if part == "first":
            w_in, w_out, gate, up, down = (a[k][0] for k in ("w_in", "w_out", "w_gate", "w_up", "w_down"))
        else:
            name = ("mlstm", "swa", "hgrn", "diff")[part]
            w_in, w_out = a[f"{name}_w_in_2"][0], a[f"{name}_w_out_2"][0]
            both, down = a["ffn_w_in_2"][part], a["ffn_w_out_2"][part]
            gate, up = both[:, :FF], both[:, FF:]
        tiles, values = IN_PROJ[part]
        out += slot_rows(w_in, tiles + values)
        if part == "first":
            for w in ("w1_k_cmp", "w1_v_cmp"):
                out += slot_rows(a[w][0], [0, P])
        out += slot_rows(w_out, every)
        hidden = [j * P for j in range(FT)]
        for g, u in zip(slot_rows(gate, hidden), slot_rows(up, hidden)):
            out += [g, u]
        out += slot_rows(down, every)
    return np.stack(out)


def ada_stream(w, parts):
    layers = [p for p in parts[1:]]
    if not layers:
        return np.zeros((1, P, SLOT), np.float32)
    return np.stack([w[p, s, c * P:(c + 1) * P, g * SLOT:(g + 1) * SLOT]
                     for p in layers for s in range(2) for g in range(3) for c in range(DT)])


def column_pack(a):
    def tiles(v):
        return v.reshape(-1, P).T

    def twice(v):
        return np.concatenate([v, v])[:, None]

    def spread(v):
        return np.broadcast_to(v.reshape(1, -1), (P, v.size))

    def by_tile(w):
        return w.reshape(-1, P, w.shape[1]).transpose(1, 0, 2).reshape(P, -1)

    pe = np.concatenate([a[k][0].reshape(16, 2, HD).transpose(2, 1, 0).reshape(HD, 32) for k in ("pe_k_cmp", "pe_v_cmp")])
    mb = np.zeros((P, 2), np.float32)
    mb[0:4, :] = a["mlstm_b_gate_2"][0].reshape(2, 4).T
    pack = {
        "g_mix": tiles(a["g_mix"][0]), "g_ffn": tiles(a["g_ffn"][0]), "g_out": tiles(a["g_out"][0]),
        "g_q_nsa": twice(a["g_q_nsa"][0]), "g_k_slc": twice(a["g_k_slc"][0]), "g_k_win": twice(a["g_k_win"][0]),
        "g_k_cmp": twice(a["g_k_cmp"][0]), "g_q_dil": twice(a["g_q_dil"][0]), "g_k_dil": twice(a["g_k_dil"][0]),
        "conv_w": a["conv_w"][0].T.reshape(2, P, 3).transpose(1, 0, 2).reshape(P, 6), "pe": pe,
        "gate_w": by_tile(a["w_in"][0][:, C_GT:C_GT + 12]), "b_gate": spread(a["b_gate"][0]),
        "w2": np.concatenate([by_tile(a["w2_k_cmp"][0]), by_tile(a["w2_v_cmp"][0])], 1),
        "c": tiles(a["c_2"]), "ada_b": tiles(a["ada_b_2"]), "ln_g": tiles(a["ln_g_2"]), "ln_b": tiles(a["ln_b_2"]),
        "mlstm_gw": by_tile(a["mlstm_w_in_2"][0][:, 3072:3080]), "mlstm_b": mb,
        "mlstm_norm": tiles(a["mlstm_norm_2"][0]), "sinks": spread(a["swa_sinks_2"][0]),
        "lower": tiles(a["hgrn_lower_bounds_2"]), "hgrn_norm": tiles(a["hgrn_norm_2"][0]),
        "diff_norm": a["diff_norm_2"][0][:, None], "diff_lambda": spread(a["diff_lambda_2"][0]),
    }
    return np.ascontiguousarray(np.concatenate([pack[name] for name in COLS], 1))


def kernel(**inputs):
    import concourse.bacc as bacc
    from concourse.bass_utils import run_bass_kernel_spmd

    a = {k: np.asarray(v) for k, v in inputs.items()}
    kept, big, layer = constants()
    arrays = {
        "x_t": np.ascontiguousarray(a["x"][0].T.reshape(DT, P, S).transpose(1, 0, 2)),
        "weights": weight_stream(a, PARTS), "ada": ada_stream(a["ada_w_2"], PARTS), "columns": column_pack(a),
        "kept_const": kept, "big_const": big, "layer_const": layer,
        "positions": np.ascontiguousarray(np.broadcast_to(a["positions_2"], (P, S))),
    }
    nc = bacc.Bacc("TRN2", target_bir_lowering=False, num_devices=1)
    args = [nc.dram_tensor(name, v.shape, mybir.dt.from_np(v.dtype), kind="ExternalInput").ap()
            for name, v in arrays.items()]
    out = nc.dram_tensor("y_t", (P, DT, S), F32, kind="ExternalOutput").ap()
    program(nc, *args, out, PARTS)
    r = run_bass_kernel_spmd(nc, [arrays], core_ids=[0])
    y = r.results[0]["y_t"]
    return np.ascontiguousarray(y.transpose(1, 0, 2).reshape(D, S).T)[None]
```

```python
from collections import namedtuple
from contextlib import ExitStack, contextmanager

import numpy as np

import concourse.bass as bass
import concourse.mybir as mybir

F32 = mybir.dt.float32
F32R = mybir.dt.float32r
I32 = mybir.dt.int32
ACT = mybir.ActivationFunctionType
ALU = mybir.AluOpType
AX_X = mybir.AxisListType.X

P = 128
S = 512
D = 1024
DT = D // P
HD = 64
FF = 2816
FT = FF // P
TT = S // P
SLOT = 8 * P
RING = 4
LEAD = 4
EARLY = 3
ADA_RING = 2
CMP_LEN, CMP_STRIDE = 32, 16
NCMP = (S - CMP_LEN) // CMP_STRIDE + 1
NSA_HEADS = 4
NEG = -1e30
ALPHA = 8 ** 0.25
LAYERS = 4
PARTS = ["first", 0, 1, 2, 3]
LAM_INIT = [0.8 - 0.6 * float(np.exp(-0.3 * i)) for i in range(LAYERS)]
ROPE_THETA = 500000.0
SCALE = HD ** -0.5
SLOPES = [2.0 ** -(i + 1) for i in range(8)]
SLOPES_A, SLOPES_D = SLOPES[0::2], SLOPES[1::2]

W_IN_COLS = np.cumsum([0, 256, 64, 64, 64, 64, 64, 64, 12, 256, 256, 256, 256, 256, 256, 256, 256, 256])
(C_QA, C_KC, C_VC, C_KS, C_VS, C_KW, C_VW, C_GT, C_CB, C_CC, C_CU,
 C_QC, C_KCC, C_VCC, C_QD, C_KD, C_VD) = (int(v) for v in W_IN_COLS[:-1])
FIRST_TILES = ([C_QA, C_QA + P, C_CB, C_CB + P, C_QC, C_QC + P, C_QD, C_QD + P, C_KC, C_KS, C_KW,
                C_CC, C_CC + P, C_CU, C_CU + P, C_KCC, C_KCC + P, C_KD, C_KD + P])
FIRST_VALUES = [C_VCC, C_VCC + P, C_VD, C_VD + P]
MLSTM_TILES = [c for h in range(4) for c in (h * P, 512 + h * P)] + [2048 + j * P for j in range(8)]
MLSTM_VALUES = [1024 + j * P for j in range(8)]
SWA_TILES = [j * P for j in range(9)]
SWA_VALUES = [9 * P]
HGRN_TILES = [j * P for j in range(16)] + [3072 + j * P for j in range(8)]
HGRN_VALUES = [2048 + j * P for j in range(8)]
DIFF_TILES = [j * P for j in range(16)]
DIFF_VALUES = [2048 + j * P for j in range(8)]
IN_PROJ = {"first": (FIRST_TILES, FIRST_VALUES), 0: (MLSTM_TILES, MLSTM_VALUES), 1: (SWA_TILES, SWA_VALUES),
           2: (HGRN_TILES, HGRN_VALUES), 3: (DIFF_TILES, DIFF_VALUES)}

COLS = {}


def _columns():
    at = 0
    for name, width in [("g_mix", 8), ("g_ffn", 8), ("g_out", 8), ("g_q_nsa", 1), ("g_k_slc", 1), ("g_k_win", 1),
                        ("g_k_cmp", 1), ("g_q_dil", 1), ("g_k_dil", 1), ("conv_w", 6), ("pe", 32), ("gate_w", 96),
                        ("b_gate", 12), ("w2", 256), ("c", 8), ("ada_b", 192), ("ln_g", 64), ("ln_b", 64),
                        ("mlstm_gw", 64), ("mlstm_b", 2), ("mlstm_norm", 8), ("sinks", 16), ("lower", 32),
                        ("hgrn_norm", 8), ("diff_norm", 1), ("diff_lambda", 256)]:
        COLS[name] = (at, width)
        at += width
    return at


NCOLS = _columns()

KEPT = {"ident": 128, "ones": 128, "block64": 128, "eps6": 1, "eps5": 1, "tiny": 1}
LAYER_CONST = 1024
BIG_CONST = 3 * S


def constants():
    p, f = np.arange(P)[:, None], np.arange(P)[None, :]
    u = np.arange(S)[None, :]
    ident = (p == f).astype(np.float32)
    kept = np.concatenate([ident, np.ones((P, P)), (p // HD == f // HD) / HD, np.full((P, 1), 1e-6),
                           np.full((P, 1), 1e-5), np.full((P, 1), 1e-19)], 1).astype(np.float32)
    dist = p + (S - P) - u
    causal = np.where(dist >= 0, 0.0, NEG)
    mult = (dist <= 128).astype(int) + (dist % 4 == 0) + (dist % 16 == 0)
    logmult = np.where((dist >= 0) & (mult > 0), np.log(np.maximum(mult, 1)), NEG)
    big = np.concatenate([dist, causal, logmult], 1).astype(np.float32)
    layer = np.zeros((5, P, LAYER_CONST), np.float32)
    t = np.arange(TT)[:, None] * P
    dc = (p[:, :, None] + t[None]) - (np.arange(NCMP) * CMP_STRIDE + CMP_LEN - 1)[None, None, :]
    dc = dc.reshape(P, TT * NCMP)
    layer[0, :, 0:124] = dc
    layer[0, :, 124:248] = dc >= 0
    layer[0, :, 248:372] = np.where(dc >= 0, 0.0, NEG)
    layer[0, :, 384:512] = p >= f
    layer[0, :, 512:640] = p < f
    layer[0, :, 640:768] = np.where(p < f, 0.0, NEG)
    for h in range(4):
        layer[1, h, h * P:(h + 1) * P] = 1.0
    layer[1, :, 512:640] = np.where(p <= f, 0.0, -NEG)
    rope = np.zeros((P, P), np.float32)
    for b in (0, HD):
        for j in range(8):
            rope[b + 8 + j, b + j] = -1.0
            rope[b + j, b + 8 + j] = 1.0
    inv = np.zeros((P, 1), np.float32)
    for b in (0, HD):
        for j in range(16):
            inv[b + j, 0] = np.float32(ROPE_THETA) ** np.float32(-(j % 8) * 2.0 / 16)
    band = (P + p) - np.arange(2 * P)[None, :]
    for at in (2, 4):
        layer[at, :, 0:128] = rope
        layer[at, :, 128:129] = inv
    layer[2, :, 256:512] = np.where((band >= 0) & (band < 128), 0.0, NEG)
    for lv in range(7):
        b = 64 >> lv
        layer[3, :, lv * P:(lv + 1) * P] = (p // (2 * b) == f // (2 * b)) & (p % (2 * b) < b) & (f % (2 * b) >= b)
    layer[4, :, 256:768] = causal
    return kept, big, layer


PARTS_SPLIT = 3 * DT + FT


def mix_steps(part):
    return {"first": 2, 1: 1, 3: 1}.get(part, 0)


def n_groups(part):
    return {"first": 8 * TT, 1: 16 * TT, 3: 8 * TT}.get(part, 0)


def lin_total(parts):
    return sum(len(IN_PROJ[p][0]) + len(IN_PROJ[p][1]) + (4 if p == "first" else 0) + 2 * DT + 2 * FT for p in parts)


class Counts(dict):
    def __missing__(self, key):
        return 0

    def add(self, **more):
        for key, by in more.items():
            self[key] = self[key] + by


@contextmanager
def loop(eng, count):
    if count > 1:
        with eng.Fori(0, count) as i:
            yield i
    else:
        yield 0


def wait(eng, semaphore, value):
    if not isinstance(value, int) or value > 0:
        eng.wait_ge(semaphore, value)


def stream_length(parts):
    n = 0
    for part in parts:
        tiles, values = IN_PROJ[part]
        n += len(tiles) + len(values) + (8 if part == "first" else 0) + DT + 2 * FT + 3 * DT
    return n


def program(nc, xT, wstream, ada, cols, kept, bigc, layerc, pos, yT, parts):
    slots_total = stream_length(parts)
    ctx = ExitStack()
    with ctx:
        base = 16512
        top = [0]

        def place(name, shape, dt, at=None):
            size = int(np.prod(shape[1:]))
            if at is None:
                at = top[0]
                top[0] += -(-size // 8) * 8
            return nc.alloc_sbuf_tensor_at(name, shape, dt, offset=base + 4 * at)

        x = place("x", [P, DT, S], F32)
        h_at = top[0]
        h_hi = place("h_hi", [P, DT, S], F32R)
        h_lo = place("h_lo", [P, DT, S], F32R)
        big = top[0]
        hid_hi = place("hid_hi", [P, FT, S], F32R)
        hid_lo = place("hid_lo", [P, FT, S], F32R)
        raw = [place(f"raw{r}", [P, 8, P], F32) for r in range(RING)]
        w_hi = [place(f"w_hi{r}", [P, 8, P], F32R) for r in range(RING)]
        w_lo = [place(f"w_lo{r}", [P, 8, P], F32R) for r in range(RING)]
        ada_raw = [place(f"ada_raw{r}", [P, SLOT], F32) for r in range(ADA_RING)]
        ada_acc = place("ada_acc", [P, SLOT], F32)
        kp = place("kept", [P, sum(KEPT.values())], F32)
        co = place("cols", [P, NCOLS], F32)
        lc = place("layer_const", [P, LAYER_CONST], F32)
        cond = place("cond", [P, 8], F32)
        mod = [place(f"mod{r}", [P, 48], F32) for r in range(2)]
        small = place("small", [P, 160], F32)
        assert base + 4 * top[0] <= nc.sbuf_usable_end, top[0]

        h_tmp = place("h_tmp", [P, DT, S], F32, big + 16384)
        sq = [place(f"sq{r}", [P, S], F32, big + 20480 + r * S) for r in range(2)]
        rt = [place(f"rt{r}", [P, S], F32, big + 21504 + r * S) for r in range(2)]
        proj = place("proj", [P, 24, S], F32, big)
        first_v = place("first_v", [P, TT, S], F32, big + 19 * S)
        v_slc = place("v_slc", [P, TT, HD], F32, big + 23 * S)
        v_win = place("v_win", [P, TT, HD], F32, big + 23 * S + 256)
        tables = place("tables", [P, 3, S], F32, big + 12288)
        s1 = big + 12288 + 3 * S
        AT = {}
        for name, at in (("first", s1), ("late", big + 13312)):
            AT[name] = dict(
                s=[place(f"att_s_{name}{r}", [P, 520], F32, at + r * 520) for r in range(2)],
                p=[place(f"att_p_{name}{r}", [P, 520], F32, at + 1040 + r * 520) for r in range(2)],
                pt=[place(f"att_pt_{name}{r}", [P, S], F32, at + 2080 + r * S) for r in range(2)])
        bias = place("bias", [P, 4, S], F32, s1 + 3104)
        cmp_bias = place("cmp_bias", [P, 4, TT * NCMP], F32, s1 + 5152)
        blk = place("blk", [P, 2, 16, 32], F32, s1)
        blk_hi = place("blk_hi", [P, 2, 16, 32], F32R, s1 + 1024)
        blk_lo = place("blk_lo", [P, 2, 16, 32], F32R, s1 + 2048)
        CW = [S - P * j for j in range(TT)]
        CO = [sum(CW[:j]) for j in range(TT)]
        CWS = sum(CW)
        st_z = [place(f"st_z{e}", [P, CWS], F32, s1 + 3 * e * CWS) for e in range(2)]
        st_e = [place(f"st_e{e}", [P, CWS], F32, s1 + (3 * e + 1) * CWS) for e in range(2)]
        st_l = [place(f"st_l{e}", [P, CWS], F32, s1 + (3 * e + 2) * CWS) for e in range(2)]
        ml_v = place("ml_v", [P, TT, D], F32, big + 16 * S)
        ml_r = place("ml_rows", [8, 8, S], F32, h_at)
        ml_e = place("ml_e", [P, CWS], F32, big + 12288)
        ml_a = place("ml_a", [P, CWS], F32, big + 12288 + CWS)
        ml_d = place("ml_d", [P, S], F32, big + 12288 + 2 * CWS)
        ml_x = place("ml_x", [P, S], F32, big + 12288 + 2 * CWS + S)
        swa_v = place("swa_v", [P, TT, P], F32, big + 9 * S)
        swa_k = place("swa_k", [P, 2, S], F32, big + 10 * S)
        rope_cs = place("rope_cs", [P, 2, S], F32, big + 12288)
        rope_t = [place(f"rope_t{r}", [P, S], F32, big + 13312 + r * S) for r in range(4)]
        rope_i = place("rope_i", [P, S], I32, big + 13312 + 4 * S)
        hg_v = place("hg_v", [P, TT, D], F32, big + 24 * S)
        hg_k = place("hg_k", [P, 8, S], F32, big + 16384)
        hg_one = place("hg_one", [P, S], F32, big + 20480)
        hg_d = [place(f"hg_d{r}", [P, S], F32, h_at + r * S) for r in range(2)]
        hg_q = [place(f"hg_q{r}", [P, S], F32, h_at + (2 + r) * S) for r in range(2)]
        hg_t = [place(f"hg_t{r}", [P, S], F32, h_at + (4 + r) * S) for r in range(2)]
        hg_p = [place(f"hg_p{r}", [P, TT, 640], F32, h_at + (6 + 5 * r) * S) for r in range(2)]
        df_v = place("df_v", [P, TT, D], F32, big + 16 * S)

        bank = [ctx.enter_context(nc.psum_tensor(f"bank{b}", [P, S], F32)) for b in range(8)]

        def kept_at(name):
            at = 0
            for k, w in KEPT.items():
                if k == name:
                    return kp[:, at:at + w]
                at += w

        ident, ones, block64 = kept_at("ident"), kept_at("ones"), kept_at("block64")
        eps6, eps5, tiny = kept_at("eps6"), kept_at("eps5"), kept_at("tiny")

        def col(name, j=0, n=1):
            a = COLS[name][0]
            return co[:, a + j:a + j + n]

        dist, causal, logmult = tables[:, 0, :], tables[:, 1, :], tables[:, 2, :]
        gates = small[:, 0:48]
        kcmp = small[:, 48:80]
        vcmp = small[0:32, 80:144]
        att_max = [small[:, 144 + r:145 + r] for r in range(2)]
        att_sum = [small[:, 146 + r:147 + r] for r in range(2)]
        att_inv = [small[:, 148 + r:149 + r] for r in range(2)]
        lam = small[:, 150:151]
        lam_w = small[:, 151:157]
        hid_cmp = place("hid_cmp", [P, 4, 32], F32, s1 + 5648)
        hid_pre = place("hid_pre", [P, 4, 32], F32, s1 + 5776)
        ml_w = small[:, 0:16]
        lb = small[:, 0:8]
        one_lb = small[:, 8:16]
        lb_w = small[:, 16:80]

        names = ["const_loaded", "layer_const_loaded", "pos_loaded", "hi_done", "lo_done", "slot_used", "lin_free",
                 "ada_used", "ada_sum", "ada_mod", "cond_done", "sil_done", "part_hi", "part_lo", "n_sq", "n_sum",
                 "n_root", "h_ready", "ln_mean", "ln_centred", "ln_y", "ln_x", "x_scaled", "g_sq", "g_sum", "g_root",
                 "g_out", "att_scores", "att_ready", "att_exp", "att_normed", "att_turned", "att_copied", "att_pv",
                 "att_out", "gate_in", "gate_pre", "gate_out", "blk_ready", "blk_hi_done", "blk_lo_done", 
                 "cmp_act", "cmp_mm", "cmp_sq", "cmp_root", "cmp_out", "v_turned", "v_out", "mix_ready",
                 "st_scores", "st_scaled", "st_log", "st_keep", "st_suffix", "st_arg", "st_attn", "st_pv", "st_out",
                 "rope_ready", "rope_mm", "rope_out", "rope_ang", "ml_gate", "ml_pre", "ml_log", "ml_rows",
                 "ml_turn", "ml_w", "ml_spread", "ml_diag", "ml_exp", "ml_a", "ml_den", "ml_num", "ml_out", "ml_sig",
                 "hg_lb", "hg_lbe", "hg_sig", "hg_dec", "hg_log", "hg_diff", "hg_e", "hg_qk", "hg_mm", "hg_put",
                 "hg_pv", "hg_out", "hg_gate", "hg_zero", "lam_in", "lam_exp", "lam_done", "stored",
                 "act_chain", "dve_chain"]
        sm = namedtuple("Semaphores", names)(*[ctx.enter_context(nc.semaphore(name)) for name in names])
        raw_loaded = [ctx.enter_context(nc.semaphore(f"raw_loaded{r}")) for r in range(RING)]
        ada_loaded = [ctx.enter_context(nc.semaphore(f"ada_loaded{r}")) for r in range(ADA_RING)]

        def half(tile_index, head):
            return proj[HD * (head % 2):HD * (head % 2) + HD, tile_index, :]

        def job(q, k, width, bias_ap, values, **more):
            return dict(q=q, k=k, w=width, bias=bias_ap, v=values, sink=None, vis=None, gate=None, first=True,
                        last=True, dv=HD, row=0, dest=None) | more

        def nsa_jobs():
            jobs = []
            for hd in range(NSA_HEADS):
                b = HD * (hd % 2)
                for i in range(TT):
                    q = half(hd // 2, hd)[:, i * P:(i + 1) * P]
                    w = (i + 1) * P
                    common = dict(row=b, dest=q)
                    tok = dict(bias_ap=bias[:, hd, S - w:S])
                    gate = [gates[:, i * 12 + hd * 3 + br:i * 12 + hd * 3 + br + 1] for br in range(3)]
                    jobs.append(job(q, kcmp[b:b + HD, 0:NCMP], NCMP, cmp_bias[:, hd, i * NCMP:(i + 1) * NCMP],
                                    [(vcmp[0:NCMP, :], NCMP)], vis=lc[:, 124 + i * NCMP:124 + (i + 1) * NCMP],
                                    gate=gate[0], last=False, **common))
                    jobs.append(job(q, half(9, hd)[:, 0:w], w, values=[(v_slc[:, j, :], P) for j in range(i + 1)],
                                    gate=gate[1], first=False, last=False, **tok, **common))
                    jobs.append(job(q, half(10, hd)[:, 0:w], w, values=[(v_win[:, j, :], P) for j in range(i + 1)],
                                    gate=gate[2], first=False, **tok, **common))
            return jobs

        def dil_jobs():
            jobs = []
            for hd in range(4):
                for i in range(TT):
                    q, w = half(6 + hd // 2, hd)[:, i * P:(i + 1) * P], (i + 1) * P
                    jobs.append(job(q, half(17 + hd // 2, hd)[:, 0:w], w, bias[:, hd, S - w:S],
                                    [(first_v[:, j, 256 + hd * HD:256 + (hd + 1) * HD], P) for j in range(i + 1)],
                                    row=HD * (hd % 2), dest=q))
            return jobs

        def swa_jobs():
            jobs = []
            for hd in range(16):
                kv = hd // 8
                b = HD * (hd % 2)
                for i in range(TT):
                    q, lo = half(hd // 2, hd)[:, i * P:(i + 1) * P], max(0, i - 1)
                    w = (i + 1 - lo) * P
                    jobs.append(job(q, swa_k[b:b + HD, kv, lo * P:(i + 1) * P], w, lc[:, 512 - w:512],
                                    [(swa_v[:, j, kv * HD:(kv + 1) * HD], P) for j in range(lo, i + 1)],
                                    sink=col("sinks", hd), row=b, dest=q))
            return jobs

        def diff_jobs():
            jobs = []
            for hd in range(8):
                for i in range(TT):
                    w = (i + 1) * P
                    for c in range(2):
                        jobs.append(job(proj[HD * c:HD * c + HD, hd, i * P:(i + 1) * P],
                                        proj[HD * c:HD * c + HD, 8 + hd, 0:w], w, lc[:, 768 - w:768],
                                        [(df_v[:, j, hd * P:(hd + 1) * P], P) for j in range(i + 1)],
                                        gate=lam if c else None, first=c == 0, last=c == 1, dv=P,
                                        dest=proj[:, hd, i * P:(i + 1) * P]))
            return jobs

        def item(src, mat, scale, gain, out, mul=None):
            return dict(src=src, mat=mat, scale=scale, gain=gain, out=out, mul=mul)

        def first_norms():
            items = []
            for t, g in ((0, "g_q_nsa"), (1, "g_q_nsa"), (6, "g_q_dil"), (7, "g_q_dil"), (17, "g_k_dil"),
                         (18, "g_k_dil")):
                items.append(item([proj[:, t, :]], block64, 1.0, [col(g)], [[proj[:, t, :]]]))
            for t, g in ((9, "g_k_slc"), (10, "g_k_win")):
                items.append(item([proj[0:HD, t, :]], block64[0:HD, 0:HD], 1.0, [col(g)[0:HD, :]],
                                  [[proj[HD:P, t, :], proj[0:HD, t, :]]]))
            return items

        def out_norms(part):
            if part == "first":
                return [item([proj[:, t, :]], block64, 1.0, [col("g_out", t)], [[proj[:, t, :]]]) for t in range(DT)]
            if part == 0:
                return [item([proj[:, 2 * g + e, :] for e in range(2)], ones, 1 / 256,
                             [col("mlstm_norm", 2 * g + e) for e in range(2)],
                             [[proj[:, 2 * g + e, :]] for e in range(2)], [proj[:, 8 + 2 * g + e, :] for e in range(2)])
                        for g in range(4)]
            if part == 2:
                return [item([proj[:, t, :]], ones, 1 / P, [col("hgrn_norm", t)], [[proj[:, t, :]]],
                             [proj[:, 16 + t, :]]) for t in range(DT)]
            if part == 3:
                return [item([proj[:, t, :]], ones, 1 / P, [lam_w[:, 5:6]], [[proj[:, t, :]]]) for t in range(DT)]
            return []

        def mod_col(layer, sub, kind, j, n=1):
            a = sub * 24 + kind * 8 + j
            return mod[layer % 2][:, a:a + n]

        SHIFT, ONE_SCALE, ONE_GATE = range(3)
        LV = [256, 128, 64, 32, 16, 8, 4, 2, 1]

        def halves(ap, b):
            q = ap.rearrange("p (n h b) -> p n h b", h=2, b=b)
            return q[:, :, 0, :], q[:, :, 1, :]

        block = ctx.enter_context(nc.Block())

        @block.sync
        def _(sp):
            n = Counts()

            def load_slot(k, i=0, step=0):
                if k >= RING:
                    sp.wait_ge(sm.lo_done, k - RING + 1 + step * i)
                sp.dma_start(raw[k % RING][:, :, :].rearrange("p a b -> p (a b)"),
                             wstream[k + step * i, :, :]).then_inc(raw_loaded[k % RING], 16)

            def load_ada(a, i=0, step=0):
                if a >= ADA_RING or not isinstance(i, int):
                    sp.wait_ge(sm.ada_used, a - ADA_RING + 1 + step * i)
                sp.dma_start(ada_raw[a % ADA_RING][:, :],
                             ada[a + step * i, :, :]).then_inc(ada_loaded[a % ADA_RING], 16)

            def load_slots(count):
                k = n["slot"]
                n.add(slot=count)
                if k == 0:
                    for q in range(RING):
                        load_slot(q)
                    k, count = RING, count - RING
                with loop(sp, count // RING) as i:
                    for q in range(RING):
                        load_slot(k + q, i, RING)
                for q in range(count // RING * RING, count):
                    load_slot(k + q)

            def load_ffn(with_ada):
                ahead = 6
                load_slots(ahead)
                k, a = n["slot"], n["ada"]
                if with_ada:
                    first = 0
                    if a == 0:
                        for q in range(8):
                            load_slot(k + q)
                            load_ada(a + q)
                        first = 1
                    with sp.Fori(first, 5) as i:
                        for q in range(8):
                            load_slot(k + q, i, 8)
                            load_ada(a + q, i, 8)
                    for q, lot in ((40, (40, 41)), (41, (42, 43)), (42, ()), (43, (44, 45)), (44, (46, 47))):
                        for more in lot:
                            load_ada(a + more)
                        load_slot(k + q)
                    n.add(slot=45, ada=48)
                load_slots(2 * FT + 3 * DT - ahead - (45 if with_ada else 0))

            sp.dma_start(kp[:, :], kept).then_inc(sm.const_loaded, 16)
            sp.dma_start(x[:, :, :], xT).then_inc(sm.const_loaded, 16)
            sp.dma_start(co[:, :], cols).then_inc(sm.const_loaded, 16)
            for at, part in enumerate(parts):
                tiles, values = IN_PROJ[part]
                if part != "first":
                    sp.wait_ge(sm.part_lo, PARTS_SPLIT * at)
                    sp.dma_start(lc[:, :], layerc[1 + part, :, :]).then_inc(sm.layer_const_loaded, 16)
                load_slots(len(tiles) + len(values))
                if part == "first":
                    sp.dma_start(lc[:, :], layerc[0, :, :]).then_inc(sm.layer_const_loaded, 16)
                    sp.dma_start(tables[:, :, :].rearrange("p a b -> p (a b)"), bigc).then_inc(sm.layer_const_loaded, 16)
                if part in (1, 3):
                    sp.wait_ge(sm.lin_free, lin_total(parts[:at]))
                    sp.dma_start(rope_i[:, :], pos).then_inc(sm.pos_loaded, 16)
                if part == "first":
                    load_slots(8)
                load_slots(DT)
                load_ffn(at + 1 < len(parts))
            if parts[-1] == "first":
                sp.wait_ge(sm.lin_free, lin_total(parts))
            else:
                sp.wait_ge(sm.ln_x, 2 * DT * (len(parts) - 1))
            sp.dma_start(yT, x[:, :, :]).then_inc(sm.stored, 16)
            sp.wait_ge(sm.stored, 16)

        @block.gpsimd
        def _(pool):
            def low(k, i=0, step=0):
                pool.wait_ge(sm.hi_done, k + 1 + step * i)
                nc.gpsimd.tensor_tensor(w_lo[k % RING][:, :, :], raw[k % RING][:, :, :],
                                        w_hi[k % RING][:, :, :].bitcast(F32), ALU.subtract).then_inc(sm.lo_done, 1)

            def low_to(end):
                k, count = n["slot"], end - n["slot"]
                with loop(pool, count // RING) as i:
                    for q in range(RING):
                        low(k + q, i, RING)
                for q in range(count // RING * RING, count):
                    low(k + q)
                n.add(slot=count)

            def hgrn():
                for r in range(2):
                    nc.gpsimd.memset(hg_q[r][:, :], 0.0)
                    op = nc.gpsimd.memset(hg_t[r][:, :], 0.0)
                op.then_inc(sm.hg_zero, 1)
                pool.wait_ge(sm.hg_zero, 1)
                for hd in range(8):
                    for at in range(9):
                        m, i, b = hd * 10 + at, hd * 9 + at, LV[at]
                        pool.wait_ge(sm.hg_e, i + 1)
                        wait(pool, sm.hg_mm, m - 1)
                        d = halves(hg_d[i % 2][:, :], b)
                        nc.gpsimd.tensor_tensor(halves(hg_q[m % 2][:, :], b)[1], halves(proj[:, hd, :], b)[1], d[1],
                                                ALU.mult)
                        nc.gpsimd.tensor_tensor(halves(hg_t[m % 2][:, :], b)[0], halves(hg_k[:, hd, :], b)[0], d[0],
                                                ALU.mult).then_inc(sm.hg_qk, 2 if at == 8 else 1)

            n = Counts()
            first_slot = 0
            for at, part in enumerate(parts):
                tiles, values = IN_PROJ[part]
                if part == 2:
                    low_to(first_slot + len(tiles) + len(values) + LEAD)
                    pool.wait_ge(sm.lin_free, lin_total(parts[:at]) + len(tiles) + len(values))
                    hgrn()
                first_slot += stream_length([part])
            low_to(slots_total)

        @block.tensor
        def _(pe):
            n = Counts()
            mm, turn = nc.tensor.matmul, nc.tensor.transpose

            def slot_products(k, i, step, pairs, first, last):
                pe.wait_ge(sm.lo_done, k + 1 + step * i)
                r = k % RING
                for at, (out, w, hi, lo) in enumerate(pairs):
                    begin, end = first and w == 0, last and w == len(pairs) - 1
                    mm(out, w_hi[r][:, at, :], hi, start=first and at == 0, stop=False)
                    mm(out, w_hi[r][:, at, :], lo, start=False, stop=False)
                    op = mm(out, w_lo[r][:, at, :], hi, start=False, stop=last and at == len(pairs) - 1)
                op.then_inc(sm.slot_used, 1)

            def m_tile(k, mt, i, step, mt_step, hi, lo, chunks, parts_from=None):
                if mt >= 4:
                    pe.wait_ge(sm.lin_free, mt - 3 + mt_step * i)
                c0 = 0
                for s, m in enumerate(chunks):
                    if parts_from is not None:
                        pe.wait_ge(sm.part_lo, parts_from + c0 + m)
                    slot_products(k + s, i, step,
                                  [(bank[mt % 4][:, 0:hi.shape[2]], c, hi[:, c0 + c, :], lo[:, c0 + c, :])
                                   for c in range(m)], s == 0, s == len(chunks) - 1)
                    c0 += m

            def linear(tiles, hi, lo, chunks):
                k, mt, per = n["slot"], n["mt"], len(chunks)
                done = 0
                if mt < 4:
                    for q in range(4):
                        m_tile(k + q * per, mt + q, 0, 0, 0, hi, lo, chunks)
                    done = 4
                count = (tiles - done) // 4
                if count:
                    with loop(pe, count) as i:
                        for q in range(4):
                            m_tile(k + (done + q) * per, mt + done + q, i, 4 * per, 4, hi, lo, chunks)
                for q in range(done + 4 * count, tiles):
                    m_tile(k + q * per, mt + q, 0, 0, 0, hi, lo, chunks)
                n.add(slot=tiles * per, mt=tiles)

            def value_group(k, mt, i, step):
                for s in range(TT):
                    pe.wait_ge(sm.lo_done, k + s + 1 + step * i)
                    r = (k + s) % RING
                    hi, lo = (w[r][:, :, :].rearrange("p (c t) m -> p c (t m)", c=2) for w in (w_hi, w_lo))
                    for t in range(TT):
                        if s == 0:
                            pe.wait_ge(sm.lin_free, mt + t - 3 + step * i)
                        out, tok = bank[(mt + t) % 4][:, :], slice(t * P, (t + 1) * P)
                        for c in range(2):
                            d = 2 * s + c
                            mm(out, h_hi[:, d, tok], hi[:, c, :], start=d == 0, stop=False)
                            mm(out, h_hi[:, d, tok], lo[:, c, :], start=False, stop=False)
                            op = mm(out, h_lo[:, d, tok], hi[:, c, :], start=False, stop=d == DT - 1)
                    op.then_inc(sm.slot_used, 1)

            def value_tile(k, mt):
                pe.wait_ge(sm.lin_free, mt - 3)
                pe.wait_ge(sm.lo_done, k + 1)
                r = k % RING
                for t in range(TT):
                    out, tok = bank[mt % 4][:, t * P:(t + 1) * P], slice(t * P, (t + 1) * P)
                    for c in range(DT):
                        mm(out, h_hi[:, c, tok], w_hi[r][:, c, :], start=c == 0, stop=False)
                        mm(out, h_hi[:, c, tok], w_lo[r][:, c, :], start=False, stop=False)
                        op = mm(out, h_lo[:, c, tok], w_hi[r][:, c, :], start=False, stop=c == DT - 1)
                op.then_inc(sm.slot_used, 1)

            def value_tiles(count):
                k, mt = n["slot"], n["mt"]
                n.add(slot=count, mt=count)
                if count < TT:
                    value_tile(k, mt)
                else:
                    with loop(pe, count // TT) as i:
                        value_group(k, mt, i, TT)

            def early_chunk(c):
                k, mt = n["slot"], n["mt"]
                pe.wait_ge(sm.part_lo, n["part"] + c + 1)
                for q in range(EARLY):
                    if c == 0:
                        wait(pe, sm.lin_free, mt + q - 3)
                        pe.wait_ge(sm.lo_done, k + q + 1)
                    r, out = (k + q) % RING, bank[(mt + q) % 4][:, :]
                    mm(out, w_hi[r][:, c, :], h_hi[:, c, :], start=c == 0, stop=False)
                    mm(out, w_hi[r][:, c, :], h_lo[:, c, :], start=False, stop=False)
                    op = mm(out, w_lo[r][:, c, :], h_hi[:, c, :], start=False, stop=c == DT - 1)
                    if c == DT - 1:
                        op.then_inc(sm.slot_used, 1)

            def early_done():
                n.add(part=DT, slot=EARLY, mt=EARLY)

            def early_tiles():
                for c in range(DT):
                    early_chunk(c)
                early_done()

            def residual_tiles(done, hi, lo, chunks, sums, parts_from=None, after_first=None):
                k, mt, per = n["slot"], n["mt"], len(chunks)
                summed = 0
                for q in range(done, DT + 1):
                    if q < DT:
                        m_tile(k + (q - done) * per, mt + q - done, 0, 0, 0, hi, lo, chunks,
                               parts_from if q == 0 else None)
                        if q == 0:
                            after_first()
                    if sums:
                        while summed < q:
                            sums(summed, mt - done)
                            summed += 1
                n.add(slot=(DT - done) * per, mt=DT - done)

            def sum_x(c, mt):
                pe.wait_ge(sm.lin_free, mt + c + 1)
                mm(bank[5][:, :], ones, x[:, c, :], start=c == 0, stop=c == DT - 1).then_inc(sm.ln_mean, 1)

            def sum_squares(c, mt):
                pe.wait_ge(sm.n_sq, n["sq"] + 1)
                mm(bank[6][:, :], ones, sq[c % 2][:, :], start=c == 0, stop=c == DT - 1).then_inc(sm.n_sum, 1)
                n.add(sq=1)

            def mean_squares():
                for c in range(DT):
                    sum_squares(c, 0)

            def group_norms(items, linear_follows=False):
                c = 0
                for t in range(len(items) + 2):
                    if t < len(items):
                        it = items[t]
                        wait(pe, sm.g_root, n["gn"] + t - 1)
                        for u in range(len(it["src"])):
                            n.add(gt=1)
                            pe.wait_ge(sm.g_sq, n["gt"])
                            rows = it["src"][u].shape[0]
                            mm(bank[6 + t % 2][0:rows, :], it["mat"], sq[(n["gt"] - 1) % 2][0:rows, :],
                               start=u == 0, stop=u == len(it["src"]) - 1).then_inc(sm.g_sum, 1)
                    if t >= 2 and linear_follows:
                        for _ in items[t - 2]["src"]:
                            early_chunk(c)
                            c += 1
                n.add(gn=len(items))

            def attention(jobs, bufs):
                a, g = n["att"], n["att_g"]
                for step in range(len(jobs) + 3):
                    if step < len(jobs):
                        j, it = step, jobs[step]
                        wait(pe, sm.att_ready, a + j - 1)
                        mm(bank[j % 2][:, 0:it["w"]], it["q"], it["k"], start=True,
                           stop=True).then_inc(sm.att_scores, 1)
                    if 2 <= step <= len(jobs) + 1:
                        j, it = step - 2, jobs[step - 2]
                        pe.wait_ge(sm.att_normed, a + j + 1)
                        wait(pe, sm.att_copied, a + j - 1)
                        at = 0
                        for t, (_, keys) in enumerate(it["v"]):
                            op = turn(bank[2 + j % 2][0:keys, t * P:(t + 1) * P], bufs["p"][j % 2][:, at:at + keys],
                                      ident)
                            at += keys
                        op.then_inc(sm.att_turned, 1)
                    if step >= 3:
                        j, it = step - 3, jobs[step - 3]
                        pe.wait_ge(sm.att_copied, a + j + 1)
                        if it["first"]:
                            g += 1
                            wait(pe, sm.att_out, g - 4)
                        out = bank[4 + g % 4][it["row"]:it["row"] + it["dv"], 0:P]
                        for t, (v, keys) in enumerate(it["v"]):
                            op = mm(out, v, bufs["pt"][j % 2][0:keys, t * P:(t + 1) * P],
                                    start=it["first"] and t == 0, stop=it["last"] and t == len(it["v"]) - 1)
                        op.then_inc(sm.att_pv, 1)
                n.add(att=len(jobs), att_g=sum(it["last"] for it in jobs))

            def first_mixer():
                for kv in range(2):
                    if kv == 0:
                        pe.wait_ge(sm.blk_lo_done, 2)
                    linear(2, blk_hi[:, kv, :, :], blk_lo[:, kv, :, :], [8, 8])
                pe.wait_ge(sm.cmp_act, 2)
                w2 = [col("w2", 128 * kv, 128).rearrange("p (m d) -> p m d", m=2) for kv in range(2)]
                for m in range(2):
                    op = mm(bank[4][0:HD, 0:32], w2[0][:, m, :], hid_cmp[:, m, :], start=m == 0, stop=m == 1)
                for m in range(2):
                    op = mm(bank[5][0:32, 0:HD], hid_cmp[:, 2 + m, :], w2[1][:, m, :], start=m == 0, stop=m == 1)
                op.then_inc(sm.cmp_mm, 1)
                pe.wait_ge(sm.cmp_sq, 1)
                mm(bank[6][0:HD, 0:32], block64[0:HD, 0:HD], hid_pre[0:HD, 0, :], start=True,
                   stop=True).then_inc(sm.cmp_mm, 1)
                for b, tile in ((0, 9), (1, 10)):
                    for t in range(TT):
                        op = turn(bank[7][:, (b * TT + t) * HD:(b * TT + t + 1) * HD],
                                  proj[HD:P, tile, t * P:(t + 1) * P], ident[HD:P, HD:P])
                op.then_inc(sm.v_turned, 1)
                pe.wait_ge(sm.cmp_root, 1)
                pe.wait_ge(sm.v_out, 1)
                group_norms(first_norms())
                pe.wait_ge(sm.mix_ready, 1)
                attention(nsa_jobs(), AT["first"])
                stick_breaking()
                pe.wait_ge(sm.mix_ready, 2)
                attention(dil_jobs(), AT["first"])

            def stick_breaking():
                suffix, every = lc[:, 384:512], ones
                pe.wait_ge(sm.att_out, n["att_g"])
                for h0 in (0, 2):
                    for e in range(2):
                        hd = h0 + e
                        q, k = half(4 + hd // 2, hd), half(15 + hd // 2, hd)
                        wait(pe, sm.st_out, hd - 1)
                        for j in range(TT):
                            op = mm(bank[4 * e + j][:, 0:CW[j]], k[:, j * P:(j + 1) * P], q[:, j * P:S], start=True,
                                    stop=True)
                        op.then_inc(sm.st_scores, 1)
                    for e in range(2):
                        pe.wait_ge(sm.st_keep, h0 + e + 1)
                        for j in range(TT):
                            for jj in range(j, TT):
                                op = mm(bank[4 * e + j][:, P * (jj - j):CW[j]], suffix if jj == j else every,
                                        st_l[e][:, CO[jj]:CO[jj] + CW[jj]], start=jj == j, stop=jj == TT - 1)
                        op.then_inc(sm.st_suffix, 1)
                    for e in range(2):
                        hd, b = h0 + e, HD * e
                        pe.wait_ge(sm.st_attn, hd + 1)
                        for j in range(TT):
                            op = mm(bank[4 * e][b:b + HD, j * P:S], first_v[:, j, hd * HD:(hd + 1) * HD],
                                    st_z[e][:, CO[j]:CO[j] + CW[j]], start=j == 0, stop=j == TT - 1)
                        op.then_inc(sm.st_pv, 1)

            def rope(tiles):
                pe.wait_ge(sm.layer_const_loaded, 16 * n["lc"])
                for t in tiles:
                    wait(pe, sm.rope_out, n["rope"] - 1)
                    mm(bank[4 + n["rope"] % 2][:, :], lc[:, 0:128], proj[:, t, :], start=True,
                       stop=True).then_inc(sm.rope_mm, 1)
                    n.add(rope=1)

            def mlstm_gates():
                gw = col("mlstm_gw", 0, 64).rearrange("p (c g) -> p c g", c=DT)
                for g in range(2):
                    for c in range(DT):
                        op = mm(bank[6 + g][0:4, :], gw[:, c, 4 * g:4 * g + 4], h_tmp[:, c, :], start=c == 0,
                                stop=c == DT - 1)
                op.then_inc(sm.ml_gate, 1)

            def mlstm():
                pe.wait_ge(sm.ml_rows, 1)
                for t in range(TT):
                    op = turn(bank[0][:, 4 * t:4 * t + 4], ml_r[0:4, 4, t * P:(t + 1) * P], ident[0:4, 0:4])
                op.then_inc(sm.ml_turn, 1)
                pe.wait_ge(sm.ml_w, 1)
                for hd in range(4):
                    q, k = proj[:, 2 * hd, :], proj[:, 2 * hd + 1, :]
                    sel = lc[0:4, hd * P:(hd + 1) * P]
                    wait(pe, sm.ml_out, hd)
                    mm(bank[0][:, :], sel, ml_r[0:4, 5, :], start=True, stop=True)
                    mm(bank[1][:, :], sel, ml_r[0:4, 6, :], start=True, stop=True)
                    for j in range(TT):
                        op = mm(bank[2 + j][:, 0:CW[j]], k[:, j * P:(j + 1) * P], q[:, j * P:S], start=True, stop=True)
                    op.then_inc(sm.ml_spread, 1)
                    pe.wait_ge(sm.ml_a, hd + 1)
                    for j in range(TT):
                        op = mm(bank[6][:, j * P:S], ones, ml_a[:, CO[j]:CO[j] + CW[j]], start=j == 0,
                                stop=j == TT - 1)
                    op.then_inc(sm.ml_den, 1)
                    for e in range(2):
                        for j in range(TT):
                            op = mm(bank[7 if e else 0][:, j * P:S], ml_v[:, j, hd * 256 + e * P:hd * 256 + (e + 1) * P],
                                    ml_a[:, CO[j]:CO[j] + CW[j]], start=j == 0, stop=j == TT - 1)
                    op.then_inc(sm.ml_num, 1)

            def hgrn():
                def values(hd):
                    pe.wait_ge(sm.hg_put, hd * 10 + 10)
                    wait(pe, sm.hg_out, hd - 1)
                    for j in range(TT):
                        op = mm(bank[6 + hd % 2][:, j * P:S], hg_v[:, j, hd * P:(hd + 1) * P],
                                hg_p[hd % 2][:, j, 0:CW[j]], start=j == 0, stop=j == TT - 1)
                    op.then_inc(sm.hg_pv, 1)

                for hd in range(8):
                    for at, b in enumerate(LV + [0]):
                        m = hd * 10 + at
                        pe.wait_ge(sm.hg_qk, m + 1)
                        wait(pe, sm.hg_put, m - 1)
                        kk = hg_t[m % 2][:, :] if b else hg_k[:, hd, :]
                        qq = hg_q[m % 2][:, :] if b else proj[:, hd, :]
                        if b == 256:
                            for j in range(2):
                                op = mm(bank[j][:, 0:256], kk[:, j * P:(j + 1) * P], qq[:, 256:S], start=True, stop=True)
                        elif b == 128:
                            for j in (0, 2):
                                op = mm(bank[2][:, j * 64:j * 64 + P], kk[:, j * P:(j + 1) * P],
                                        qq[:, (j + 1) * P:(j + 2) * P], start=True, stop=True)
                        else:
                            for j in range(TT):
                                op = mm(bank[4 + m % 2][:, j * P:(j + 1) * P], kk[:, j * P:(j + 1) * P],
                                        qq[:, j * P:(j + 1) * P], start=True, stop=True)
                        op.then_inc(sm.hg_mm, 1)
                        if at == 2 and hd:
                            values(hd - 1)
                values(7)

            def ffn(with_ada, sums):
                early_tiles()
                k, mt, a = n["slot"], n["mt"], n["ada"]

                def ada_sums(g, i):
                    if not with_ada:
                        return
                    pe.wait_ge(sm.ada_used, a + 8 * g + 8 + 8 * i)
                    for j in range(8):
                        op = mm(bank[7][:, j:j + 1], ada_acc[:, j * P:(j + 1) * P], ones[:, 0:1], start=True, stop=True)
                    op.then_inc(sm.ada_sum, 1)

                with pe.Fori(0, 5) as i:
                    for q in range(8):
                        m_tile(k + q, mt + q, i, 8, 8, h_hi, h_lo, [8])
                        if q == 5:
                            ada_sums(0, i)
                for q in range(40, 2 * FT - EARLY):
                    m_tile(k + q, mt + q, 0, 0, 0, h_hi, h_lo, [8])
                n.add(slot=2 * FT - EARLY, mt=2 * FT - EARLY, ada=48 if with_ada else 0)
                residual_tiles(0, hid_hi, hid_lo, [8, 8, 6], sums, parts_from=n["part"],
                               after_first=lambda: ada_sums(5, 0))
                n.add(part=FT)

            pe.wait_ge(sm.const_loaded, 48)
            for at, part in enumerate(parts):
                tiles, values = IN_PROJ[part]
                n.add(lc=2 if part == "first" else 1)
                if part == "first":
                    mean_squares()
                early_tiles()
                if part == "first":
                    gw = col("gate_w", 0, 96).rearrange("p (c g) -> p c g", c=DT)
                    for t in range(TT):
                        for c in range(DT):
                            op = mm(bank[6][:, t * 12:(t + 1) * 12], h_tmp[:, c, t * P:(t + 1) * P], gw[:, c, :],
                                    start=c == 0, stop=c == DT - 1)
                    op.then_inc(sm.gate_in, 1)
                if part == 0:
                    mlstm_gates()
                linear(len(tiles) - EARLY, h_hi, h_lo, [8])
                value_tiles(len(values))
                pe.wait_ge(sm.layer_const_loaded, 16 * n["lc"])
                pe.wait_ge(sm.lin_free, n["mt"])
                if part == "first":
                    first_mixer()
                elif part == 0:
                    mlstm()
                elif part == 1:
                    rope(range(9))
                    pe.wait_ge(sm.mix_ready, n["mix"] + 1)
                    attention(swa_jobs(), AT["late"])
                elif part == 2:
                    hgrn()
                else:
                    rope(range(16))
                    pe.wait_ge(sm.mix_ready, n["mix"] + 1)
                    attention(diff_jobs(), AT["late"])
                n.add(mix=mix_steps(part))
                if out_norms(part):
                    group_norms(out_norms(part), linear_follows=True)
                    early_done()
                else:
                    early_tiles()
                residual_tiles(EARLY, h_hi, h_lo, [8], sum_squares if part == "first" else sum_x)
                if part != "first":
                    mean_squares()
                ffn(at + 1 < len(parts), None if part == "first" else sum_x)
                if part != "first":
                    mean_squares()

        @block.scalar
        def _(act):
            n = Counts()
            fn = nc.scalar.activation

            def link(ins):
                n.add(act_chain=1)
                ins.then_inc(sm.act_chain, 1)
                act.wait_ge(sm.act_chain, n["act_chain"])

            def split(t, i=0, step=0):
                if not isinstance(i, int) or t < slots_total:
                    act.wait_ge(raw_loaded[t % RING], 16 * (t // RING + 1) + 16 * step // RING * i)
                    if t >= RING:
                        act.wait_ge(sm.slot_used, t - RING + 1 + step * i)
                    fn(w_hi[t % RING][:, :, :], raw[t % RING][:, :, :], ACT.Copy).then_inc(sm.hi_done, 1)

            def split_ahead(count):
                k = n["slot"]
                n.add(slot=count)
                done = 0
                if k + LEAD < RING:
                    for q in range(RING):
                        split(k + q + LEAD)
                    done = RING
                full = (count - done) // RING
                if k + LEAD + count > slots_total:
                    full = 0
                if full:
                    with loop(act, full) as i:
                        for q in range(RING):
                            split(k + done + q + LEAD, i, RING)
                for q in range(done + full * RING, count):
                    split(k + q + LEAD)

            def mean_squares(eps, ready):
                for c in range(DT):
                    ready(c)
                    wait(act, sm.n_sum, n["sq"] + c - 1)
                    fn(sq[c % 2][:, :], x[:, c, :], ACT.Square).then_inc(sm.n_sq, 1)
                n.add(sq=DT)
                act.wait_ge(sm.n_sum, n["sq"])
                fn(rt[0][:, :], bank[6][:, :], ACT.Sqrt, bias=eps, scale=1 / D).then_inc(sm.n_root, 1)

            def high(c, src):
                fn(h_hi[:, c, :], src, ACT.Copy).then_inc(sm.part_hi, 1)

            def split_input(normed, scaled):
                for c in range(DT + 1):
                    if normed and c < DT:
                        add_bias(c)
                    if c:
                        act.wait_ge(sm.h_ready, n["h"] + c)
                        high(c - 1, h_tmp[:, c - 1, :])
                        if scaled:
                            nc.scalar.mul(x[:, c - 1, :], x[:, c - 1, :], ALPHA).then_inc(sm.x_scaled, 1)
                n.add(h=DT, part=DT)

            def centred_squares():
                mean_squares(eps5, lambda c: act.wait_ge(sm.ln_centred, n["ln"] * DT + c + 1))
                n.add(ln=1)

            def add_bias(c):
                act.wait_ge(sm.ln_y, (n["ln"] - 1) * DT + c + 1)
                fn(x[:, c, :], x[:, c, :], ACT.Identity,
                   bias=col("ln_b", n["ln_at"] * 8 + c)).then_inc(sm.ln_x, 1)

            def group_norms(items, linear_follows=False):
                sums, c = [], 0
                for t in range(len(items) + 2):
                    if t < len(items):
                        for src in items[t]["src"]:
                            wait(act, sm.g_sum, n["gt"] - 1)
                            fn(sq[n["gt"] % 2][0:src.shape[0], :], src, ACT.Square).then_inc(sm.g_sq, 1)
                            n.add(gt=1)
                        sums.append(n["gt"])
                    if 1 <= t <= len(items):
                        it = items[t - 1]
                        act.wait_ge(sm.g_sum, sums[t - 1])
                        wait(act, sm.g_out, n["gn"] + t - 2)
                        r = it["src"][0].shape[0]
                        fn(rt[(t - 1) % 2][0:r, :], bank[6 + (t - 1) % 2][0:r, :], ACT.Sqrt, bias=eps6[0:r, :],
                           scale=it["scale"]).then_inc(sm.g_root, 1)
                    if t >= 2 and linear_follows:
                        act.wait_ge(sm.g_out, n["gn"] + t - 1)
                        for _ in items[t - 2]["src"]:
                            high(c, proj[:, c, :])
                            c += 1
                n.add(gn=len(items), part=c)

            def attention(jobs, bufs):
                a = n["att"]
                for step in range(len(jobs) + 1):
                    if step < len(jobs):
                        j, it = step, jobs[step]
                        w = it["w"] + (it["sink"] is not None)
                        act.wait_ge(sm.att_ready, a + j + 1)
                        wait(act, sm.att_turned, a + j - 1)
                        fn(bufs["p"][j % 2][:, 0:w], bufs["s"][j % 2][:, 0:w], ACT.Exp, bias=att_max[j % 2],
                           accum_out=att_sum[j % 2]).then_inc(sm.att_exp, 1)
                    if step >= 1:
                        j, it = step - 1, jobs[step - 1]
                        act.wait_ge(sm.att_turned, a + j + 1)
                        wait(act, sm.att_pv, a + j - 1)
                        r, w = it["v"][0][1], len(it["v"]) * P
                        fn(bufs["pt"][j % 2][0:r, 0:w], bank[2 + j % 2][0:r, 0:w], ACT.Copy).then_inc(sm.att_copied, 1)
                n.add(att=len(jobs))

            def first_mixer():
                act.wait_ge(sm.blk_ready, 2)
                for kv in range(2):
                    fn(blk_hi[:, kv, :, :], blk[:, kv, :, :], ACT.Copy).then_inc(sm.blk_hi_done, 1)
                split_ahead(8)
                for kv in range(2):
                    act.wait_ge(sm.lin_free, n["mt"] + 2 * kv + 2)
                    fn(hid_cmp[:, 2 * kv:2 * kv + 2, :], hid_pre[:, 2 * kv:2 * kv + 2, :],
                       ACT.Gelu_apprx_tanh).then_inc(sm.cmp_act, 1)
                act.wait_ge(sm.cmp_mm, 1)
                fn(hid_pre[0:HD, 0, :], bank[4][0:HD, 0:32], ACT.Square).then_inc(sm.cmp_sq, 1)
                act.wait_ge(sm.cmp_mm, 2)
                fn(hid_pre[0:HD, 1, :], bank[6][0:HD, 0:32], ACT.Sqrt, bias=eps6[0:HD, :]).then_inc(sm.cmp_root, 1)
                group_norms(first_norms())
                attention(nsa_jobs(), AT["first"])
                act.wait_ge(sm.att_out, TT * NSA_HEADS)
                for h0 in (0, 2):
                    for e in range(2):
                        z, s = st_z[e], st_e[e]
                        act.wait_ge(sm.st_scores, h0 + e + 1)
                        wait(act, sm.st_pv, h0 + e - 1)
                        for j in range(TT):
                            op = fn(z[:, CO[j]:CO[j] + CW[j]], bank[4 * e + j][:, 0:CW[j]], ACT.Copy, scale=SCALE)
                        link(op)
                        link(fn(s[:, :], z[:, :], ACT.Abs))
                        link(fn(s[:, :], s[:, :], ACT.Exp, scale=-1.0))
                        fn(s[:, :], s[:, :], ACT.Ln, bias=1.0).then_inc(sm.st_log, 1)
                    for e in range(2):
                        act.wait_ge(sm.st_arg, h0 + e + 1)
                        fn(st_z[e][:, :], st_e[e][:, :], ACT.Exp).then_inc(sm.st_attn, 1)
                attention(dil_jobs(), AT["first"])

            def rope_tables():
                n.add(rt=1)
                for f in range(2):
                    act.wait_ge(sm.rope_ang, 2 * n["rt"] - 1 + f)
                    fn(rope_cs[:, 1 - f, :], rope_t[f][:, :], ACT.Sin).then_inc(sm.rope_ready, 1)

            def mlstm():
                act.wait_ge(sm.ml_pre, 1)
                link(fn(ml_r[0:4, 2, :], ml_r[0:4, 1, :], ACT.Abs))
                link(fn(ml_r[0:4, 2, :], ml_r[0:4, 2, :], ACT.Exp, scale=-1.0))
                fn(ml_r[0:4, 2, :], ml_r[0:4, 2, :], ACT.Ln, bias=1.0).then_inc(sm.ml_log, 1)
                act.wait_ge(sm.ml_pre, 2)
                fn(ml_r[0:4, 6, :], ml_r[0:4, 2, :], ACT.Exp, scale=-1.0).then_inc(sm.ml_rows, 1)
                act.wait_ge(sm.ml_w, 1)
                for hd in range(4):
                    act.wait_ge(sm.ml_spread, hd + 1)
                    fn(ml_x[:, :], bank[1][:, :], ACT.Copy)
                    act.wait_ge(sm.ml_diag, hd + 1)
                    for j in range(TT - 1):
                        fn(ml_e[:, CO[j] + P:CO[j] + CW[j]], bank[0][:, (j + 1) * P:S], ACT.Exp, scale=-1.0,
                           bias=ml_w[:, 4 * j + hd:4 * j + hd + 1])
                    for j in range(TT):
                        op = fn(ml_e[:, CO[j]:CO[j] + P], ml_d[:, j * P:(j + 1) * P], ACT.Exp, scale=-1.0,
                                bias=ml_w[:, 4 * j + hd:4 * j + hd + 1])
                    op.then_inc(sm.ml_exp, 1)
                for t in range(8, 16):
                    op = fn(proj[:, t, :], proj[:, t, :], ACT.Sigmoid)
                op.then_inc(sm.ml_sig, 1)
                act.wait_ge(sm.ml_out, 4)

            def hgrn_gates():
                mt = n["mt"]
                split_ahead(8)
                act.wait_ge(sm.hg_lb, 1)
                fn(lb_w[:, 0:32], lb_w[:, 0:32], ACT.Exp).then_inc(sm.hg_lbe, 1)
                split_ahead(8)
                for h0 in (0, 4):
                    for hd in range(h0, h0 + 4):
                        act.wait_ge(sm.lin_free, mt + 9 + hd)
                        fn(hg_k[:, hd, :], proj[:, 8 + hd, :], ACT.Sigmoid, scale=-1.0)
                        fn(proj[:, 8 + hd, :], proj[:, 8 + hd, :], ACT.Sigmoid).then_inc(sm.hg_sig, 1)
                    split_ahead(4 if h0 == 0 else 8)
                for hd in range(8):
                    act.wait_ge(sm.hg_dec, hd + 1)
                    fn(proj[:, 8 + hd, :], proj[:, 8 + hd, :], ACT.Ln).then_inc(sm.hg_log, 1)
                split_ahead(4)
                for t in range(16, 24):
                    act.wait_ge(sm.lin_free, mt + t + 1)
                    op = fn(proj[:, t, :], proj[:, t, :], ACT.Silu)
                op.then_inc(sm.hg_gate, 1)

            def hgrn():
                for e in range(72):
                    act.wait_ge(sm.hg_diff, e + 1)
                    fn(hg_d[e % 2][:, :], hg_d[e % 2][:, :], ACT.Exp).then_inc(sm.hg_e, 1)
                act.wait_ge(sm.hg_out, 8)

            def ffn():
                k, mt, m0, p0 = n["slot"], n["mt"], n["m"], n["part"]

                def up(q, i):
                    wait(act, sm.part_lo, p0 + q - 1 + 4 * i)
                    act.wait_ge(sm.slot_used, k + 2 * q + 1 + 8 * i)
                    fn(sil[q % 2], bank[(mt + 2 * q) % 4][:, :], ACT.Silu).then_inc(sm.sil_done, 1)
                    split(k + 2 * q + LEAD, i, 8)
                    split(k + 2 * q + 1 + LEAD, i, 8)
                    act.wait_ge(sm.lin_free, mt + 2 * q + 2 + 8 * i)
                    act.wait_ge(sm.const_loaded, 48)
                    fn(hid_hi[:, q + 4 * i, :], sil[q % 2], ACT.Copy).then_inc(sm.part_hi, 1)

                with act.Fori(0, 5) as i:
                    for q in range(4):
                        up(q, i)
                for q in range(20, 22):
                    up(q, 0)
                n.add(slot=2 * FT, mt=2 * FT, part=FT)
                split_ahead(3 * DT)
                n.add(mt=DT)

            sil = [lc[:, r * S:(r + 1) * S] for r in range(2)]
            act.wait_ge(sm.const_loaded, 48)
            fn(cond[:, :], col("c", 0, 8), ACT.Silu).then_inc(sm.cond_done, 1)
            for t in range(LEAD):
                split(t)
            normed = False
            for at, part in enumerate(parts):
                tiles, values = IN_PROJ[part]
                n.add(lc=2 if part == "first" else 1)
                if part == "first":
                    mean_squares(eps6, lambda c: None)
                split_input(normed, part != "first")
                if part == "first":
                    act.wait_ge(sm.gate_pre, 1)
                    fn(gates, gates, ACT.Sigmoid).then_inc(sm.gate_out, 1)
                if part == 2:
                    hgrn_gates()
                else:
                    split_ahead(len(tiles) + len(values))
                n.add(mt=len(tiles) + len(values))
                act.wait_ge(sm.lin_free, n["mt"])
                act.wait_ge(sm.layer_const_loaded, 16 * n["lc"])
                if part == "first":
                    first_mixer()
                    n.add(mt=4)
                    act.wait_ge(sm.att_out, n_groups("first"))
                    act.wait_ge(sm.mix_ready, 2)
                    n.add(mix=2)
                elif part == 0:
                    mlstm()
                elif part == 1:
                    rope_tables()
                    attention(swa_jobs(), AT["late"])
                    n.add(att_g=64)
                elif part == 2:
                    hgrn()
                else:
                    act.wait_ge(sm.lam_in, 1)
                    fn(lam_w[:, 2:4], lam_w[:, 0:2], ACT.Exp).then_inc(sm.lam_exp, 1)
                    rope_tables()
                    attention(diff_jobs(), AT["late"])
                n.add(out=n_groups(part))
                wait(act, sm.att_out, n["out"])
                if out_norms(part):
                    group_norms(out_norms(part), linear_follows=True)
                else:
                    for c in range(DT):
                        high(c, proj[:, c, :])
                    n.add(part=DT)
                if part == "first":
                    k, mt = n["slot"], n["mt"]

                    def whole(c):
                        split(k + c + LEAD)
                        act.wait_ge(sm.lin_free, mt + c + 1)

                    mean_squares(eps6, whole)
                    n.add(slot=DT, mt=DT)
                else:
                    split_ahead(DT)
                    n.add(mt=DT)
                    centred_squares()
                    n["ln_at"] = 2 * part
                split_input(part != "first", part != "first")
                ffn()
                normed = part != "first"
                if normed:
                    centred_squares()
                    n["ln_at"] = 2 * part + 1
            for c in range(DT if normed else 0):
                add_bias(c)

        @block.vector
        def _(dve):
            n = Counts()
            v = nc.vector

            def link(ins):
                n.add(dve_chain=1)
                ins.then_inc(sm.dve_chain, 1)
                dve.wait_ge(sm.dve_chain, n["dve_chain"])

            def low(c, src):
                n.add(part=1)
                dve.wait_ge(sm.part_hi, n["part"])
                v.tensor_tensor(h_lo[:, c, :], src, h_hi[:, c, :].bitcast(F32), ALU.subtract).then_inc(sm.part_lo, 1)

            def root():
                n.add(root=1)
                dve.wait_ge(sm.n_root, n["root"])
                link(v.reciprocal(rt[0][:, :], rt[0][:, :]))

            def rms_input(gain):
                root()
                for c in range(DT + 1):
                    if c < DT:
                        v.scalar_tensor_tensor(h_tmp[:, c, :], x[:, c, :], col(gain, c), rt[0][:, :], ALU.mult,
                                               ALU.mult).then_inc(sm.h_ready, 1)
                    if c:
                        low(c - 1, h_tmp[:, c - 1, :])

            def normed_tile(c, gain_at):
                v.scalar_tensor_tensor(x[:, c, :], x[:, c, :], col("ln_g", gain_at * 8 + c), rt[0][:, :], ALU.mult,
                                       ALU.mult).then_inc(sm.ln_y, 1)

            def modulated_input(layer, sub, gain_at):
                normed = gain_at is not None
                for c in range(DT + 2):
                    if normed and c < DT:
                        normed_tile(c, gain_at)
                    if 1 <= c <= DT:
                        if normed:
                            dve.wait_ge(sm.ln_x, n["lx"] * DT + c)
                        v.tensor_scalar(h_tmp[:, c - 1, :], x[:, c - 1, :], mod_col(layer, sub, ONE_SCALE, c - 1),
                                        mod_col(layer, sub, SHIFT, c - 1), ALU.mult, ALU.add).then_inc(sm.h_ready, 1)
                    if c >= 2:
                        low(c - 2, h_tmp[:, c - 2, :])
                n.add(lx=1 if normed else 0)

            def centre():
                n.add(ln=DT)
                dve.wait_ge(sm.ln_mean, n["ln"])
                for c in range(DT):
                    v.scalar_tensor_tensor(x[:, c, :], bank[5][:, :], -1.0 / D, x[:, c, :], ALU.mult,
                                           ALU.add).then_inc(sm.ln_centred, 1)
                root()

            def tile_done(slots):
                n.add(slot=slots)
                dve.wait_ge(sm.slot_used, n["slot"])
                n.add(mt=1)
                return bank[(n["mt"] - 1) % 4]

            def keep(tiles, values, between=lambda t: None):
                for t in range(tiles):
                    v.tensor_copy(proj[:, t, :], tile_done(1)[:, :]).then_inc(sm.lin_free, 1)
                    between(t)
                if len(values) == 1:
                    v.tensor_copy(values[0], tile_done(1)[:, :].rearrange("p (t d) -> p t d", t=TT)).then_inc(sm.lin_free, 1)
                else:
                    for t, out in enumerate(values):
                        v.tensor_copy(out, tile_done(0 if t % TT else TT)[:, :]).then_inc(sm.lin_free, 1)
                        between(tiles + t)
                dve.wait_ge(sm.lin_free, n["mt"])

            def add_residual(slots, layer=None, sub=None):
                if layer is not None:
                    n.add(xs=DT)
                    dve.wait_ge(sm.x_scaled, n["xs"])
                for m in range(DT):
                    b = tile_done(slots)
                    if layer is None:
                        v.tensor_tensor(x[:, m, :], b[:, :], x[:, m, :], ALU.add).then_inc(sm.lin_free, 1)
                    else:
                        v.scalar_tensor_tensor(x[:, m, :], b[:, :], mod_col(layer, sub, ONE_GATE, m), x[:, m, :],
                                               ALU.mult, ALU.add).then_inc(sm.lin_free, 1)
                dve.wait_ge(sm.lin_free, n["mt"])

            def group_norms(items, linear_follows=False):
                done = 0
                for t in range(len(items) + 1):
                    if t < len(items):
                        it = items[t]
                        rows = it["src"][0].shape[0]
                        r = rt[t % 2][0:rows, :]
                        dve.wait_ge(sm.g_root, n["gn"] + t + 1)
                        link(v.reciprocal(r, r))
                        for u, src in enumerate(it["src"]):
                            for out in it["out"][u]:
                                op = v.scalar_tensor_tensor(out, src, it["gain"][u], r, ALU.mult, ALU.mult)
                            if it["mul"]:
                                link(op)
                                op = v.tensor_tensor(out, out, it["mul"][u], ALU.mult)
                        op.then_inc(sm.g_out, 1)
                    if t and linear_follows:
                        for _ in items[t - 1]["src"]:
                            low(done, proj[:, done, :])
                            done += 1
                n.add(gn=len(items))

            def attention(jobs, bufs):
                a, g = n["att"], n["att_g"]
                for step in range(len(jobs) + 4):
                    if step < len(jobs):
                        j, it = step, jobs[step]
                        s, w = bufs["s"][j % 2], it["w"]
                        dve.wait_ge(sm.att_scores, a + j + 1)
                        wait(dve, sm.att_exp, a + j - 1)
                        op = v.scalar_tensor_tensor(s[:, 0:w], bank[j % 2][:, 0:w], SCALE, it["bias"], ALU.mult, ALU.add)
                        if it["sink"] is not None:
                            op = v.tensor_copy(s[:, w:w + 1], it["sink"])
                            w += 1
                        link(op)
                        v.tensor_reduce(att_max[j % 2], s[:, 0:w], AX_X, ALU.max, negate=True).then_inc(sm.att_ready, 1)
                    if 1 <= step <= len(jobs):
                        j, it = step - 1, jobs[step - 1]
                        p, w, inv = bufs["p"][j % 2], it["w"], att_inv[j % 2]
                        dve.wait_ge(sm.att_exp, a + j + 1)
                        link(v.reciprocal(inv, att_sum[j % 2]))
                        if it["gate"] is not None:
                            link(v.tensor_tensor(inv, inv, it["gate"], ALU.mult))
                        if it["vis"] is not None:
                            op = v.scalar_tensor_tensor(p[:, 0:w], p[:, 0:w], inv, it["vis"], ALU.mult, ALU.mult)
                        else:
                            op = v.tensor_scalar(p[:, 0:w], p[:, 0:w], inv, None, ALU.mult)
                        op.then_inc(sm.att_normed, 1)
                    if step >= 4 and jobs[step - 4]["last"]:
                        j, it = step - 4, jobs[step - 4]
                        g += 1
                        dve.wait_ge(sm.att_pv, a + j + 1)
                        rows = slice(it["row"], it["row"] + it["dv"])
                        v.tensor_copy(it["dest"], bank[4 + g % 4][rows, 0:P]).then_inc(sm.att_out, 1)
                n.add(att=len(jobs), att_g=sum(it["last"] for it in jobs))

            def first_mixer():
                link(v.memset(blk[:, :, :, :], 0.0))
                pe_cols = col("pe", 0, 32).rearrange("p (a c) -> p a c", a=2)
                for kv in range(2):
                    rows = slice(HD * kv, HD * kv + HD)
                    tok = proj[rows, 8, :].rearrange("p (n r) -> p r n", r=CMP_STRIDE)
                    for par in range(2):
                        for c1 in range(2):
                            op = v.tensor_tensor(blk[HD * par:HD * par + HD, kv, 8 * c1:8 * c1 + 8, 0:NCMP],
                                                 tok[:, par::2, c1:c1 + NCMP],
                                                 pe_cols[rows, par, 8 * c1:8 * c1 + 8].unsqueeze(2).to_broadcast([HD, 8, NCMP]),
                                                 ALU.add)
                            if (kv, par, c1) != (1, 1, 1):
                                link(op)
                op.then_inc(sm.blk_ready, 2)
                for kv in range(2):
                    dve.wait_ge(sm.blk_hi_done, kv + 1)
                    v.tensor_tensor(blk_lo[:, kv, :, :], blk[:, kv, :, :], blk_hi[:, kv, :, :].bitcast(F32),
                                    ALU.subtract).then_inc(sm.blk_lo_done, 1)
                for kv in range(2):
                    for m in range(2):
                        v.tensor_copy(hid_pre[:, 2 * kv + m, :], tile_done(2)[:, 0:32]).then_inc(sm.lin_free, 1)
                dve.wait_ge(sm.cmp_mm, 1)
                v.tensor_copy(vcmp[0:NCMP, :], bank[5][0:NCMP, 0:HD])
                dve.wait_ge(sm.cmp_root, 1)
                link(v.reciprocal(hid_pre[0:HD, 1, :], hid_pre[0:HD, 1, :]))
                for b in (HD, 0):
                    v.scalar_tensor_tensor(kcmp[b:b + HD, :], bank[4][0:HD, 0:32], col("g_k_cmp")[0:HD, :],
                                           hid_pre[0:HD, 1, :], ALU.mult, ALU.mult)
                dve.wait_ge(sm.v_turned, 1)
                v.tensor_copy(v_slc[:, :, :], bank[7][:, 0:256].rearrange("p (t d) -> p t d", t=TT))
                v.tensor_copy(v_win[:, :, :], bank[7][:, 256:512].rearrange("p (t d) -> p t d", t=TT)).then_inc(sm.v_out, 1)
                group_norms(first_norms())
                for hd in range(NSA_HEADS):
                    v.scalar_tensor_tensor(bias[:, hd, :], dist, -SLOPES_A[hd], causal, ALU.mult, ALU.add)
                    op = v.scalar_tensor_tensor(cmp_bias[:, hd, :], lc[:, 0:124], -SLOPES_A[hd], lc[:, 248:372],
                                                ALU.mult, ALU.add)
                dve.wait_ge(sm.gate_out, 1)
                link(op)
                for t in range(2):
                    u, y, w = proj[:, 13 + t, :], proj[:, 11 + t, :], [col("conv_w", 3 * t + i) for i in range(3)]
                    link(v.tensor_tensor(u, u, y, ALU.mult))
                    link(v.tensor_scalar(y, u, w[2], None, ALU.mult))
                    link(v.scalar_tensor_tensor(y[:, 1:S], u[:, 0:S - 1], w[1], y[:, 1:S], ALU.mult, ALU.add))
                    link(v.scalar_tensor_tensor(y[:, 2:S], u[:, 0:S - 2], w[0], y[:, 2:S], ALU.mult, ALU.add))
                    op = v.tensor_tensor(proj[:, 2 + t, :], y, proj[:, 2 + t, :], ALU.mult)
                op.then_inc(sm.mix_ready, 1)
                attention(nsa_jobs(), AT["first"])
                stick_breaking()
                for hd in range(4):
                    op = v.scalar_tensor_tensor(bias[:, hd, :], dist, -SLOPES_D[hd], logmult, ALU.mult, ALU.add)
                op.then_inc(sm.mix_ready, 1)
                dve.wait_ge(sm.mix_ready, 2)
                attention(dil_jobs(), AT["first"])

            def stick_breaking():
                strict, shut = lc[:, 512:640], lc[:, 640:768]
                for h0 in (0, 2):
                    for e in range(2):
                        dve.wait_ge(sm.st_log, h0 + e + 1)
                        link(v.scalar_tensor_tensor(st_l[e][:, :], st_z[e][:, :], 0.0, st_e[e][:, :], ALU.max, ALU.add))
                        for j in range(TT):
                            d = st_l[e][:, CO[j]:CO[j] + P]
                            op = v.tensor_tensor(d, d, strict, ALU.mult)
                        op.then_inc(sm.st_keep, 1)
                    for e in range(2):
                        dve.wait_ge(sm.st_suffix, h0 + e + 1)
                        for j in range(TT):
                            d = slice(CO[j], CO[j] + CW[j])
                            op = v.tensor_tensor(st_e[e][:, d], st_z[e][:, d], bank[4 * e + j][:, 0:CW[j]], ALU.subtract)
                        link(op)
                        for j in range(TT):
                            d = st_e[e][:, CO[j]:CO[j] + P]
                            op = v.tensor_tensor(d, d, shut, ALU.add)
                        op.then_inc(sm.st_arg, 1)
                    for e in range(2):
                        hd, b = h0 + e, HD * e
                        dve.wait_ge(sm.st_pv, hd + 1)
                        v.tensor_copy(half(4 + hd // 2, hd), bank[4 * e][b:b + HD, :]).then_inc(sm.st_out, 1)
                dve.wait_ge(sm.st_out, 4)

            def rope_tables():
                n.add(rt=1, lcw=0)
                ang, y = rope_t[2], rope_t[3]
                dve.wait_ge(sm.pos_loaded, 16 * n["rt"])
                link(v.tensor_copy(y[:, :], rope_i[:, :]))
                link(v.tensor_scalar(ang[:, :], y[:, :], lc[:, 128:129], None, ALU.mult))
                turns = [6.28125, 0.0019350051879882812, 3.0200114160515973e-07]
                for f, shift in enumerate((0.0, 0.25)):
                    r = rope_t[f]
                    link(v.tensor_scalar(y[:, :], ang[:, :], 1 / (2 * np.pi), shift, ALU.mult, ALU.add))
                    link(v.tensor_scalar(y[:, :], y[:, :], 12582912.0, None, ALU.add))
                    link(v.tensor_scalar(y[:, :], y[:, :], 12582912.0, None, ALU.subtract))
                    link(v.scalar_tensor_tensor(r[:, :], y[:, :], -turns[0], ang[:, :], ALU.mult, ALU.add))
                    link(v.scalar_tensor_tensor(r[:, :], y[:, :], -turns[1], r[:, :], ALU.mult, ALU.add))
                    link(v.scalar_tensor_tensor(r[:, :], y[:, :], -turns[2], r[:, :], ALU.mult, ALU.add))
                    if f:
                        link(v.tensor_scalar(r[:, :], r[:, :], float(np.pi / 2), None, ALU.add))
                    v.tensor_scalar(r[:, :], r[:, :], 3.1415925, -3.1415925, ALU.min, ALU.max).then_inc(sm.rope_ang, 1)

            def rope(tiles):
                dve.wait_ge(sm.rope_ready, 2 * n["rt"])
                for t in tiles:
                    n.add(rope=1)
                    a = rope_t[n["rope"] % 2]
                    dve.wait_ge(sm.rope_mm, n["rope"])
                    v.tensor_tensor(a[:, :], bank[4 + (n["rope"] - 1) % 2][:, :], rope_cs[:, 1, :], ALU.mult)
                    link(v.tensor_tensor(proj[:, t, :], proj[:, t, :], rope_cs[:, 0, :], ALU.mult))
                    v.tensor_tensor(proj[:, t, :], proj[:, t, :], a[:, :], ALU.add).then_inc(sm.rope_out, 1)
                dve.wait_ge(sm.rope_out, n["rope"])

            def mlstm():
                b = col("mlstm_b", 0, 2)
                dve.wait_ge(sm.ml_gate, 1)
                v.tensor_scalar(ml_r[0:4, 0, :], bank[6][0:4, :], b[0:4, 0:1], None, ALU.add)
                v.tensor_scalar(ml_r[0:4, 1, :], bank[7][0:4, :], b[0:4, 1:2], None, ALU.add).then_inc(sm.ml_pre, 1)
                link(v.memset(ml_r[0:4, 7, :], 1.0))
                dve.wait_ge(sm.ml_log, 1)
                link(v.scalar_tensor_tensor(ml_r[0:4, 3, :], ml_r[0:4, 1, :], 0.0, ml_r[0:4, 2, :], ALU.min, ALU.subtract))
                link(v.tensor_tensor_scan(ml_r[0:4, 1, :], ml_r[0:4, 7, :], ml_r[0:4, 3, :], 0.0, ALU.mult, ALU.add))
                link(v.tensor_tensor(ml_r[0:4, 4, :], ml_r[0:4, 0, :], ml_r[0:4, 1, :], ALU.subtract))
                link(v.tensor_tensor_scan(ml_r[0:4, 5, :], ml_r[0:4, 4, :], ml_r[0:4, 4, :], 0.0, ALU.max, ALU.max))
                v.tensor_tensor(ml_r[0:4, 2, :], ml_r[0:4, 1, :], ml_r[0:4, 5, :], ALU.add).then_inc(sm.ml_pre, 1)
                dve.wait_ge(sm.ml_turn, 1)
                v.tensor_copy(ml_w, bank[0][:, 0:16]).then_inc(sm.ml_w, 1)
                for hd in range(4):
                    dve.wait_ge(sm.ml_spread, hd + 1)
                    v.tensor_tensor(ml_d[:, :].rearrange("p (t q) -> p t q", t=TT),
                                    bank[0][:, :].rearrange("p (t q) -> p t q", t=TT),
                                    lc[:, 512:640].unsqueeze(1).to_broadcast([P, TT, P]), ALU.add).then_inc(sm.ml_diag, 1)
                    dve.wait_ge(sm.ml_exp, hd + 1)
                    for j in range(TT):
                        d = slice(CO[j], CO[j] + CW[j])
                        op = v.scalar_tensor_tensor(ml_a[:, d], bank[2 + j][:, 0:CW[j]], P ** -0.5, ml_e[:, d], ALU.mult,
                                                    ALU.mult)
                    op.then_inc(sm.ml_a, 1)
                    dve.wait_ge(sm.ml_den, hd + 1)
                    link(v.scalar_tensor_tensor(ml_x[:, :], bank[6][:, :], -1.0, ml_x[:, :], ALU.mult, ALU.max))
                    link(v.scalar_tensor_tensor(ml_d[:, :], bank[6][:, :], 1.0, ml_x[:, :], ALU.mult, ALU.max))
                    link(v.reciprocal(ml_d[:, :], ml_d[:, :]))
                    dve.wait_ge(sm.ml_num, hd + 1)
                    for e in range(2):
                        op = v.tensor_tensor(proj[:, 2 * hd + e, :], bank[7 if e else 0][:, :], ml_d[:, :], ALU.mult)
                    op.then_inc(sm.ml_out, 1)
                dve.wait_ge(sm.ml_out, 4)
                dve.wait_ge(sm.ml_sig, 1)

            def hgrn_gates(t):
                low = col("lower", 0, 32).rearrange("p (l c) -> p c l", l=4)
                top, e = lb_w[:, 32:40], lb_w[:, 0:32]
                if t == 3:
                    link(v.tensor_reduce(top, low, AX_X, ALU.max))
                    v.tensor_tensor(e.rearrange("p (l c) -> p l c", l=4),
                                    col("lower", 0, 32).rearrange("p (l c) -> p l c", l=4),
                                    top.unsqueeze(1).to_broadcast([P, 4, 8]), ALU.subtract).then_inc(sm.hg_lb, 1)
                elif t == 12:
                    v.memset(hg_one[:, :], 1.0)
                    dve.wait_ge(sm.hg_lbe, 1)
                    link(v.tensor_reduce(top, e.rearrange("p (l c) -> p c l", l=4), AX_X, ALU.add))
                    v.tensor_tensor(lb, e[:, 8:16], e[:, 16:24], ALU.add)
                    v.tensor_tensor(one_lb, e[:, 0:8], e[:, 24:32], ALU.add)
                    link(v.reciprocal(top, top))
                    v.tensor_tensor(lb, lb, top, ALU.mult)
                    link(v.tensor_tensor(one_lb, one_lb, top, ALU.mult))
                elif t in (19, 23):
                    for hd in range(t - 19, t - 15):
                        f = proj[:, 8 + hd, :]
                        dve.wait_ge(sm.hg_sig, hd + 1)
                        link(v.tensor_scalar(f, f, one_lb[:, hd:hd + 1], lb[:, hd:hd + 1], ALU.mult, ALU.add))
                        v.tensor_scalar(hg_k[:, hd, :], hg_k[:, hd, :], one_lb[:, hd:hd + 1], None, ALU.mult)
                        v.tensor_scalar(f, f, tiny, None, ALU.max).then_inc(sm.hg_dec, 1)
                elif t == 27:
                    for hd in range(8):
                        f = proj[:, 8 + hd, :]
                        dve.wait_ge(sm.hg_log, hd + 1)
                        v.tensor_tensor_scan(f, hg_one[:, :], f, 0.0, ALU.mult, ALU.add)

            def hgrn():
                for r in range(2):
                    op = v.memset(hg_p[r][:, :, :], 0.0)
                link(op)

                def decays(hd, at):
                    b, i = LV[at], hd * 9 + at
                    early, late = halves(proj[:, 8 + hd, :], b)
                    mid = early[:, :, b - 1:b].to_broadcast([P, S // (2 * b), b])
                    d = halves(hg_d[i % 2][:, :], b)
                    wait(dve, sm.hg_qk, hd * 10 + (at - 1 if at else -2))
                    v.tensor_tensor(d[0], mid, early, ALU.subtract)
                    v.tensor_tensor(d[1], late, mid, ALU.subtract).then_inc(sm.hg_diff, 1)

                def put(hd, at):
                    m, b, weights = hd * 10 + at, (LV + [0])[at], hg_p[hd % 2]
                    dve.wait_ge(sm.hg_mm, m + 1)
                    wait(dve, sm.hg_put, m)
                    if b == 256:
                        wait(dve, sm.hg_pv, hd - 1)
                        v.tensor_copy(weights[:, 0, 256:512], bank[0][:, 0:256])
                        op = v.tensor_copy(weights[:, 1, 128:384], bank[1][:, 0:256])
                    elif b == 128:
                        v.tensor_copy(weights[:, 0, 128:256], bank[2][:, 0:128])
                        op = v.tensor_copy(weights[:, 2, 128:256], bank[2][:, 128:256])
                    else:
                        mask = lc[:, (at - 2) * P:(at - 1) * P] if b else ident
                        op = v.copy_predicated(weights[:, :, 0:P],
                                               mask.bitcast(I32).unsqueeze(1).to_broadcast([P, TT, P]),
                                               bank[4 + m % 2][:, :].rearrange("p (t q) -> p t q", t=TT))
                    op.then_inc(sm.hg_put, 1)

                def output(hd):
                    dve.wait_ge(sm.hg_pv, hd + 1)
                    v.tensor_copy(proj[:, hd, :], bank[6 + hd % 2][:, :]).then_inc(sm.hg_out, 1)

                decays(0, 0)
                for hd in range(8):
                    for at in range(9):
                        if at < 8:
                            decays(hd, at + 1)
                        elif hd < 7:
                            decays(hd + 1, 0)
                        if at:
                            put(hd, at - 1)
                        elif hd:
                            put(hd - 1, 8)
                            put(hd - 1, 9)
                        if at == 4 and hd:
                            output(hd - 1)
                put(7, 8)
                put(7, 9)
                output(7)
                dve.wait_ge(sm.hg_out, 8)
                dve.wait_ge(sm.hg_gate, 1)

            def lambdas():
                a = col("diff_lambda", 0, 256).rearrange("p (l d) -> p l d", l=4)
                prod = small[:, 0:128].rearrange("p (l d) -> p l d", l=2)
                link(v.tensor_tensor(prod, a[:, 0:4:2, :], a[:, 1:4:2, :], ALU.mult))
                v.tensor_reduce(lam_w[:, 0:2], prod, AX_X, ALU.add).then_inc(sm.lam_in, 1)
                v.tensor_scalar(lam_w[:, 5:6], col("diff_norm"), 1.0 - LAM_INIT[3], None, ALU.mult)
                dve.wait_ge(sm.lam_exp, 1)
                link(v.tensor_tensor(lam, lam_w[:, 3:4], lam_w[:, 2:3], ALU.subtract))
                link(v.tensor_scalar(lam, lam, -LAM_INIT[3], None, ALU.add))

            def ffn(ahead, layer):
                k, mt, p0, s0, a0, cg = n["slot"], n["mt"], n["part"], n["sil"], n["ada"], n["cg"]

                def ada_slot(a, kc, i):
                    dve.wait_ge(ada_loaded[a % ADA_RING], 16 * (a // ADA_RING + 1) + 64 * i)
                    if kc == 0:
                        op = v.tensor_scalar(ada_acc[:, :], ada_raw[a % ADA_RING][:, :], cond[:, 0:1], None, ALU.mult)
                    else:
                        dve.wait_ge(sm.ada_used, a + 8 * i)
                        op = v.scalar_tensor_tensor(ada_acc[:, :], ada_raw[a % ADA_RING][:, :], cond[:, kc:kc + 1],
                                                    ada_acc[:, :], ALU.mult, ALU.add)
                    op.then_inc(sm.ada_used, 1)

                def ada_out(g, i):
                    dve.wait_ge(sm.ada_sum, cg + g + 1 + i)
                    v.tensor_tensor(mod[ahead % 2][:, bass.ds(8 * g + 8 * i, 8)], bank[7][:, 0:8],
                                    co[:, bass.ds(COLS["ada_b"][0] + 48 * ahead + 8 * g + 8 * i, 8)],
                                    ALU.add).then_inc(sm.ada_mod, 1)

                def up(q, i):
                    dve.wait_ge(sm.sil_done, s0 + q + 1 + 4 * i)
                    dve.wait_ge(sm.slot_used, k + 2 * q + 2 + 8 * i)
                    v.tensor_tensor(sil[q % 2], bank[(mt + 2 * q + 1) % 4][:, :], sil[q % 2],
                                    ALU.mult).then_inc(sm.lin_free, 2)
                    dve.wait_ge(sm.part_hi, p0 + q + 1 + 4 * i)
                    v.tensor_tensor(hid_lo[:, q + 4 * i, :], sil[q % 2], hid_hi[:, q + 4 * i, :].bitcast(F32),
                                    ALU.subtract).then_inc(sm.part_lo, 1)

                if ahead is not None and a0 == 0:
                    dve.wait_ge(sm.cond_done, 1)
                with dve.Fori(0, 5) as i:
                    for q in range(4):
                        if ahead is not None:
                            ada_slot(a0 + 2 * q, 2 * q, i)
                            ada_slot(a0 + 2 * q + 1, 2 * q + 1, i)
                        up(q, i)
                    if ahead is not None:
                        ada_out(0, i)
                for q in range(20, 22):
                    if ahead is not None:
                        for kc in range(4 * (q - 20), 4 * (q - 20) + 4):
                            ada_slot(a0 + 40 + kc, kc, 0)
                    up(q, 0)
                if ahead is not None:
                    ada_out(5, 0)
                    n.add(ada=48, cg=6)
                    dve.wait_ge(sm.ada_mod, n["cg"])
                    more = mod[ahead % 2][:, :].rearrange("p (s k) -> p s k", s=2)[:, :, 8:24]
                    link(v.tensor_scalar(more, more, 1.0, None, ALU.add))
                n.add(slot=2 * FT, mt=2 * FT, part=FT, sil=FT)
                add_residual(3, layer, 1)

            sil = [lc[:, r * S:(r + 1) * S] for r in range(2)]
            dve.wait_ge(sm.const_loaded, 48)
            for at, part in enumerate(parts):
                tiles, values = IN_PROJ[part]
                layer = None if part == "first" else part
                n.add(lc=2 if part == "first" else 1)
                if part == "first":
                    rms_input("g_mix")
                    dve.wait_ge(sm.gate_in, 1)
                    v.tensor_tensor(gates.rearrange("p (t g) -> p t g", t=TT),
                                    bank[6][:, 0:48].rearrange("p (t g) -> p t g", t=TT),
                                    col("b_gate", 0, 12).unsqueeze(1).to_broadcast([P, TT, 12]),
                                    ALU.add).then_inc(sm.gate_pre, 1)
                    keep(len(tiles), [first_v[:, t, :] for t in range(TT)])
                else:
                    modulated_input(layer, 0, last_gain)
                    vals = {0: ml_v, 1: swa_v, 2: hg_v, 3: df_v}[part]
                    keep(len(tiles), [swa_v[:, :, :]] if part == 1 else
                         [vals[:, t, g * S:(g + 1) * S] for g in range(D // S) for t in range(TT)],
                         hgrn_gates if part == 2 else lambda t: None)
                dve.wait_ge(sm.layer_const_loaded, 16 * n["lc"])
                if part == "first":
                    first_mixer()
                elif part == 0:
                    mlstm()
                elif part == 1:
                    rope_tables()
                    rope(range(9))
                    for g in range(2):
                        for b in (0, HD):
                            op = v.tensor_copy(swa_k[b:b + HD, g, :], proj[HD * g:HD * g + HD, 8, :])
                    op.then_inc(sm.mix_ready, 1)
                    attention(swa_jobs(), AT["late"])
                elif part == 2:
                    hgrn()
                else:
                    lambdas()
                    rope_tables()
                    rope(range(16))
                    v.tensor_copy(lam_w[:, 4:5], eps6).then_inc(sm.mix_ready, 1)
                    attention(diff_jobs(), AT["late"])
                wait(dve, sm.att_out, n["att_g"])
                if out_norms(part):
                    group_norms(out_norms(part), linear_follows=True)
                else:
                    for c in range(DT):
                        low(c, proj[:, c, :])
                add_residual(1, layer, 0)
                if part == "first":
                    rms_input("g_ffn")
                else:
                    centre()
                    modulated_input(layer, 1, 2 * part)
                ffn(parts[at + 1] if at + 1 < len(parts) else None, layer)
                last_gain = None
                if part != "first":
                    centre()
                    last_gain = 2 * part + 1
            for c in range(DT if last_gain is not None else 0):
                normed_tile(c, last_gain)


def slot_rows(w, columns):
    rows = w.shape[0] // P
    slots = []
    for c in columns:
        t = w[:, c:c + P].reshape(rows, P, P).transpose(1, 0, 2)
        for r in range(0, rows, 8):
            s = np.zeros((P, 8, P), w.dtype)
            s[:, 0:min(8, rows - r), :] = t[:, r:r + 8, :]
            slots.append(s.reshape(P, SLOT))
    return slots


def weight_stream(a, parts):
    out = []
    every = [j * P for j in range(DT)]
    for part in parts:
        if part == "first":
            w_in, w_out, gate, up, down = (a[k][0] for k in ("w_in", "w_out", "w_gate", "w_up", "w_down"))
        else:
            name = ("mlstm", "swa", "hgrn", "diff")[part]
            w_in, w_out = a[f"{name}_w_in_2"][0], a[f"{name}_w_out_2"][0]
            both, down = a["ffn_w_in_2"][part], a["ffn_w_out_2"][part]
            gate, up = both[:, :FF], both[:, FF:]
        tiles, values = IN_PROJ[part]
        out += slot_rows(w_in, tiles)
        if len(values) < TT:
            out += slot_rows(w_in, values)
        else:
            for g in range(0, len(values), TT):
                w = np.concatenate([w_in[:, c:c + P] for c in values[g:g + TT]], 1)
                out += list(w.reshape(TT, 2, P, S).transpose(0, 2, 1, 3).reshape(TT, P, SLOT))
        if part == "first":
            for w in ("w1_k_cmp", "w1_v_cmp"):
                out += slot_rows(a[w][0], [0, P])
        out += slot_rows(w_out, every)
        hidden = [j * P for j in range(FT)]
        for g, u in zip(slot_rows(gate, hidden), slot_rows(up, hidden)):
            out += [g, u]
        out += slot_rows(down, every)
    return np.stack(out)


def ada_stream(w, parts):
    layers = [p for p in parts[1:]]
    if not layers:
        return np.zeros((1, P, SLOT), np.float32)
    return np.stack([w[p, s, c * P:(c + 1) * P, g * SLOT:(g + 1) * SLOT]
                     for p in layers for s in range(2) for g in range(3) for c in range(DT)])


def column_pack(a):
    def tiles(v):
        return v.reshape(-1, P).T

    def twice(v):
        return np.concatenate([v, v])[:, None]

    def spread(v):
        return np.broadcast_to(v.reshape(1, -1), (P, v.size))

    def by_tile(w):
        return w.reshape(-1, P, w.shape[1]).transpose(1, 0, 2).reshape(P, -1)

    pe = np.concatenate([a[k][0].reshape(16, 2, HD).transpose(2, 1, 0).reshape(HD, 32) for k in ("pe_k_cmp", "pe_v_cmp")])
    mb = np.zeros((P, 2), np.float32)
    mb[0:4, :] = a["mlstm_b_gate_2"][0].reshape(2, 4).T
    pack = {
        "g_mix": tiles(a["g_mix"][0]), "g_ffn": tiles(a["g_ffn"][0]), "g_out": tiles(a["g_out"][0]),
        "g_q_nsa": twice(a["g_q_nsa"][0]), "g_k_slc": twice(a["g_k_slc"][0]), "g_k_win": twice(a["g_k_win"][0]),
        "g_k_cmp": twice(a["g_k_cmp"][0]), "g_q_dil": twice(a["g_q_dil"][0]), "g_k_dil": twice(a["g_k_dil"][0]),
        "conv_w": a["conv_w"][0].T.reshape(2, P, 3).transpose(1, 0, 2).reshape(P, 6), "pe": pe,
        "gate_w": by_tile(a["w_in"][0][:, C_GT:C_GT + 12]), "b_gate": spread(a["b_gate"][0]),
        "w2": np.concatenate([by_tile(a["w2_k_cmp"][0]), by_tile(a["w2_v_cmp"][0])], 1),
        "c": tiles(a["c_2"]), "ada_b": tiles(a["ada_b_2"]), "ln_g": tiles(a["ln_g_2"]), "ln_b": tiles(a["ln_b_2"]),
        "mlstm_gw": by_tile(a["mlstm_w_in_2"][0][:, 3072:3080]), "mlstm_b": mb,
        "mlstm_norm": tiles(a["mlstm_norm_2"][0]), "sinks": spread(a["swa_sinks_2"][0]),
        "lower": tiles(a["hgrn_lower_bounds_2"]), "hgrn_norm": tiles(a["hgrn_norm_2"][0]),
        "diff_norm": a["diff_norm_2"][0][:, None], "diff_lambda": spread(a["diff_lambda_2"][0]),
    }
    return np.ascontiguousarray(np.concatenate([pack[name] for name in COLS], 1))


def kernel(**inputs):
    import concourse.bacc as bacc
    from concourse.bass_utils import run_bass_kernel_spmd

    a = {k: np.asarray(v) for k, v in inputs.items()}
    kept, big, layer = constants()
    arrays = {
        "x_t": np.ascontiguousarray(a["x"][0].T.reshape(DT, P, S).transpose(1, 0, 2)),
        "weights": weight_stream(a, PARTS), "ada": ada_stream(a["ada_w_2"], PARTS), "columns": column_pack(a),
        "kept_const": kept, "big_const": big, "layer_const": layer,
        "positions": np.ascontiguousarray(np.broadcast_to(a["positions_2"], (P, S))),
    }
    nc = bacc.Bacc("TRN2", target_bir_lowering=False, num_devices=1)
    args = [nc.dram_tensor(name, v.shape, mybir.dt.from_np(v.dtype), kind="ExternalInput").ap()
            for name, v in arrays.items()]
    out = nc.dram_tensor("y_t", (P, DT, S), F32, kind="ExternalOutput").ap()
    program(nc, *args, out, PARTS)
    r = run_bass_kernel_spmd(nc, [arrays], core_ids=[0])
    y = r.results[0]["y_t"]
    return np.ascontiguousarray(y.transpose(1, 0, 2).reshape(D, S).T)[None]
```

```python
from collections import namedtuple
from contextlib import ExitStack, contextmanager

import numpy as np

import concourse.bass as bass
import concourse.mybir as mybir

F32 = mybir.dt.float32
F32R = mybir.dt.float32r
I32 = mybir.dt.int32
ACT = mybir.ActivationFunctionType
ALU = mybir.AluOpType
AX_X = mybir.AxisListType.X

P = 128
S = 512
D = 1024
DT = D // P
HD = 64
FF = 2816
FT = FF // P
TT = S // P
SLOT = 8 * P
RING = 4
LEAD = 4
EARLY = 3
ADA_RING = 2
CMP_LEN, CMP_STRIDE = 32, 16
NCMP = (S - CMP_LEN) // CMP_STRIDE + 1
NSA_HEADS = 4
NEG = -1e30
BIG = 3e38
ALPHA = 8 ** 0.25
LAYERS = 4
PARTS = ["first", 0, 1, 2, 3]
LAM_INIT = [0.8 - 0.6 * float(np.exp(-0.3 * i)) for i in range(LAYERS)]
ROPE_THETA = 500000.0
SCALE = HD ** -0.5
SLOPES = [2.0 ** -(i + 1) for i in range(8)]
SLOPES_A, SLOPES_D = SLOPES[0::2], SLOPES[1::2]

W_IN_COLS = np.cumsum([0, 256, 64, 64, 64, 64, 64, 64, 12, 256, 256, 256, 256, 256, 256, 256, 256, 256])
(C_QA, C_KC, C_VC, C_KS, C_VS, C_KW, C_VW, C_GT, C_CB, C_CC, C_CU,
 C_QC, C_KCC, C_VCC, C_QD, C_KD, C_VD) = (int(v) for v in W_IN_COLS[:-1])
FIRST_TILES = ([C_QA, C_QA + P, C_CB, C_CB + P, C_QC, C_QC + P, C_QD, C_QD + P, C_KC, C_KS, C_KW,
                C_CC, C_CC + P, C_CU, C_CU + P, C_KCC, C_KCC + P, C_KD, C_KD + P])
FIRST_VALUES = [C_VCC, C_VCC + P, C_VD, C_VD + P]
MLSTM_TILES = [c for h in range(4) for c in (h * P, 512 + h * P)] + [2048 + j * P for j in range(8)]
MLSTM_VALUES = [1024 + j * P for j in range(8)]
SWA_TILES = [j * P for j in range(9)]
SWA_VALUES = [9 * P]
HGRN_TILES = [j * P for j in range(16)] + [3072 + j * P for j in range(8)]
HGRN_VALUES = [2048 + j * P for j in range(8)]
DIFF_TILES = [j * P for j in range(16)]
DIFF_VALUES = [2048 + j * P for j in range(8)]
VALUES_AND_BLOCKS = "vbbvbbvbbvbb"
IN_PROJ = {"first": (FIRST_TILES, FIRST_VALUES), 0: (MLSTM_TILES, MLSTM_VALUES), 1: (SWA_TILES, SWA_VALUES),
           2: (HGRN_TILES, HGRN_VALUES), 3: (DIFF_TILES, DIFF_VALUES)}

COLS = {}


def _columns():
    at = 0
    for name, width in [("g_mix", 8), ("g_ffn", 8), ("g_out", 8), ("g_q_nsa", 1), ("g_k_slc", 1), ("g_k_win", 1),
                        ("g_k_cmp", 1), ("g_q_dil", 1), ("g_k_dil", 1), ("conv_w", 6), ("pe", 32), ("gate_w", 96),
                        ("b_gate", 12), ("w2", 256), ("c", 8), ("ada_b", 192), ("ln_g", 64), ("ln_b", 64),
                        ("mlstm_gw", 64), ("mlstm_b", 2), ("mlstm_norm", 8), ("sinks", 16), ("lower", 32),
                        ("hgrn_norm", 8), ("diff_norm", 1), ("diff_lambda", 256)]:
        COLS[name] = (at, width)
        at += width
    return at


NCOLS = _columns()

KEPT = {"ident": 128, "ones": 128, "block64": 128, "eps6": 1, "tiny": 1, "eps6_32": 1, "eps5_32": 1}
LAYER_CONST = 1024
BIG_CONST = 3 * S


def constants():
    p, f = np.arange(P)[:, None], np.arange(P)[None, :]
    u = np.arange(S)[None, :]
    ident = (p == f).astype(np.float32)
    kept = np.concatenate([ident, np.ones((P, P)), (p // HD == f // HD) / HD, np.full((P, 1), 1e-6),
                           np.full((P, 1), 1e-19), np.full((P, 1), 32 * 32 * 1e-6), np.full((P, 1), 32 * 32 * 1e-5)], 1).astype(np.float32)
    dist = p + (S - P) - u
    causal = np.where(dist >= 0, 0.0, NEG)
    mult = (dist <= 128).astype(int) + (dist % 4 == 0) + (dist % 16 == 0)
    logmult = np.where((dist >= 0) & (mult > 0), np.log(np.maximum(mult, 1)) / SCALE, NEG)
    big = np.concatenate([dist, causal, logmult], 1).astype(np.float32)
    layer = np.zeros((5, P, LAYER_CONST), np.float32)
    t = np.arange(TT)[:, None] * P
    dc = (p[:, :, None] + t[None]) - (np.arange(NCMP) * CMP_STRIDE + CMP_LEN - 1)[None, None, :]
    dc = dc.reshape(P, TT * NCMP)
    layer[0, :, 0:124] = dc
    layer[0, :, 124:248] = dc >= 0
    layer[0, :, 248:372] = np.where(dc >= 0, 0.0, NEG)
    layer[0, :, 384:512] = p >= f
    layer[0, :, 512:640] = p < f
    layer[0, :, 640:768] = np.where(p < f, 0.0, NEG)
    layer[0, :, 768:896] = (p % 32 == 16 * (f // HD))
    layer[1, :, 768:896] = layer[4, :, 768:896] = layer[3, :, 896:] = (p % 32 == 0)
    for h in range(4):
        layer[1, h, h * P:(h + 1) * P] = 1.0
    layer[1, :, 512:640] = np.where(p <= f, 0.0, -NEG)
    rope = np.zeros((P, P), np.float32)
    for b in (0, HD):
        for j in range(8):
            rope[b + 8 + j, b + j] = -1.0
            rope[b + j, b + 8 + j] = 1.0
    inv = np.zeros((P, 1), np.float32)
    for b in (0, HD):
        for j in range(16):
            inv[b + j, 0] = np.float32(ROPE_THETA) ** np.float32(-(j % 8) * 2.0 / 16)
    band = (P + p) - np.arange(2 * P)[None, :]
    for at in (2, 4):
        layer[at, :, 0:128] = rope
        layer[at, :, 128:129] = inv
    layer[2, :, 256:512] = np.where((band >= 0) & (band < 128), 0.0, NEG)
    for lv in range(7):
        b = 64 >> lv
        layer[3, :, lv * P:(lv + 1) * P] = (p // (2 * b) == f // (2 * b)) & (p % (2 * b) < b) & (f % (2 * b) >= b)
    layer[4, :, 256:768] = causal
    return kept, big, layer


PARTS_SPLIT = 3 * DT + FT


def mix_steps(part):
    return {"first": 2, 1: 1, 3: 1}.get(part, 0)


def n_groups(part):
    return {"first": 8 * TT, 1: 16 * TT, 3: 8 * TT}.get(part, 0)


def lin_total(parts):
    return sum(len(IN_PROJ[p][0]) + len(IN_PROJ[p][1]) + 2 * DT + 2 * FT for p in parts)


class Counts(dict):
    def __missing__(self, key):
        return 0

    def add(self, **more):
        for key, by in more.items():
            self[key] = self[key] + by


@contextmanager
def loop(eng, count):
    if count > 1:
        with eng.Fori(0, count) as i:
            yield i
    else:
        yield 0


def wait(eng, semaphore, value):
    if not isinstance(value, int) or value > 0:
        eng.wait_ge(semaphore, value)


def stream_length(parts):
    n = 0
    for part in parts:
        tiles, values = IN_PROJ[part]
        n += len(tiles) + len(values) + (8 if part == "first" else 0) + DT + 2 * FT + 3 * DT
    return n


def program(nc, xT, wstream, ada, cols, kept, bigc, layerc, pos, yT, parts):
    slots_total = stream_length(parts)
    ctx = ExitStack()
    with ctx:
        base = 16512
        top = [0]

        def place(name, shape, dt, at=None):
            size = int(np.prod(shape[1:]))
            if at is None:
                at = top[0]
                top[0] += -(-size // 8) * 8
            return nc.alloc_sbuf_tensor_at(name, shape, dt, offset=base + 4 * at)

        x = place("x", [P, DT, S], F32)
        h_at = top[0]
        h_hi = place("h_hi", [P, DT, S], F32R)
        h_lo = place("h_lo", [P, DT, S], F32R)
        big = top[0]
        hid_hi = place("hid_hi", [P, FT, S], F32R)
        hid_lo = place("hid_lo", [P, FT, S], F32R)
        raw = [place(f"raw{r}", [P, 8, P], F32) for r in range(RING)]
        w_hi = [place(f"w_hi{r}", [P, 8, P], F32R) for r in range(RING)]
        w_lo = [place(f"w_lo{r}", [P, 8, P], F32R) for r in range(RING)]
        ada_raw = [place(f"ada_raw{r}", [P, SLOT], F32) for r in range(ADA_RING)]
        ada_acc = place("ada_acc", [P, SLOT], F32)
        kp = place("kept", [P, sum(KEPT.values())], F32)
        co = place("cols", [P, NCOLS], F32)
        lc = place("layer_const", [P, LAYER_CONST], F32)
        cond = place("cond", [P, 8], F32)
        mod = [place(f"mod{r}", [P, 48], F32) for r in range(2)]
        small = place("small", [P, 160], F32)
        scaled_bias = place("scaled_bias", [P, 8], F32)
        late_shift = place("late_shift", [P, 8], F32)
        assert base + 4 * top[0] <= nc.sbuf_usable_end, top[0]

        h_tmp = place("h_tmp", [P, DT, S], F32, big + 16384)
        sum_out = place("sum_out", [P, S], F32, big + 16384 + 7 * S)
        sum_down = place("sum_down", [P, S], F32, h_at + 15 * S)
        sq = [place(f"sq{r}", [P, S], F32, big + 20480 + r * S) for r in range(2)]
        rt = [place(f"rt{r}", [P, S], F32, big + 21504 + r * S) for r in range(2)]
        proj = place("proj", [P, 24, S], F32, big)
        first_v = place("first_v", [P, TT, S], F32, big + 19 * S)
        v_slc = place("v_slc", [P, TT, HD], F32, big + 23 * S)
        v_win = place("v_win", [P, TT, HD], F32, big + 23 * S + 256)
        tables = place("tables", [P, 3, S], F32, big + 12288)
        s1 = big + 12288 + 3 * S
        AT = {}
        for name, at in (("first", s1), ("late", big + 13312)):
            AT[name] = dict(
                s=[place(f"att_s_{name}{r}", [P, 520], F32, at + r * 520) for r in range(2)],
                p=[place(f"att_p_{name}{r}", [P, 520], F32, at + 1040 + r * 520) for r in range(2)],
                pt=[place(f"att_pt_{name}{r}", [P, S], F32, at + 2080 + r * S) for r in range(2)])
        bias = place("bias", [P, 4, S], F32, s1 + 3104)
        cmp_bias = place("cmp_bias", [P, 4, TT * NCMP], F32, s1 + 5152)
        blk = place("blk", [P, 2, 16, 32], F32, s1)
        blk_parts = place("blk_parts", [P, 2, 16, 2, 32], F32R, s1 + 1024)
        blk_hi, blk_lo = blk_parts[:, :, :, 0, :], blk_parts[:, :, :, 1, :]
        CW = [S - P * j for j in range(TT)]
        CO = [sum(CW[:j]) for j in range(TT)]
        CWS = sum(CW)
        st_z = [place(f"st_z{e}", [P, CWS], F32, s1 + 3 * e * CWS) for e in range(2)]
        st_e = [place(f"st_e{e}", [P, CWS], F32, s1 + (3 * e + 1) * CWS) for e in range(2)]
        st_l = [place(f"st_l{e}", [P, CWS], F32, s1 + (3 * e + 2) * CWS) for e in range(2)]
        ml_v = place("ml_v", [P, TT, D], F32, big + 16 * S)
        ml_e = place("ml_e", [P, CWS], F32, big + 12288)
        ml_a = [place(f"ml_a{r}", [P, CWS], F32, big + 12288 + (1 + r) * CWS) for r in range(2)]
        ml_x = place("ml_x", [P, 4, S], F32, big + 12288 + 3 * CWS)
        ml_r = place("ml_rows", [8, 8, S], F32, big + 36 * S)
        ml_d = place("ml_d", [P, S], F32, h_at)
        ml_t = place("ml_t", [P, S], F32, h_at + S)
        swa_v = place("swa_v", [P, TT, P], F32, big + 9 * S)
        swa_k = place("swa_k", [P, 2, S], F32, big + 10 * S)
        rope_cs = place("rope_cs", [P, 2, S], F32, big + 12288)
        rope_t = [place(f"rope_t{r}", [P, S], F32, big + 13312 + r * S) for r in range(4)]
        rope_i = place("rope_i", [P, S], I32, big + 13312 + 4 * S)
        hg_v = place("hg_v", [P, TT, D], F32, big + 24 * S)
        hg_k = place("hg_k", [P, 8, S], F32, big + 16384)
        hg_one = place("hg_one", [P, S], F32, big + 20480)
        hg_d, hg_q, hg_t = ([place(f"hg_{name}{r}", [P, S], F32, at) for r, at in
                             enumerate((h_at + 2 * b * S, h_at + (2 * b + 1) * S, big + (41 + b) * S))]
                            for b, name in enumerate("dqt"))
        hg_p = [place(f"hg_p{r}", [P, TT, 640], F32, h_at + (6 + 5 * r) * S) for r in range(2)]
        df_v = place("df_v", [P, TT, D], F32, big + 16 * S)

        bank = [ctx.enter_context(nc.psum_tensor(f"bank{b}", [P, S], F32)) for b in range(8)]

        def kept_at(name):
            at = 0
            for k, w in KEPT.items():
                if k == name:
                    return kp[:, at:at + w]
                at += w

        ident, ones, block64 = kept_at("ident"), kept_at("ones"), kept_at("block64")
        eps6, tiny = kept_at("eps6"), kept_at("tiny")
        eps6_32, eps5_32 = kept_at("eps6_32"), kept_at("eps5_32")

        def col(name, j=0, n=1):
            a = COLS[name][0]
            return co[:, a + j:a + j + n]

        dist, causal, logmult = tables[:, 0, :], tables[:, 1, :], tables[:, 2, :]
        gates = small[:, 0:48]
        kcmp = small[:, 48:80]
        vcmp = small[0:32, 80:144]
        att_min = [small[:, 144 + r:145 + r] for r in range(2)]
        att_sum = [small[:, 146 + r:147 + r] for r in range(2)]
        att_inv = [small[:, 148 + r:149 + r] for r in range(2)]
        lam = small[:, 150:151]
        lam_w = small[:, 151:157]
        neg_sinks = small[:, 0:16]
        conv_tmp = place("conv_tmp", [P, S], F32, big + 20480 - S)
        hid_cmp = place("hid_cmp", [P, 4, 32], F32, s1 + 5648)
        hid_pre = place("hid_pre", [P, 4, 32], F32, s1 + 5776)
        ml_w = small[:, 0:16]
        lb = small[:, 0:8]
        one_lb = small[:, 8:16]
        lb_w = small[:, 16:80]

        names = ["const_loaded", "layer_const_loaded", "pos_loaded", "hi_done", "lo_done", "slot_used", "lin_free",
                 "ada_used", "ada_sum", "ada_mod", "cond_done", "sil_done", "part_hi", "part_lo", "n_sq", "n_sum",
                 "n_root", "n_inv", "n_spread", "h_ready", "ln_part", "ln_mean", "ln_centred", "ln_y", "ln_x",
                 "x_scaled", "g_sq", "g_sum", "g_root", "g_inv", "g_spread", "g_out", "att_scores", "att_ready",
                 "att_exp", "att_normed", "att_turned", "att_copied", "att_pv", "att_out", "gate_in", "gate_pre",
                 "gate_out", "blk_ready", "blk_hi_done", "blk_lo_done", "cmp_hidden", "cmp_act", "cmp_mm", "cmp_sq",
                 "cmp_root", "v_turned", "v_out", "conv_step", "mix_ready", "st_scores", "st_log", "st_keep",
                 "st_suffix", "st_arg", "st_attn", "st_pv", "st_out", "rope_ready", "rope_mm", "rope_out",
                 "rope_ang", "ml_gate", "ml_pre", "ml_log", "ml_rows", "ml_turn", "ml_w", "ml_floor",
                 "ml_floor_kept", "ml_spread", "ml_diag", "ml_exp", "ml_a", "ml_den", "ml_num", "ml_out", "ml_sig",
                 "hg_lb", "hg_lbe", "hg_sig", "hg_dec", "hg_log", "hg_diff", "hg_e", "hg_qk", "hg_mm", "hg_put",
                 "hg_pv", "hg_out", "hg_gate", "hg_zero", "lam_in", "lam_exp", "stored", "act_chain", "dve_chain"]
        sm = namedtuple("Semaphores", names)(*[ctx.enter_context(nc.semaphore(name)) for name in names])
        raw_loaded = [ctx.enter_context(nc.semaphore(f"raw_loaded{r}")) for r in range(RING)]
        ada_loaded = [ctx.enter_context(nc.semaphore(f"ada_loaded{r}")) for r in range(ADA_RING)]

        def half(tile_index, head):
            return proj[HD * (head % 2):HD * (head % 2) + HD, tile_index, :]

        def job(q, k, width, bias_ap, values, **more):
            return dict(q=q, k=k, w=width, bias=bias_ap, v=values, sink=None, vis=None, gate=None, first=True,
                        last=True, dv=HD, row=0, dest=None) | more

        def nsa_jobs():
            jobs = []
            for hd in range(NSA_HEADS):
                b = HD * (hd % 2)
                for i in range(TT):
                    q = half(hd // 2, hd)[:, i * P:(i + 1) * P]
                    w = (i + 1) * P
                    common = dict(row=b, dest=q)
                    tok = dict(bias_ap=bias[:, hd, S - w:S])
                    gate = [gates[:, i * 12 + hd * 3 + br:i * 12 + hd * 3 + br + 1] for br in range(3)]
                    jobs.append(job(q, kcmp[b:b + HD, 0:NCMP], NCMP, cmp_bias[:, hd, i * NCMP:(i + 1) * NCMP],
                                    [(vcmp[0:NCMP, :], NCMP)], vis=lc[:, 124 + i * NCMP:124 + (i + 1) * NCMP],
                                    gate=gate[0], last=False, **common))
                    jobs.append(job(q, half(9, hd)[:, 0:w], w, values=[(v_slc[:, j, :], P) for j in range(i + 1)],
                                    gate=gate[1], first=False, last=False, **tok, **common))
                    jobs.append(job(q, half(10, hd)[:, 0:w], w, values=[(v_win[:, j, :], P) for j in range(i + 1)],
                                    gate=gate[2], first=False, **tok, **common))
            return jobs

        def dil_jobs():
            jobs = []
            for hd in range(4):
                for i in range(TT):
                    q, w = half(6 + hd // 2, hd)[:, i * P:(i + 1) * P], (i + 1) * P
                    jobs.append(job(q, half(17 + hd // 2, hd)[:, 0:w], w, bias[:, hd, S - w:S],
                                    [(first_v[:, j, 256 + hd * HD:256 + (hd + 1) * HD], P) for j in range(i + 1)],
                                    row=HD * (hd % 2), dest=q))
            return jobs

        def swa_jobs():
            jobs = []
            for hd in range(16):
                kv = hd // 8
                b = HD * (hd % 2)
                for i in range(TT):
                    q, lo = half(hd // 2, hd)[:, i * P:(i + 1) * P], max(0, i - 1)
                    w = (i + 1 - lo) * P
                    jobs.append(job(q, swa_k[b:b + HD, kv, lo * P:(i + 1) * P], w, lc[:, 512 - w:512],
                                    [(swa_v[:, j, kv * HD:(kv + 1) * HD], P) for j in range(lo, i + 1)],
                                    sink=neg_sinks[:, hd:hd + 1], row=b, dest=q))
            return jobs

        def diff_jobs():
            jobs = []
            for hd in range(8):
                for i in range(TT):
                    w = (i + 1) * P
                    for c in range(2):
                        jobs.append(job(proj[HD * c:HD * c + HD, hd, i * P:(i + 1) * P],
                                        proj[HD * c:HD * c + HD, 8 + hd, 0:w], w, lc[:, 768 - w:768],
                                        [(df_v[:, j, hd * P:(hd + 1) * P], P) for j in range(i + 1)],
                                        gate=lam if c else None, first=c == 0, last=c == 1, dv=P,
                                        dest=proj[:, hd, i * P:(i + 1) * P]))
            return jobs

        def item(src, mat, scale, gain, out, mul=None):
            return dict(src=src, mat=mat, scale=scale, gain=gain, out=out, mul=mul)

        halves32 = block64[:, 48:80]

        def spread_rows(part):
            at = 896 if part == 2 else 768
            return lc[:, at:at + P]

        def first_norms():
            items = []
            for t, g in ((0, "g_q_nsa"), (1, "g_q_nsa"), (6, "g_q_dil"), (7, "g_q_dil"), (17, "g_k_dil"),
                         (18, "g_k_dil")):
                items.append(item([proj[:, t, :]], halves32, 1.0, [col(g)], [[proj[:, t, :]]]))
            for t, g in ((9, "g_k_slc"), (10, "g_k_win")):
                items.append(item([proj[0:HD, t, :]], halves32[0:HD, :], 1.0, [col(g)[0:HD, :]],
                                  [[proj[HD:P, t, :], proj[0:HD, t, :]]]))
            return items

        def out_norms(part):
            if part == "first":
                return [item([proj[:, t, :]], halves32, 1.0, [col("g_out", t)], [[proj[:, t, :]]]) for t in range(DT)]
            if part == 0:
                return [item([proj[:, 2 * g + e, :] for e in range(2)], ones[:, 0:32], 1 / 256,
                             [col("mlstm_norm", 2 * g + e) for e in range(2)],
                             [[proj[:, 2 * g + e, :]] for e in range(2)], [proj[:, 8 + 2 * g + e, :] for e in range(2)])
                        for g in range(4)]
            if part == 2:
                return [item([proj[:, t, :]], ones[:, 0:32], 1 / P, [col("hgrn_norm", t)], [[proj[:, t, :]]],
                             [proj[:, 16 + t, :]]) for t in range(DT)]
            if part == 3:
                return [item([proj[:, t, :]], ones[:, 0:32], 1 / P, [lam_w[:, 5:6]], [[proj[:, t, :]]]) for t in range(DT)]
            return []

        def mod_col(layer, sub, kind, j, n=1):
            a = sub * 24 + kind * 8 + j
            return mod[layer % 2][:, a:a + n]

        SHIFT, ONE_SCALE, ONE_GATE = range(3)
        LV = [256, 128, 64, 32, 16, 8, 4, 2, 1]

        def halves(ap, b):
            q = ap.rearrange("p (n h b) -> p n h b", h=2, b=b)
            return q[:, :, 0, :], q[:, :, 1, :]

        block = ctx.enter_context(nc.Block())

        @block.sync
        def _(sp):
            n = Counts()

            def load_slot(k, i=0, step=0):
                if k >= RING:
                    sp.wait_ge(sm.lo_done, k - RING + 1 + step * i)
                sp.dma_start(raw[k % RING][:, :, :].rearrange("p a b -> p (a b)"),
                             wstream[k + step * i, :, :]).then_inc(raw_loaded[k % RING], 16)

            def load_ada(a, i=0, step=0):
                if a >= ADA_RING or not isinstance(i, int):
                    sp.wait_ge(sm.ada_used, a - ADA_RING + 1 + step * i)
                sp.dma_start(ada_raw[a % ADA_RING][:, :],
                             ada[a + step * i, :, :]).then_inc(ada_loaded[a % ADA_RING], 16)

            def load_slots(count):
                k = n["slot"]
                n.add(slot=count)
                if k == 0:
                    for q in range(RING):
                        load_slot(q)
                    k, count = RING, count - RING
                with loop(sp, count // RING) as i:
                    for q in range(RING):
                        load_slot(k + q, i, RING)
                for q in range(count // RING * RING, count):
                    load_slot(k + q)

            def load_ffn(with_ada):
                ahead = 6
                load_slots(ahead)
                k, a = n["slot"], n["ada"]
                if with_ada:
                    first = 0
                    if a == 0:
                        for q in range(8):
                            load_slot(k + q)
                            load_ada(a + q)
                        first = 1
                    with sp.Fori(first, 5) as i:
                        for q in range(8):
                            load_slot(k + q, i, 8)
                            load_ada(a + q, i, 8)
                    for q, lot in ((40, (40, 41)), (41, (42, 43)), (42, ()), (43, (44, 45)), (44, (46, 47))):
                        for more in lot:
                            load_ada(a + more)
                        load_slot(k + q)
                    n.add(slot=45, ada=48)
                load_slots(2 * FT + 3 * DT - ahead - (45 if with_ada else 0))

            sp.dma_start(kp[:, :], kept).then_inc(sm.const_loaded, 16)
            sp.dma_start(x[:, :, :], xT).then_inc(sm.const_loaded, 16)
            sp.dma_start(co[:, :], cols).then_inc(sm.const_loaded, 16)
            for at, part in enumerate(parts):
                tiles, values = IN_PROJ[part]
                if part != "first":
                    sp.wait_ge(sm.part_lo, PARTS_SPLIT * at)
                    sp.dma_start(lc[:, :], layerc[1 + part, :, :]).then_inc(sm.layer_const_loaded, 16)
                if part == "first":
                    load_slots(8)
                    sp.dma_start(lc[:, :], layerc[0, :, :]).then_inc(sm.layer_const_loaded, 16)
                    sp.dma_start(tables[:, :, :].rearrange("p a b -> p (a b)"), bigc).then_inc(sm.layer_const_loaded, 16)
                load_slots(len(tiles) + len(values))
                load_slots(DT)
                load_ffn(at + 1 < len(parts))
            if parts[-1] == "first":
                sp.wait_ge(sm.lin_free, lin_total(parts))
            else:
                sp.wait_ge(sm.ln_x, DT)
            sp.dma_start(yT, x[:, :, :]).then_inc(sm.stored, 16)
            sp.wait_ge(sm.stored, 16)

        @block.gpsimd
        def _(pool):
            def low(k, i=0, step=0):
                pool.wait_ge(sm.hi_done, k + 1 + step * i)
                nc.gpsimd.tensor_tensor(w_lo[k % RING][:, :, :], raw[k % RING][:, :, :],
                                        w_hi[k % RING][:, :, :].bitcast(F32), ALU.subtract).then_inc(sm.lo_done, 1)

            def low_to(end):
                k, count = n["slot"], end - n["slot"]
                with loop(pool, count // RING) as i:
                    for q in range(RING):
                        low(k + q, i, RING)
                for q in range(count // RING * RING, count):
                    low(k + q)
                n.add(slot=count)

            def hgrn():
                for r in range(3):
                    nc.gpsimd.memset(hg_q[r][:, :], 0.0)
                    op = nc.gpsimd.memset(hg_t[r][:, :], 0.0)
                op.then_inc(sm.hg_zero, 1)
                pool.wait_ge(sm.hg_zero, 1)
                for hd in range(8):
                    for at in range(9):
                        m, i, b = hd * 10 + at, hd * 9 + at, LV[at]
                        pool.wait_ge(sm.hg_e, i + 1)
                        wait(pool, sm.hg_mm, m - 2)
                        d = halves(hg_d[i % 3][:, :], b)
                        nc.gpsimd.tensor_tensor(halves(hg_q[m % 3][:, :], b)[1], halves(proj[:, hd, :], b)[1], d[1],
                                                ALU.mult)
                        nc.gpsimd.tensor_tensor(halves(hg_t[m % 3][:, :], b)[0], halves(hg_k[:, hd, :], b)[0], d[0],
                                                ALU.mult).then_inc(sm.hg_qk, 2 if at == 8 else 1)

            n = Counts()
            def gated_convolution():
                g = nc.gpsimd
                steps = 0

                def link(ins):
                    nonlocal steps
                    steps += 1
                    ins.then_inc(sm.conv_step, 1)
                    pool.wait_ge(sm.conv_step, steps)

                pool.wait_ge(sm.lin_free, len(IN_PROJ["first"][0]))
                for t in range(2):
                    u, y, w = proj[:, 13 + t, :], proj[:, 11 + t, :], [col("conv_w", 3 * t + i) for i in range(3)]
                    link(g.tensor_tensor(u, u, y, ALU.mult))
                    link(g.tensor_scalar(y, u, w[2], None, ALU.mult))
                    for lag in (1, 2):
                        link(g.tensor_scalar(conv_tmp[:, lag:S], u[:, 0:S - lag], w[2 - lag], None, ALU.mult))
                        link(g.tensor_tensor(y[:, lag:S], y[:, lag:S], conv_tmp[:, lag:S], ALU.add))
                    link(g.tensor_tensor(proj[:, 2 + t, :], y, proj[:, 2 + t, :], ALU.mult))

            first_slot = 0
            for at, part in enumerate(parts):
                tiles, values = IN_PROJ[part]
                if part == "first":
                    low_to(len(tiles) + len(values) + 8 + LEAD)
                    gated_convolution()
                if part in (1, 3):
                    low_to(first_slot + LEAD)
                    pool.wait_ge(sm.lin_free, lin_total(parts[:at]))
                    pool.dma_start(rope_i[:, :], pos).then_inc(sm.pos_loaded, 16)
                if part == 2:
                    low_to(first_slot + len(tiles) + len(values) + LEAD)
                    pool.wait_ge(sm.lin_free, lin_total(parts[:at]) + len(tiles) + len(values))
                    hgrn()
                first_slot += stream_length([part])
            low_to(slots_total)

        @block.tensor
        def _(pe):
            n = Counts()
            mm, turn = nc.tensor.matmul, nc.tensor.transpose

            def slot_products(k, i, step, pairs, first, last):
                pe.wait_ge(sm.lo_done, k + 1 + step * i)
                r = k % RING
                for at, (out, w, hi, lo) in enumerate(pairs):
                    begin, end = first and w == 0, last and w == len(pairs) - 1
                    mm(out, w_hi[r][:, at, :], hi, start=first and at == 0, stop=False)
                    mm(out, w_hi[r][:, at, :], lo, start=False, stop=False)
                    op = mm(out, w_lo[r][:, at, :], hi, start=False, stop=last and at == len(pairs) - 1)
                op.then_inc(sm.slot_used, 1)

            def m_tile(k, mt, i, step, mt_step, hi, lo, chunks, parts_from=None):
                if mt >= 4:
                    pe.wait_ge(sm.lin_free, mt - 3 + mt_step * i)
                c0 = 0
                for s, m in enumerate(chunks):
                    if parts_from is not None:
                        pe.wait_ge(sm.part_lo, parts_from + c0 + m)
                    slot_products(k + s, i, step,
                                  [(bank[mt % 4][:, 0:hi.shape[2]], c, hi[:, c0 + c, :], lo[:, c0 + c, :])
                                   for c in range(m)], s == 0, s == len(chunks) - 1)
                    c0 += m

            def linear(tiles, hi, lo, chunks):
                k, mt, per = n["slot"], n["mt"], len(chunks)
                done = 0
                if mt < 4:
                    for q in range(4):
                        m_tile(k + q * per, mt + q, 0, 0, 0, hi, lo, chunks)
                    done = 4
                count = (tiles - done) // 4
                if count:
                    with loop(pe, count) as i:
                        for q in range(4):
                            m_tile(k + (done + q) * per, mt + done + q, i, 4 * per, 4, hi, lo, chunks)
                for q in range(done + 4 * count, tiles):
                    m_tile(k + q * per, mt + q, 0, 0, 0, hi, lo, chunks)
                n.add(slot=tiles * per, mt=tiles)

            def value_slot(k, mt, s, i=0, step=0):
                pe.wait_ge(sm.lo_done, k + 1 + step * i)
                hi, lo = (w[k % RING][:, :, :].rearrange("p (c t) m -> p c (t m)", c=2) for w in (w_hi, w_lo))
                for t in range(TT):
                    if s == 0:
                        pe.wait_ge(sm.lin_free, mt + t - 3 + step * i)
                    out, tok = bank[(mt + t) % 4][:, :], slice(t * P, (t + 1) * P)
                    for c in range(2):
                        d = 2 * s + c
                        mm(out, h_hi[:, d, tok], hi[:, c, :], start=d == 0, stop=False)
                        mm(out, h_hi[:, d, tok], lo[:, c, :], start=False, stop=False)
                        op = mm(out, h_lo[:, d, tok], hi[:, c, :], start=False, stop=d == DT - 1)
                op.then_inc(sm.slot_used, 1)

            def value_tile(k, mt, between):
                pe.wait_ge(sm.lin_free, mt - 3)
                pe.wait_ge(sm.lo_done, k + 1)
                r = k % RING
                for t in range(TT):
                    out, tok = bank[mt % 4][:, t * P:(t + 1) * P], slice(t * P, (t + 1) * P)
                    for c in range(DT):
                        mm(out, h_hi[:, c, tok], w_hi[r][:, c, :], start=c == 0, stop=False)
                        mm(out, h_hi[:, c, tok], w_lo[r][:, c, :], start=False, stop=False)
                        op = mm(out, h_lo[:, c, tok], w_hi[r][:, c, :], start=False, stop=c == DT - 1)
                    if t == TT - 1:
                        op.then_inc(sm.slot_used, 1)
                    between(t)

            def value_tiles(count, between=None):
                k, mt = n["slot"], n["mt"]
                n.add(slot=count, mt=count)
                if count < TT:
                    value_tile(k, mt, between)
                elif between:
                    for s in range(count):
                        value_slot(k + s, mt + s // TT * TT, s % TT)
                        between(s)
                else:
                    with loop(pe, count // TT) as i:
                        for s in range(TT):
                            value_slot(k + s, mt, s, i, TT)

            def early_chunk(c):
                k, mt = n["slot"], n["mt"]
                pe.wait_ge(sm.part_lo, n["part"] + c + 1)
                for q in range(EARLY):
                    if c == 0:
                        wait(pe, sm.lin_free, mt + q - 3)
                        pe.wait_ge(sm.lo_done, k + q + 1)
                    r, out = (k + q) % RING, bank[(mt + q) % 4][:, :]
                    mm(out, w_hi[r][:, c, :], h_hi[:, c, :], start=c == 0, stop=False)
                    mm(out, w_hi[r][:, c, :], h_lo[:, c, :], start=False, stop=False)
                    op = mm(out, w_lo[r][:, c, :], h_hi[:, c, :], start=False, stop=c == DT - 1)
                    if c == DT - 1:
                        op.then_inc(sm.slot_used, 1)

            def early_done():
                n.add(part=DT, slot=EARLY, mt=EARLY)

            def early_tiles():
                for c in range(DT):
                    early_chunk(c)
                early_done()

            def residual_tiles(done, hi, lo, chunks, sums, parts_from=None, after_first=None):
                k, mt, per = n["slot"], n["mt"], len(chunks)
                summed = 0
                for q in range(done, DT + 1):
                    if q < DT:
                        m_tile(k + (q - done) * per, mt + q - done, 0, 0, 0, hi, lo, chunks,
                               parts_from if q == 0 else None)
                        if q == 0:
                            after_first()
                    if sums:
                        while summed < q:
                            sums(summed, mt - done)
                            summed += 1
                n.add(slot=(DT - done) * per, mt=DT - done)

            def sum_x(part_sum):
                def add(c, mt):
                    if c == DT - 2:
                        n.add(ln=1)
                        pe.wait_ge(sm.ln_part, n["ln"])
                        mm(bank[5][:, :], ones, part_sum[:, :], start=True, stop=False)
                    if c == DT - 1:
                        pe.wait_ge(sm.lin_free, mt + DT)
                        mm(bank[5][:, :], ones, x[:, c, :], start=False, stop=True).then_inc(sm.ln_mean, 1)
                return add

            def sum_squares(c, mt):
                pe.wait_ge(sm.n_sq, n["sq"] + 1)
                for t in range(TT):
                    op = mm(bank[6][32 * t:32 * t + 32, 0:P], ones[:, 0:32], sq[c % 2][:, t * P:(t + 1) * P],
                            start=c == 0, stop=c == DT - 1)
                op.then_inc(sm.n_sum, 1)
                n.add(sq=1)
                if c == DT - 1:
                    n.add(norm=1)
                    pe.wait_ge(sm.n_inv, n["norm"])
                    mm(bank[4][:, :], ones, rt[1][:, :], start=True, stop=True).then_inc(sm.n_spread, 1)

            def mean_squares():
                for c in range(DT):
                    sum_squares(c, 0)

            def group_sum(items, t):
                it = items[t]
                for u in range(len(it["src"])):
                    n.add(gt=1)
                    pe.wait_ge(sm.g_sq, n["gt"])
                    rows, at = it["src"][u].shape[0], 32 * (t % 4)
                    mm(bank[6 + t // 4][at:at + 32, :], it["mat"], sq[(n["gt"] - 1) % 2][0:rows, :], start=u == 0,
                       stop=u == len(it["src"]) - 1).then_inc(sm.g_sum, 1)

            def group_spread(part, t, outs):
                at, q = 32 * (t % 4), t // 4
                pe.wait_ge(sm.g_inv, n["gq"] + q + 1)
                wait(pe, sm.g_out, n["gn"] + t - len(outs) + 1)
                mm(bank[outs[t % len(outs)]][:, :], spread_rows(part)[at:at + 32, :], rt[q][at:at + 32, :], start=True,
                   stop=True).then_inc(sm.g_spread, 1)

            def normed_linear(part, items):
                c = 0
                for t in range(len(items)):
                    group_sum(items, t)
                for t in range(len(items) + 2):
                    if t < len(items):
                        group_spread(part, t, (4, 5))
                    if t >= 2:
                        for _ in items[t - 2]["src"]:
                            early_chunk(c)
                            c += 1
                n.add(gn=len(items), gq=len(items) // 4)
                early_done()

            def attention(jobs, bufs):
                a, g = n["att"], n["att_g"]
                for step in range(len(jobs) + 3):
                    if step < len(jobs):
                        j, it = step, jobs[step]
                        wait(pe, sm.att_ready, a + j - 1)
                        mm(bank[j % 2][:, 0:it["w"]], it["q"], it["k"], start=True,
                           stop=True).then_inc(sm.att_scores, 1)
                    if 2 <= step <= len(jobs) + 1:
                        j, it = step - 2, jobs[step - 2]
                        pe.wait_ge(sm.att_normed, a + j + 1)
                        wait(pe, sm.att_copied, a + j - 1)
                        at = 0
                        for t, (_, keys) in enumerate(it["v"]):
                            op = turn(bank[2 + j % 2][0:keys, t * P:(t + 1) * P], bufs["p"][j % 2][:, at:at + keys],
                                      ident)
                            at += keys
                        op.then_inc(sm.att_turned, 1)
                    if step >= 3:
                        j, it = step - 3, jobs[step - 3]
                        pe.wait_ge(sm.att_copied, a + j + 1)
                        if it["first"]:
                            g += 1
                            wait(pe, sm.att_out, g - 4)
                        out = bank[4 + g % 4][it["row"]:it["row"] + it["dv"], 0:P]
                        for t, (v, keys) in enumerate(it["v"]):
                            op = mm(out, v, bufs["pt"][j % 2][0:keys, t * P:(t + 1) * P],
                                    start=it["first"] and t == 0, stop=it["last"] and t == len(it["v"]) - 1)
                        op.then_inc(sm.att_pv, 1)
                n.add(att=len(jobs), att_g=sum(it["last"] for it in jobs))

            def first_values():
                k, mt, items = n["slot"], n["mt"], first_norms()
                used = {"v": 0, "b": 0}
                pe.wait_ge(sm.lin_free, mt)
                for s, kind in enumerate(VALUES_AND_BLOCKS):
                    at = used[kind]
                    used[kind] += 1
                    if kind == "v":
                        value_slot(k + s, mt, at)
                    else:
                        kv, half_in = at // 4, at % 2
                        if at == 0:
                            pe.wait_ge(sm.blk_lo_done, 2)
                        pe.wait_ge(sm.lo_done, k + s + 1)
                        r, out = (k + s) % RING, bank[5][:, at // 2 * 64:at // 2 * 64 + 64]
                        for c in range(8):
                            both = blk_parts[:, kv, 8 * half_in + c, :, :]
                            first, last = half_in == 0 and c == 0, half_in == 1 and c == 7
                            mm(out, w_hi[r][:, c, :], both.rearrange("p e n -> p (e n)"), start=first, stop=False)
                            op = mm(out[:, 0:32], w_lo[r][:, c, :], both[:, 0, :], start=False, stop=last)
                        op.then_inc(sm.slot_used, 1)
                    if s == 0:
                        for b, tile in ((0, 9), (1, 10)):
                            for t in range(TT):
                                op = turn(bank[7][:, (b * TT + t) * HD:(b * TT + t + 1) * HD],
                                          proj[HD:P, tile, t * P:(t + 1) * P], ident[HD:P, HD:P])
                        op.then_inc(sm.v_turned, 1)
                    if 1 <= s <= len(items):
                        if s == 5:
                            pe.wait_ge(sm.v_out, 1)
                        group_sum(items, s - 1)
                    if s == 6:
                        pe.wait_ge(sm.layer_const_loaded, 32)
                    if s >= 6:
                        group_spread("first", s - 6, (4,))
                for t in range(len(VALUES_AND_BLOCKS) - 6, len(items)):
                    group_spread("first", t, (4,))
                n.add(slot=len(VALUES_AND_BLOCKS), mt=TT, gn=len(items), gq=2)
                pe.wait_ge(sm.g_out, n["gn"])
                pe.wait_ge(sm.cmp_act, 1)
                w2 = [col("w2", 128 * kv, 128).rearrange("p (m d) -> p m d", m=2) for kv in range(2)]
                for m in range(2):
                    op = mm(bank[4][0:HD, 0:32], w2[0][:, m, :], hid_cmp[:, m, :], start=m == 0, stop=m == 1)
                for m in range(2):
                    op = mm(bank[5][0:32, 256:256 + HD], hid_cmp[:, 2 + m, :], w2[1][:, m, :], start=m == 0, stop=m == 1)
                op.then_inc(sm.cmp_mm, 1)
                pe.wait_ge(sm.cmp_sq, 1)
                mm(bank[4][0:HD, 64:96], block64[0:HD, 0:HD], hid_pre[0:HD, 0, :], start=True,
                   stop=True).then_inc(sm.cmp_mm, 1)

            def first_mixer():
                pe.wait_ge(sm.mix_ready, 1)
                attention(nsa_jobs(), AT["first"])
                stick_breaking()
                pe.wait_ge(sm.mix_ready, 2)
                attention(dil_jobs(), AT["first"])

            def stick_breaking():
                suffix, every = lc[:, 384:512], ones
                pe.wait_ge(sm.att_out, n["att_g"])
                for h0 in (0, 2):
                    for e in range(2):
                        hd = h0 + e
                        q, k = half(4 + hd // 2, hd), half(15 + hd // 2, hd)
                        wait(pe, sm.st_out, hd - 1)
                        for j in range(TT):
                            op = mm(bank[4 * e + j][:, 0:CW[j]], k[:, j * P:(j + 1) * P], q[:, j * P:S], start=True,
                                    stop=True)
                        op.then_inc(sm.st_scores, 1)
                    for e in range(2):
                        pe.wait_ge(sm.st_keep, h0 + e + 1)
                        for j in range(TT):
                            for jj in range(j, TT):
                                op = mm(bank[4 * e + j][:, P * (jj - j):CW[j]], suffix if jj == j else every,
                                        st_l[e][:, CO[jj]:CO[jj] + CW[jj]], start=jj == j, stop=jj == TT - 1)
                        op.then_inc(sm.st_suffix, 1)
                    for e in range(2):
                        hd, b = h0 + e, HD * e
                        pe.wait_ge(sm.st_attn, hd + 1)
                        for j in range(TT):
                            op = mm(bank[4 * e][b:b + HD, j * P:S], first_v[:, j, hd * HD:(hd + 1) * HD],
                                    st_z[e][:, CO[j]:CO[j] + CW[j]], start=j == 0, stop=j == TT - 1)
                        op.then_inc(sm.st_pv, 1)

            def turned_halves(t):
                wait(pe, sm.rope_out, n["rope"] - 1)
                mm(bank[4 + n["rope"] % 2][:, :], lc[:, 0:128], proj[:, t, :], start=True,
                   stop=True).then_inc(sm.rope_mm, 1)
                n.add(rope=1)

            def mlstm_gates():
                gw = col("mlstm_gw", 0, 64).rearrange("p (c g) -> p c g", c=DT)
                for g in range(2):
                    for c in range(DT):
                        op = mm(bank[6 + g][0:4, :], gw[:, c, 4 * g:4 * g + 4], h_tmp[:, c, :], start=c == 0,
                                stop=c == DT - 1)
                op.then_inc(sm.ml_gate, 1)

            def mlstm():
                pe.wait_ge(sm.ml_rows, 1)
                for t in range(TT):
                    op = turn(bank[0][:, 4 * t:4 * t + 4], ml_r[0:4, 4, t * P:(t + 1) * P], ident[0:4, 0:4])
                op.then_inc(sm.ml_turn, 1)
                pe.wait_ge(sm.ml_w, 1)
                for hd in range(4):
                    op = mm(bank[(1, 6, 7, 2)[hd]][:, :], lc[0:4, hd * P:(hd + 1) * P], ml_r[0:4, 6, :], start=True, stop=True)
                op.then_inc(sm.ml_floor, 1)
                pe.wait_ge(sm.ml_floor_kept, 1)

                def scores(hd):
                    q, k = proj[:, 2 * hd, :], proj[:, 2 * hd + 1, :]
                    wait(pe, sm.ml_a, hd)
                    mm(bank[0][:, :], lc[0:4, hd * P:(hd + 1) * P], ml_r[0:4, 5, :], start=True, stop=True)
                    for j in range(TT):
                        op = mm(bank[2 + j][:, 0:CW[j]], k[:, j * P:(j + 1) * P], q[:, j * P:S], start=True, stop=True)
                    op.then_inc(sm.ml_spread, 1)

                scores(0)
                for hd in range(4):
                    a = ml_a[hd % 2]
                    if hd < 3:
                        scores(hd + 1)
                    pe.wait_ge(sm.ml_a, hd + 1)
                    wait(pe, sm.ml_out, hd)
                    for j in range(TT):
                        op = mm(bank[6][:, j * P:S], ones, a[:, CO[j]:CO[j] + CW[j]], start=j == 0, stop=j == TT - 1)
                    op.then_inc(sm.ml_den, 1)
                    for e in range(2):
                        for j in range(TT):
                            op = mm(bank[7 if e else 1][:, j * P:S], ml_v[:, j, hd * 256 + e * P:hd * 256 + (e + 1) * P],
                                    a[:, CO[j]:CO[j] + CW[j]], start=j == 0, stop=j == TT - 1)
                    op.then_inc(sm.ml_num, 1)

            def hgrn():
                def values(hd):
                    pe.wait_ge(sm.hg_put, hd * 10 + 10)
                    wait(pe, sm.hg_out, hd - 1)
                    for j in range(TT):
                        op = mm(bank[6 + hd % 2][:, j * P:S], hg_v[:, j, hd * P:(hd + 1) * P],
                                hg_p[hd % 2][:, j, 0:CW[j]], start=j == 0, stop=j == TT - 1)
                    op.then_inc(sm.hg_pv, 1)

                for hd in range(8):
                    for at, b in enumerate(LV + [0]):
                        m = hd * 10 + at
                        pe.wait_ge(sm.hg_qk, m + 1)
                        wait(pe, sm.hg_put, m - 2)
                        kk = hg_t[m % 3][:, :] if b else hg_k[:, hd, :]
                        qq = hg_q[m % 3][:, :] if b else proj[:, hd, :]
                        if b == 256:
                            for j in range(2):
                                op = mm(bank[j][:, 0:256], kk[:, j * P:(j + 1) * P], qq[:, 256:S], start=True, stop=True)
                        elif b == 128:
                            for j in (0, 2):
                                op = mm(bank[2][:, j * 64:j * 64 + P], kk[:, j * P:(j + 1) * P],
                                        qq[:, (j + 1) * P:(j + 2) * P], start=True, stop=True)
                        else:
                            for j in range(TT):
                                op = mm(bank[3 + m % 3][:, j * P:(j + 1) * P], kk[:, j * P:(j + 1) * P],
                                        qq[:, j * P:(j + 1) * P], start=True, stop=True)
                        op.then_inc(sm.hg_mm, 1)
                        if at == 2 and hd:
                            values(hd - 1)
                values(7)

            def ffn(with_ada, sums):
                early_tiles()
                k, mt, a = n["slot"], n["mt"], n["ada"]

                def ada_sums(g, i):
                    if not with_ada:
                        return
                    pe.wait_ge(sm.ada_used, a + 8 * g + 8 + 8 * i)
                    for j in range(8):
                        op = mm(bank[7][:, j:j + 1], ada_acc[:, j * P:(j + 1) * P], ones[:, 0:1], start=True, stop=True)
                    op.then_inc(sm.ada_sum, 1)

                with pe.Fori(0, 5) as i:
                    for q in range(8):
                        m_tile(k + q, mt + q, i, 8, 8, h_hi, h_lo, [8])
                        if q == 5:
                            ada_sums(0, i)
                for q in range(40, 2 * FT - EARLY):
                    m_tile(k + q, mt + q, 0, 0, 0, h_hi, h_lo, [8])
                n.add(slot=2 * FT - EARLY, mt=2 * FT - EARLY, ada=48 if with_ada else 0)
                residual_tiles(0, hid_hi, hid_lo, [8, 8, 6], sums, parts_from=n["part"],
                               after_first=lambda: ada_sums(5, 0))
                n.add(part=FT)

            pe.wait_ge(sm.const_loaded, 48)
            for at, part in enumerate(parts):
                tiles, values = IN_PROJ[part]
                n.add(lc=2 if part == "first" else 1)
                if part == "first":
                    mean_squares()
                early_tiles()
                if part == "first":
                    gw = col("gate_w", 0, 96).rearrange("p (c g) -> p c g", c=DT)
                    for t in range(TT):
                        for c in range(DT):
                            op = mm(bank[6][:, t * 12:(t + 1) * 12], h_tmp[:, c, t * P:(t + 1) * P], gw[:, c, :],
                                    start=c == 0, stop=c == DT - 1)
                    op.then_inc(sm.gate_in, 1)
                if part == 0:
                    mlstm_gates()
                linear(len(tiles) - EARLY, h_hi, h_lo, [8])
                if part == "first":
                    first_values()
                elif part in (1, 3):
                    pe.wait_ge(sm.layer_const_loaded, 16 * n["lc"])
                    if part == 3:
                        pe.wait_ge(sm.lin_free, n["mt"])

                    def two_tiles(s):
                        if part == 1 and s == 0:
                            pe.wait_ge(sm.lin_free, n["mt"] - 1)
                        for t in range(2 * s, min(2 * s + 2, len(tiles))):
                            turned_halves(t)

                    value_tiles(len(values), two_tiles)
                    if part == 1:
                        two_tiles(TT)
                else:
                    value_tiles(len(values))
                pe.wait_ge(sm.layer_const_loaded, 16 * n["lc"])
                pe.wait_ge(sm.lin_free, n["mt"])
                if part == "first":
                    first_mixer()
                elif part == 0:
                    mlstm()
                elif part == 1:
                    pe.wait_ge(sm.mix_ready, n["mix"] + 1)
                    attention(swa_jobs(), AT["late"])
                elif part == 2:
                    hgrn()
                else:
                    pe.wait_ge(sm.mix_ready, n["mix"] + 1)
                    attention(diff_jobs(), AT["late"])
                n.add(mix=mix_steps(part))
                if out_norms(part):
                    normed_linear(part, out_norms(part))
                else:
                    early_tiles()
                residual_tiles(EARLY, h_hi, h_lo, [8], sum_squares if part == "first" else sum_x(sum_out))
                if part != "first":
                    mean_squares()
                ffn(at + 1 < len(parts), None if part == "first" else sum_x(sum_down))
                if part != "first":
                    mean_squares()

        @block.scalar
        def _(act):
            n = Counts()
            fn = nc.scalar.activation

            def link(ins):
                n.add(act_chain=1)
                ins.then_inc(sm.act_chain, 1)
                act.wait_ge(sm.act_chain, n["act_chain"])

            def split(t, i=0, step=0):
                if not isinstance(i, int) or t < slots_total:
                    act.wait_ge(raw_loaded[t % RING], 16 * (t // RING + 1) + 16 * step // RING * i)
                    if t >= RING:
                        act.wait_ge(sm.slot_used, t - RING + 1 + step * i)
                    fn(w_hi[t % RING][:, :, :], raw[t % RING][:, :, :], ACT.Copy).then_inc(sm.hi_done, 1)

            def split_ahead(count):
                k = n["slot"]
                n.add(slot=count)
                done = 0
                if k + LEAD < RING:
                    for q in range(RING):
                        split(k + q + LEAD)
                    done = RING
                full = (count - done) // RING
                if k + LEAD + count > slots_total:
                    full = 0
                if full:
                    with loop(act, full) as i:
                        for q in range(RING):
                            split(k + done + q + LEAD, i, RING)
                for q in range(done + full * RING, count):
                    split(k + q + LEAD)

            def mean_squares(eps, ready):
                for c in range(DT):
                    ready(c)
                    wait(act, sm.n_sum, n["sq"] + c - 1)
                    fn(sq[c % 2][:, :], x[:, c, :], ACT.Square).then_inc(sm.n_sq, 1)
                n.add(sq=DT)
                act.wait_ge(sm.n_sum, n["sq"])
                fn(rt[0][:, 0:P], bank[6][:, 0:P], ACT.Sqrt, bias=eps, scale=32 * 32 / D).then_inc(sm.n_root, 1)

            def high(c, src):
                fn(h_hi[:, c, :], src, ACT.Copy).then_inc(sm.part_hi, 1)

            def split_input(normed, scaled):
                for c in range(DT):
                    act.wait_ge(sm.h_ready, n["h"] + c + 1)
                    high(c, h_tmp[:, c, :])
                    if normed:
                        fn(x[:, c, :], x[:, c, :], ACT.Identity, bias=scaled_bias[:, c:c + 1],
                           scale=ALPHA).then_inc(sm.x_scaled, 1)
                    elif scaled:
                        nc.scalar.mul(x[:, c, :], x[:, c, :], ALPHA).then_inc(sm.x_scaled, 1)
                n.add(h=DT, part=DT)

            def centred_squares():
                mean_squares(eps5_32, lambda c: act.wait_ge(sm.ln_centred, n["ln"] * DT + c + 1))
                n.add(ln=1)

            def add_bias(c):
                act.wait_ge(sm.ln_y, (n["ln"] - 1) * DT + c + 1)
                return fn(x[:, c, :], x[:, c, :], ACT.Identity, bias=col("ln_b", n["ln_at"] * 8 + c))

            def group_squares(items, t):
                for src in items[t]["src"]:
                    wait(act, sm.g_sum, n["gt"] - 1)
                    fn(sq[n["gt"] % 2][0:src.shape[0], :], src, ACT.Square).then_inc(sm.g_sq, 1)
                    n.add(gt=1)

            def group_root(items, q):
                it, per = items[4 * q], len(items[0]["src"])
                n.add(gr=4 * per)
                act.wait_ge(sm.g_sum, n["gr"])
                fn(rt[q][:, :], bank[6 + q][:, :], ACT.Sqrt, bias=eps6, scale=it["scale"]).then_inc(sm.g_root, 1)

            def group_norms(items):
                c = 0
                for t in range(len(items)):
                    group_squares(items, t)
                    if t in (4, len(items) - 1):
                        group_root(items, 0 if t == 4 or len(items) == 4 else 1)
                for t in range(len(items)):
                    act.wait_ge(sm.g_out, n["gn"] + t + 1)
                    for _ in items[t]["src"]:
                        high(c, proj[:, c, :])
                        c += 1
                n.add(gn=len(items), part=c)

            def attention(jobs, bufs):
                a = n["att"]
                for step in range(len(jobs) + 1):
                    if step < len(jobs):
                        j, it = step, jobs[step]
                        w = it["w"] + (it["sink"] is not None)
                        act.wait_ge(sm.att_ready, a + j + 1)
                        wait(act, sm.att_turned, a + j - 1)
                        fn(bufs["p"][j % 2][:, 0:w], bufs["s"][j % 2][:, 0:w], ACT.Exp, bias=att_min[j % 2],
                           scale=-1.0, accum_out=att_sum[j % 2]).then_inc(sm.att_exp, 1)
                    if step >= 1:
                        j, it = step - 1, jobs[step - 1]
                        act.wait_ge(sm.att_turned, a + j + 1)
                        wait(act, sm.att_pv, a + j - 1)
                        r, w = it["v"][0][1], len(it["v"]) * P
                        fn(bufs["pt"][j % 2][0:r, 0:w], bank[2 + j % 2][0:r, 0:w], ACT.Copy).then_inc(sm.att_copied, 1)
                n.add(att=len(jobs))

            def first_projections():
                items = first_norms()
                split_ahead(16)
                act.wait_ge(sm.blk_ready, 2)
                for kv in range(2):
                    fn(blk_hi[:, kv, :, :], blk[:, kv, :, :], ACT.Copy).then_inc(sm.blk_hi_done, 1)
                split_ahead(3)
                for s in range(len(VALUES_AND_BLOCKS)):
                    split(n["slot"] + s + LEAD)
                    if s < len(items):
                        group_squares(items, s)
                    if s in (4, 8):
                        group_root(items, s // 4 - 1)
                n.add(slot=len(VALUES_AND_BLOCKS), gn=len(items))
                act.wait_ge(sm.cmp_hidden, 1)
                fn(hid_cmp[:, :, :], hid_pre[:, :, :], ACT.Gelu_apprx_tanh).then_inc(sm.cmp_act, 1)
                act.wait_ge(sm.cmp_mm, 1)
                fn(hid_pre[0:HD, 0, :], bank[4][0:HD, 0:32], ACT.Square).then_inc(sm.cmp_sq, 1)
                act.wait_ge(sm.cmp_mm, 2)
                fn(hid_pre[0:HD, 1, :], bank[4][0:HD, 64:96], ACT.Sqrt, bias=eps6[0:HD, :]).then_inc(sm.cmp_root, 1)

            def first_mixer():
                attention(nsa_jobs(), AT["first"])
                act.wait_ge(sm.att_out, TT * NSA_HEADS)
                act.wait_ge(sm.conv_step, 14)
                for h0 in (0, 2):
                    for e in range(2):
                        z, s = st_z[e], st_e[e]
                        act.wait_ge(sm.st_scores, h0 + e + 1)
                        wait(act, sm.st_pv, h0 + e - 1)
                        for j in range(TT):
                            op = fn(z[:, CO[j]:CO[j] + CW[j]], bank[4 * e + j][:, 0:CW[j]], ACT.Copy, scale=SCALE)
                        link(op)
                        link(fn(s[:, :], z[:, :], ACT.Abs))
                        link(fn(s[:, :], s[:, :], ACT.Exp, scale=-1.0))
                        fn(s[:, :], s[:, :], ACT.Ln, bias=1.0).then_inc(sm.st_log, 1)
                    for e in range(2):
                        act.wait_ge(sm.st_arg, h0 + e + 1)
                        fn(st_z[e][:, :], st_e[e][:, :], ACT.Exp).then_inc(sm.st_attn, 1)
                attention(dil_jobs(), AT["first"])

            def rope_tables():
                n.add(rt=1)
                for f in range(2):
                    act.wait_ge(sm.rope_ang, 2 * n["rt"] - 1 + f)
                    fn(rope_cs[:, 1 - f, :], rope_t[f][:, :], ACT.Sin).then_inc(sm.rope_ready, 1)

            def mlstm_gates():
                mt = n["mt"]
                split_ahead(8)
                act.wait_ge(sm.ml_pre, 1)
                link(fn(ml_r[0:4, 2, :], ml_r[0:4, 1, :], ACT.Abs))
                link(fn(ml_r[0:4, 2, :], ml_r[0:4, 2, :], ACT.Exp, scale=-1.0))
                fn(ml_r[0:4, 2, :], ml_r[0:4, 2, :], ACT.Ln, bias=1.0).then_inc(sm.ml_log, 1)
                split_ahead(8)
                act.wait_ge(sm.ml_pre, 2)
                fn(ml_r[0:4, 6, :], ml_r[0:4, 2, :], ACT.Exp, scale=-1.0).then_inc(sm.ml_rows, 1)
                for t in range(8, 16):
                    act.wait_ge(sm.lin_free, mt + t + 1)
                    op = fn(proj[:, t, :], proj[:, t, :], ACT.Sigmoid)
                op.then_inc(sm.ml_sig, 1)
                split_ahead(8)

            def mlstm():
                act.wait_ge(sm.ml_floor, 1)
                for hd in range(4):
                    op = fn(ml_x[:, hd, :], bank[(1, 6, 7, 2)[hd]][:, :], ACT.Copy)
                op.then_inc(sm.ml_floor_kept, 1)
                act.wait_ge(sm.ml_w, 1)
                for hd in range(4):
                    act.wait_ge(sm.ml_diag, hd + 1)
                    for j in range(TT - 1):
                        fn(ml_e[:, CO[j] + P:CO[j] + CW[j]], bank[0][:, (j + 1) * P:S], ACT.Exp, scale=-1.0,
                           bias=ml_w[:, 4 * j + hd:4 * j + hd + 1])
                    for j in range(TT):
                        op = fn(ml_e[:, CO[j]:CO[j] + P], ml_d[:, j * P:(j + 1) * P], ACT.Exp, scale=-1.0,
                                bias=ml_w[:, 4 * j + hd:4 * j + hd + 1])
                    op.then_inc(sm.ml_exp, 1)
                act.wait_ge(sm.ml_out, 4)

            def hgrn_gates():
                mt = n["mt"]
                split_ahead(8)
                act.wait_ge(sm.hg_lb, 1)
                fn(lb_w[:, 0:32], lb_w[:, 0:32], ACT.Exp).then_inc(sm.hg_lbe, 1)
                split_ahead(8)
                for h0 in (0, 4):
                    for hd in range(h0, h0 + 4):
                        act.wait_ge(sm.lin_free, mt + 9 + hd)
                        fn(hg_k[:, hd, :], proj[:, 8 + hd, :], ACT.Sigmoid, scale=-1.0)
                        fn(proj[:, 8 + hd, :], proj[:, 8 + hd, :], ACT.Sigmoid).then_inc(sm.hg_sig, 1)
                    split_ahead(4 if h0 == 0 else 8)
                for hd in range(8):
                    act.wait_ge(sm.hg_dec, hd + 1)
                    fn(proj[:, 8 + hd, :], proj[:, 8 + hd, :], ACT.Ln).then_inc(sm.hg_log, 1)
                split_ahead(4)
                for t in range(16, 24):
                    act.wait_ge(sm.lin_free, mt + t + 1)
                    op = fn(proj[:, t, :], proj[:, t, :], ACT.Silu)
                op.then_inc(sm.hg_gate, 1)

            def hgrn():
                for e in range(72):
                    act.wait_ge(sm.hg_diff, e + 1)
                    fn(hg_d[e % 3][:, :], hg_d[e % 3][:, :], ACT.Exp).then_inc(sm.hg_e, 1)
                act.wait_ge(sm.hg_out, 8)

            def ffn():
                k, mt, m0, p0 = n["slot"], n["mt"], n["m"], n["part"]

                def up(q, i):
                    wait(act, sm.part_lo, p0 + q - 1 + 4 * i)
                    act.wait_ge(sm.slot_used, k + 2 * q + 1 + 8 * i)
                    fn(sil[q % 2], bank[(mt + 2 * q) % 4][:, :], ACT.Silu).then_inc(sm.sil_done, 1)
                    split(k + 2 * q + LEAD, i, 8)
                    split(k + 2 * q + 1 + LEAD, i, 8)
                    act.wait_ge(sm.lin_free, mt + 2 * q + 2 + 8 * i)
                    act.wait_ge(sm.const_loaded, 48)
                    fn(hid_hi[:, q + 4 * i, :], sil[q % 2], ACT.Copy).then_inc(sm.part_hi, 1)

                with act.Fori(0, 5) as i:
                    for q in range(4):
                        up(q, i)
                for q in range(20, 22):
                    up(q, 0)
                n.add(slot=2 * FT, mt=2 * FT, part=FT)
                split_ahead(3 * DT)
                n.add(mt=DT)

            sil = [lc[:, r * S:(r + 1) * S] for r in range(2)]
            act.wait_ge(sm.const_loaded, 48)
            normed = False

            def first_slots(c):
                if 2 <= c < 2 + LEAD:
                    split(c - 2)

            for at, part in enumerate(parts):
                tiles, values = IN_PROJ[part]
                n.add(lc=2 if part == "first" else 1)
                if part == "first":
                    mean_squares(eps6_32, first_slots)
                split_input(normed, part != "first")
                if part == "first":
                    fn(cond[:, :], col("c", 0, 8), ACT.Silu).then_inc(sm.cond_done, 1)
                    act.wait_ge(sm.gate_pre, 1)
                    fn(gates, gates, ACT.Sigmoid).then_inc(sm.gate_out, 1)
                if part == "first":
                    first_projections()
                elif part == 0:
                    mlstm_gates()
                elif part == 2:
                    hgrn_gates()
                elif part in (1, 3):
                    split_ahead(8)
                    rope_tables()
                    split_ahead(len(tiles) + len(values) - 8)
                else:
                    split_ahead(len(tiles) + len(values))
                n.add(mt=len(tiles) + len(values))
                act.wait_ge(sm.lin_free, n["mt"])
                act.wait_ge(sm.layer_const_loaded, 16 * n["lc"])
                if part == "first":
                    first_mixer()
                    act.wait_ge(sm.att_out, n_groups("first"))
                    act.wait_ge(sm.mix_ready, 2)
                    n.add(mix=2)
                elif part == 0:
                    mlstm()
                elif part == 1:
                    attention(swa_jobs(), AT["late"])
                elif part == 2:
                    hgrn()
                else:
                    act.wait_ge(sm.lam_in, 1)
                    fn(lam_w[:, 2:4], lam_w[:, 0:2], ACT.Exp).then_inc(sm.lam_exp, 1)
                    attention(diff_jobs(), AT["late"])
                n.add(out=n_groups(part))
                wait(act, sm.att_out, n["out"])
                if out_norms(part):
                    group_norms(out_norms(part))
                else:
                    for c in range(DT):
                        high(c, proj[:, c, :])
                    n.add(part=DT)
                if part == "first":
                    k, mt = n["slot"], n["mt"]

                    def whole(c):
                        split(k + c + LEAD)
                        act.wait_ge(sm.lin_free, mt + c + 1)

                    mean_squares(eps6_32, whole)
                    n.add(slot=DT, mt=DT)
                else:
                    split_ahead(DT)
                    n.add(mt=DT)
                    centred_squares()
                    n["ln_at"] = 2 * part
                split_input(part != "first", part != "first")
                ffn()
                normed = part != "first"
                if normed:
                    centred_squares()
                    n["ln_at"] = 2 * part + 1
            for c in range(DT if normed else 0):
                add_bias(c).then_inc(sm.ln_x, 1)

        @block.vector
        def _(dve):
            n = Counts()
            v = nc.vector

            def link(ins):
                n.add(dve_chain=1)
                ins.then_inc(sm.dve_chain, 1)
                dve.wait_ge(sm.dve_chain, n["dve_chain"])

            def low(c, src):
                n.add(part=1)
                dve.wait_ge(sm.part_hi, n["part"])
                v.tensor_tensor(h_lo[:, c, :], src, h_hi[:, c, :].bitcast(F32), ALU.subtract).then_inc(sm.part_lo, 1)

            inverse_root = bank[4][:, :]

            def root():
                n.add(root=1)
                link(v.memset(rt[1][:, :], 0.0))
                dve.wait_ge(sm.n_root, n["root"])
                link(v.reciprocal(rt[0][:, 0:P], rt[0][:, 0:P]))
                for t in range(TT):
                    rows = slice(32 * t, 32 * t + 32)
                    op = v.tensor_copy(rt[1][rows, t * P:(t + 1) * P], rt[0][rows, 0:P])
                op.then_inc(sm.n_inv, 1)
                dve.wait_ge(sm.n_spread, n["root"])

            def rms_input(gain):
                root()
                for c in range(DT + 1):
                    if c < DT:
                        v.scalar_tensor_tensor(h_tmp[:, c, :], x[:, c, :], col(gain, c), inverse_root, ALU.mult,
                                               ALU.mult).then_inc(sm.h_ready, 1)
                    if c:
                        low(c - 1, h_tmp[:, c - 1, :])

            def normed_tile(c, gain_at):
                v.scalar_tensor_tensor(x[:, c, :], x[:, c, :], col("ln_g", gain_at * 8 + c), inverse_root, ALU.mult,
                                       ALU.mult).then_inc(sm.ln_y, 1)

            def modulated_input(layer, sub, gain_at):
                normed = gain_at is not None
                for c in range(DT + 1):
                    if normed and c < DT:
                        normed_tile(c, gain_at)
                    if c:
                        low(c - 1, h_tmp[:, c - 1, :])
                    if c < DT:
                        if normed:
                            dve.wait_ge(sm.ln_y, n["ln_y"] + c + 1)
                        shift = late_shift[:, c:c + 1] if normed else mod_col(layer, sub, SHIFT, c)
                        v.tensor_scalar(h_tmp[:, c, :], x[:, c, :], mod_col(layer, sub, ONE_SCALE, c), shift,
                                        ALU.mult, ALU.add).then_inc(sm.h_ready, 1)
                n.add(ln_y=DT if normed else 0)

            def shifts(layer, sub, gain_at):
                link(v.tensor_tensor(late_shift[:, :], col("ln_b", gain_at * 8, 8), mod_col(layer, sub, ONE_SCALE, 0, 8),
                                     ALU.mult))
                link(v.tensor_tensor(late_shift[:, :], late_shift[:, :], mod_col(layer, sub, SHIFT, 0, 8), ALU.add))
                link(v.tensor_scalar(scaled_bias[:, :], col("ln_b", gain_at * 8, 8), ALPHA, None, ALU.mult))

            def centre(layer=None, sub=None, gain_at=None):
                if layer is not None:
                    shifts(layer, sub, gain_at)
                n.add(ln=1)
                dve.wait_ge(sm.ln_mean, n["ln"])
                for c in range(DT):
                    v.scalar_tensor_tensor(x[:, c, :], bank[5][:, :], -1.0 / D, x[:, c, :], ALU.mult,
                                           ALU.add).then_inc(sm.ln_centred, 1)
                root()

            def tile_done(slots):
                n.add(slot=slots)
                dve.wait_ge(sm.slot_used, n["slot"])
                n.add(mt=1)
                return bank[(n["mt"] - 1) % 4]

            def keep(tiles, values, between=lambda t: None, rotated=False):
                for t in range(tiles):
                    v.tensor_copy(proj[:, t, :], tile_done(1)[:, :]).then_inc(sm.lin_free, 1)
                    between(t)
                if len(values) == 1:
                    rope(range(tiles))
                    v.tensor_copy(values[0], tile_done(1)[:, :].rearrange("p (t d) -> p t d", t=TT)).then_inc(sm.lin_free, 1)
                else:
                    for t, out in enumerate(values):
                        if rotated and t % TT == 0:
                            rope(range(2 * t, 2 * t + 8))
                        v.tensor_copy(out, tile_done(0 if t % TT else TT)[:, :]).then_inc(sm.lin_free, 1)
                        between(tiles + t)
                dve.wait_ge(sm.lin_free, n["mt"])

            def add_residual(slots, layer=None, sub=None, part_sum=None):
                if layer is not None:
                    n.add(xs=DT)
                    dve.wait_ge(sm.x_scaled, n["xs"])
                for m in range(DT):
                    b = tile_done(slots)
                    if layer is None:
                        v.tensor_tensor(x[:, m, :], b[:, :], x[:, m, :], ALU.add).then_inc(sm.lin_free, 1)
                    else:
                        v.scalar_tensor_tensor(x[:, m, :], b[:, :], mod_col(layer, sub, ONE_GATE, m), x[:, m, :],
                                               ALU.mult, ALU.add).then_inc(sm.lin_free, 1)
                        dve.wait_ge(sm.lin_free, n["mt"])
                        if 1 <= m < DT - 1:
                            op = v.tensor_tensor(part_sum[:, :], part_sum[:, :] if m > 1 else x[:, 0, :], x[:, m, :], ALU.add)
                            if m < DT - 2:
                                link(op)
                            else:
                                op.then_inc(sm.ln_part, 1)
                dve.wait_ge(sm.lin_free, n["mt"])

            def group_inverse(q):
                n.add(gq=1)
                dve.wait_ge(sm.g_root, n["gq"])
                v.reciprocal(rt[q][:, :], rt[q][:, :]).then_inc(sm.g_inv, 1)

            def group_norm(items, t, banks):
                it = items[t]
                rows = it["src"][0].shape[0]
                r = bank[banks[t % len(banks)]][0:rows, :]
                dve.wait_ge(sm.g_spread, n["gn"] + t + 1)
                for u, src in enumerate(it["src"]):
                    for out in it["out"][u]:
                        op = v.scalar_tensor_tensor(out, src, it["gain"][u], r, ALU.mult, ALU.mult)
                    if it["mul"]:
                        link(op)
                        op = v.tensor_tensor(out, out, it["mul"][u], ALU.mult)
                op.then_inc(sm.g_out, 1)

            def group_norms(items):
                done = 0
                group_inverse(0)
                for t in range(len(items) + 1):
                    if t == 2 and len(items) > 4:
                        group_inverse(1)
                    if t < len(items):
                        group_norm(items, t, (4, 5))
                    if t:
                        for _ in items[t - 1]["src"]:
                            low(done, proj[:, done, :])
                            done += 1
                n.add(gn=len(items))

            def attention(jobs, bufs):
                a, g = n["att"], n["att_g"]
                for step in range(len(jobs) + 4):
                    if step < len(jobs):
                        j, it = step, jobs[step]
                        s, w, sink = bufs["s"][j % 2], it["w"], it["sink"]
                        dve.wait_ge(sm.att_scores, a + j + 1)
                        wait(dve, sm.att_exp, a + j - 1)
                        if sink is not None:
                            v.tensor_copy(s[:, w:w + 1], sink)
                        v.tensor_tensor_reduce(s[:, 0:w], bank[j % 2][:, 0:w], it["bias"], -SCALE,
                                               BIG if sink is None else sink, ALU.add, ALU.min,
                                               att_min[j % 2]).then_inc(sm.att_ready, 1)
                    if 1 <= step <= len(jobs):
                        j, it = step - 1, jobs[step - 1]
                        p, w, inv = bufs["p"][j % 2], it["w"], att_inv[j % 2]
                        dve.wait_ge(sm.att_exp, a + j + 1)
                        link(v.reciprocal(inv, att_sum[j % 2]))
                        if it["vis"] is not None:
                            link(v.tensor_tensor(inv, inv, it["gate"], ALU.mult))
                            op = v.scalar_tensor_tensor(p[:, 0:w], p[:, 0:w], inv, it["vis"], ALU.mult, ALU.mult)
                        elif it["gate"] is not None:
                            op = v.tensor_scalar(p[:, 0:w], p[:, 0:w], inv, it["gate"], ALU.mult, ALU.mult)
                        else:
                            op = v.tensor_scalar(p[:, 0:w], p[:, 0:w], inv, None, ALU.mult)
                        op.then_inc(sm.att_normed, 1)
                    if step >= 4 and jobs[step - 4]["last"]:
                        j, it = step - 4, jobs[step - 4]
                        g += 1
                        dve.wait_ge(sm.att_pv, a + j + 1)
                        rows = slice(it["row"], it["row"] + it["dv"])
                        v.tensor_copy(it["dest"], bank[4 + g % 4][rows, 0:P]).then_inc(sm.att_out, 1)
                n.add(att=len(jobs), att_g=sum(it["last"] for it in jobs))

            def first_between(t):
                if t == 12:
                    link(v.memset(blk[:, :, :, :], 0.0))
                    pe_cols = col("pe", 0, 32).rearrange("p (a c) -> p a c", a=2)
                    for kv in range(2):
                        rows = slice(HD * kv, HD * kv + HD)
                        tok = proj[rows, 8, :].rearrange("p (n r) -> p r n", r=CMP_STRIDE)
                        for par in range(2):
                            for c1 in range(2):
                                op = v.tensor_tensor(
                                    blk[HD * par:HD * par + HD, kv, 8 * c1:8 * c1 + 8, 0:NCMP],
                                    tok[:, par::2, c1:c1 + NCMP],
                                    pe_cols[rows, par, 8 * c1:8 * c1 + 8].unsqueeze(2).to_broadcast([HD, 8, NCMP]), ALU.add)
                    op.then_inc(sm.blk_ready, 2)
                elif t == 15:
                    dve.wait_ge(sm.layer_const_loaded, 32)
                    for hd in range(NSA_HEADS):
                        v.scalar_tensor_tensor(bias[:, hd, :], dist, -SLOPES_A[hd] / SCALE, causal, ALU.mult, ALU.add)
                        v.scalar_tensor_tensor(cmp_bias[:, hd, :], lc[:, 0:124], -SLOPES_A[hd] / SCALE, lc[:, 248:372],
                                               ALU.mult, ALU.add)
                elif t == 17:
                    for kv in range(2):
                        dve.wait_ge(sm.blk_hi_done, kv + 1)
                        v.tensor_tensor(blk_lo[:, kv, :, :], blk[:, kv, :, :], blk_hi[:, kv, :, :].bitcast(F32),
                                        ALU.subtract).then_inc(sm.blk_lo_done, 1)

            def first_values():
                items = first_norms()
                dve.wait_ge(sm.v_turned, 1)
                v.tensor_copy(v_slc[:, :, :], bank[7][:, 0:256].rearrange("p (t d) -> p t d", t=TT))
                v.tensor_copy(v_win[:, :, :], bank[7][:, 256:512].rearrange("p (t d) -> p t d", t=TT)).then_inc(sm.v_out, 1)
                group_inverse(0)
                for t in range(4):
                    if t == 3:
                        group_inverse(1)
                    group_norm(items, t, (4,))
                last = VALUES_AND_BLOCKS.rindex("v") + 1
                for t in range(TT):
                    v.tensor_copy(first_v[:, t, :], tile_done(0 if t else last)[:, :]).then_inc(sm.lin_free, 1)
                n.add(slot=len(VALUES_AND_BLOCKS) - last)
                for t in range(4, len(items)):
                    group_norm(items, t, (4,))
                    if t == 5:
                        dve.wait_ge(sm.slot_used, n["slot"])
                        v.tensor_reduce(hid_pre[:, :, :], bank[5][:, 0:256].rearrange("p (a e n) -> p a n e", a=4, e=2),
                                        AX_X, ALU.add).then_inc(sm.cmp_hidden, 1)
                n.add(gn=len(items))
                dve.wait_ge(sm.cmp_mm, 2)
                v.tensor_copy(vcmp[0:NCMP, :], bank[5][0:NCMP, 256:256 + HD])
                dve.wait_ge(sm.cmp_root, 1)
                link(v.reciprocal(hid_pre[0:HD, 1, :], hid_pre[0:HD, 1, :]))
                for b in (HD, 0):
                    op = v.scalar_tensor_tensor(kcmp[b:b + HD, :], bank[4][0:HD, 0:32], col("g_k_cmp")[0:HD, :],
                                                hid_pre[0:HD, 1, :], ALU.mult, ALU.mult)
                dve.wait_ge(sm.gate_out, 1)
                op.then_inc(sm.mix_ready, 1)
                dve.wait_ge(sm.lin_free, n["mt"])
                dve.wait_ge(sm.mix_ready, 1)

            def first_mixer():
                attention(nsa_jobs(), AT["first"])
                stick_breaking()
                for hd in range(4):
                    op = v.scalar_tensor_tensor(bias[:, hd, :], dist, -SLOPES_D[hd] / SCALE, logmult, ALU.mult, ALU.add)
                op.then_inc(sm.mix_ready, 1)
                dve.wait_ge(sm.mix_ready, 2)
                attention(dil_jobs(), AT["first"])

            def stick_breaking():
                strict, shut = lc[:, 512:640], lc[:, 640:768]
                for h0 in (0, 2):
                    for e in range(2):
                        dve.wait_ge(sm.st_log, h0 + e + 1)
                        link(v.scalar_tensor_tensor(st_l[e][:, :], st_z[e][:, :], 0.0, st_e[e][:, :], ALU.max, ALU.add))
                        for j in range(TT):
                            d = st_l[e][:, CO[j]:CO[j] + P]
                            op = v.tensor_tensor(d, d, strict, ALU.mult)
                        op.then_inc(sm.st_keep, 1)
                    for e in range(2):
                        dve.wait_ge(sm.st_suffix, h0 + e + 1)
                        for j in range(TT):
                            d = slice(CO[j], CO[j] + CW[j])
                            op = v.tensor_tensor(st_e[e][:, d], st_z[e][:, d], bank[4 * e + j][:, 0:CW[j]], ALU.subtract)
                        link(op)
                        for j in range(TT):
                            d = st_e[e][:, CO[j]:CO[j] + P]
                            op = v.tensor_tensor(d, d, shut, ALU.add)
                        op.then_inc(sm.st_arg, 1)
                    for e in range(2):
                        hd, b = h0 + e, HD * e
                        dve.wait_ge(sm.st_pv, hd + 1)
                        v.tensor_copy(half(4 + hd // 2, hd), bank[4 * e][b:b + HD, :]).then_inc(sm.st_out, 1)
                dve.wait_ge(sm.st_out, 4)

            def rope_tables():
                n.add(rt=1, lcw=0)
                ang, y = rope_t[2], rope_t[3]
                dve.wait_ge(sm.pos_loaded, 16 * n["rt"])
                link(v.tensor_copy(y[:, :], rope_i[:, :]))
                link(v.tensor_scalar(ang[:, :], y[:, :], lc[:, 128:129], None, ALU.mult))
                turns = [6.28125, 0.0019350051879882812, 3.0200114160515973e-07]
                for f, shift in enumerate((0.0, 0.25)):
                    r = rope_t[f]
                    link(v.tensor_scalar(y[:, :], ang[:, :], 1 / (2 * np.pi), shift, ALU.mult, ALU.add))
                    link(v.tensor_scalar(y[:, :], y[:, :], 12582912.0, None, ALU.add))
                    link(v.tensor_scalar(y[:, :], y[:, :], 12582912.0, None, ALU.subtract))
                    link(v.scalar_tensor_tensor(r[:, :], y[:, :], -turns[0], ang[:, :], ALU.mult, ALU.add))
                    link(v.scalar_tensor_tensor(r[:, :], y[:, :], -turns[1], r[:, :], ALU.mult, ALU.add))
                    link(v.scalar_tensor_tensor(r[:, :], y[:, :], -turns[2], r[:, :], ALU.mult, ALU.add))
                    if f:
                        link(v.tensor_scalar(r[:, :], r[:, :], float(np.pi / 2), None, ALU.add))
                    v.tensor_scalar(r[:, :], r[:, :], 3.1415925, -3.1415925, ALU.min, ALU.max).then_inc(sm.rope_ang, 1)

            def rope(tiles):
                dve.wait_ge(sm.rope_ready, 2 * n["rt"])
                for t in tiles:
                    n.add(rope=1)
                    a = rope_t[n["rope"] % 2]
                    dve.wait_ge(sm.rope_mm, n["rope"])
                    v.tensor_tensor(a[:, :], bank[4 + (n["rope"] - 1) % 2][:, :], rope_cs[:, 1, :], ALU.mult)
                    link(v.tensor_tensor(proj[:, t, :], proj[:, t, :], rope_cs[:, 0, :], ALU.mult))
                    v.tensor_tensor(proj[:, t, :], proj[:, t, :], a[:, :], ALU.add).then_inc(sm.rope_out, 1)

            def rope_between(t):
                if t == EARLY:
                    v.tensor_scalar(neg_sinks, col("sinks", 0, 16), -1.0, None, ALU.mult)
                    dve.wait_ge(sm.layer_const_loaded, 16 * n["lc"])
                    rope_tables()

            def mlstm_gates(t):
                if t == 4:
                    b = col("mlstm_b", 0, 2)
                    dve.wait_ge(sm.ml_gate, 1)
                    v.tensor_scalar(ml_r[0:4, 0, :], bank[6][0:4, :], b[0:4, 0:1], None, ALU.add)
                    v.tensor_scalar(ml_r[0:4, 1, :], bank[7][0:4, :], b[0:4, 1:2], None, ALU.add).then_inc(sm.ml_pre, 1)
                    link(v.memset(ml_r[0:4, 7, :], 1.0))
                elif t == 10:
                    dve.wait_ge(sm.ml_log, 1)
                    link(v.scalar_tensor_tensor(ml_r[0:4, 3, :], ml_r[0:4, 1, :], 0.0, ml_r[0:4, 2, :], ALU.min,
                                                ALU.subtract))
                    link(v.tensor_tensor_scan(ml_r[0:4, 1, :], ml_r[0:4, 7, :], ml_r[0:4, 3, :], 0.0, ALU.mult, ALU.add))
                    link(v.tensor_tensor(ml_r[0:4, 4, :], ml_r[0:4, 0, :], ml_r[0:4, 1, :], ALU.subtract))
                    link(v.tensor_tensor_scan(ml_r[0:4, 5, :], ml_r[0:4, 4, :], ml_r[0:4, 4, :], 0.0, ALU.max, ALU.max))
                    v.tensor_tensor(ml_r[0:4, 2, :], ml_r[0:4, 1, :], ml_r[0:4, 5, :], ALU.add).then_inc(sm.ml_pre, 1)

            def mlstm():
                dve.wait_ge(sm.ml_turn, 1)
                v.tensor_copy(ml_w, bank[0][:, 0:16]).then_inc(sm.ml_w, 1)

                def diagonal(hd):
                    dve.wait_ge(sm.ml_spread, hd + 1)
                    v.tensor_tensor(ml_d[:, :].rearrange("p (t q) -> p t q", t=TT),
                                    bank[0][:, :].rearrange("p (t q) -> p t q", t=TT),
                                    lc[:, 512:640].unsqueeze(1).to_broadcast([P, TT, P]), ALU.add).then_inc(sm.ml_diag, 1)

                def weights(hd):
                    dve.wait_ge(sm.ml_exp, hd + 1)
                    for j in range(TT):
                        d = slice(CO[j], CO[j] + CW[j])
                        op = v.scalar_tensor_tensor(ml_a[hd % 2][:, d], bank[2 + j][:, 0:CW[j]], P ** -0.5, ml_e[:, d],
                                                    ALU.mult, ALU.mult)
                    op.then_inc(sm.ml_a, 1)

                def output(hd):
                    x_h = ml_x[:, hd, :]
                    dve.wait_ge(sm.ml_den, hd + 1)
                    link(v.scalar_tensor_tensor(x_h, bank[6][:, :], -1.0, x_h, ALU.mult, ALU.max))
                    link(v.scalar_tensor_tensor(ml_t[:, :], bank[6][:, :], 1.0, x_h, ALU.mult, ALU.max))
                    link(v.reciprocal(ml_t[:, :], ml_t[:, :]))
                    dve.wait_ge(sm.ml_num, hd + 1)
                    for e in range(2):
                        op = v.tensor_tensor(proj[:, 2 * hd + e, :], bank[7 if e else 1][:, :], ml_t[:, :], ALU.mult)
                    op.then_inc(sm.ml_out, 1)

                diagonal(0)
                weights(0)
                for hd in range(4):
                    if hd < 3:
                        diagonal(hd + 1)
                    output(hd)
                    if hd < 3:
                        weights(hd + 1)
                dve.wait_ge(sm.ml_out, 4)
                dve.wait_ge(sm.ml_sig, 1)

            def hgrn_gates(t):
                low = col("lower", 0, 32).rearrange("p (l c) -> p c l", l=4)
                top, e = lb_w[:, 32:40], lb_w[:, 0:32]
                if t == 3:
                    link(v.tensor_reduce(top, low, AX_X, ALU.max))
                    v.tensor_tensor(e.rearrange("p (l c) -> p l c", l=4),
                                    col("lower", 0, 32).rearrange("p (l c) -> p l c", l=4),
                                    top.unsqueeze(1).to_broadcast([P, 4, 8]), ALU.subtract).then_inc(sm.hg_lb, 1)
                elif t == 12:
                    v.memset(hg_one[:, :], 1.0)
                    dve.wait_ge(sm.hg_lbe, 1)
                    link(v.tensor_reduce(top, e.rearrange("p (l c) -> p c l", l=4), AX_X, ALU.add))
                    v.tensor_tensor(lb, e[:, 8:16], e[:, 16:24], ALU.add)
                    v.tensor_tensor(one_lb, e[:, 0:8], e[:, 24:32], ALU.add)
                    link(v.reciprocal(top, top))
                    v.tensor_tensor(lb, lb, top, ALU.mult)
                    link(v.tensor_tensor(one_lb, one_lb, top, ALU.mult))
                elif t in (19, 23):
                    for hd in range(t - 19, t - 15):
                        f = proj[:, 8 + hd, :]
                        dve.wait_ge(sm.hg_sig, hd + 1)
                        link(v.tensor_scalar(f, f, one_lb[:, hd:hd + 1], lb[:, hd:hd + 1], ALU.mult, ALU.add))
                        v.tensor_scalar(hg_k[:, hd, :], hg_k[:, hd, :], one_lb[:, hd:hd + 1], None, ALU.mult)
                        v.tensor_scalar(f, f, tiny, None, ALU.max).then_inc(sm.hg_dec, 1)
                elif t == 27:
                    for hd in range(8):
                        f = proj[:, 8 + hd, :]
                        dve.wait_ge(sm.hg_log, hd + 1)
                        v.tensor_tensor_scan(f, hg_one[:, :], f, 0.0, ALU.mult, ALU.add)

            def hgrn():
                for r in range(2):
                    op = v.memset(hg_p[r][:, :, :], 0.0)
                link(op)

                def decays(hd, at):
                    b, i = LV[at], hd * 9 + at
                    early, late = halves(proj[:, 8 + hd, :], b)
                    mid = early[:, :, b - 1:b].to_broadcast([P, S // (2 * b), b])
                    d = halves(hg_d[i % 3][:, :], b)
                    wait(dve, sm.hg_qk, hd * 10 + (-3, -2, 0, 1, 2, 3, 4, 5, 6)[at])
                    v.tensor_tensor(d[0], mid, early, ALU.subtract)
                    v.tensor_tensor(d[1], late, mid, ALU.subtract).then_inc(sm.hg_diff, 1)

                def put(hd, at):
                    m, b, weights = hd * 10 + at, (LV + [0])[at], hg_p[hd % 2]
                    dve.wait_ge(sm.hg_mm, m + 1)
                    wait(dve, sm.hg_put, m)
                    if b == 256:
                        wait(dve, sm.hg_pv, hd - 1)
                        v.tensor_copy(weights[:, 0, 256:512], bank[0][:, 0:256])
                        op = v.tensor_copy(weights[:, 1, 128:384], bank[1][:, 0:256])
                    elif b == 128:
                        v.tensor_copy(weights[:, 0, 128:256], bank[2][:, 0:128])
                        op = v.tensor_copy(weights[:, 2, 128:256], bank[2][:, 128:256])
                    else:
                        mask = lc[:, (at - 2) * P:(at - 1) * P] if b else ident
                        op = v.copy_predicated(weights[:, :, 0:P],
                                               mask.bitcast(I32).unsqueeze(1).to_broadcast([P, TT, P]),
                                               bank[3 + m % 3][:, :].rearrange("p (t q) -> p t q", t=TT))
                    op.then_inc(sm.hg_put, 1)

                def output(hd):
                    dve.wait_ge(sm.hg_pv, hd + 1)
                    v.tensor_copy(proj[:, hd, :], bank[6 + hd % 2][:, :]).then_inc(sm.hg_out, 1)

                decays(0, 0)
                decays(0, 1)
                for hd in range(8):
                    for at in range(9):
                        if at < 7:
                            decays(hd, at + 2)
                        elif hd < 7:
                            decays(hd + 1, at - 7)
                        if at:
                            put(hd, at - 1)
                        elif hd:
                            put(hd - 1, 8)
                            put(hd - 1, 9)
                        if at == 4 and hd:
                            output(hd - 1)
                put(7, 8)
                put(7, 9)
                output(7)
                dve.wait_ge(sm.hg_out, 8)
                dve.wait_ge(sm.hg_gate, 1)

            def lambdas():
                a = col("diff_lambda", 0, 256).rearrange("p (l d) -> p l d", l=4)
                prod = small[:, 0:128].rearrange("p (l d) -> p l d", l=2)
                link(v.tensor_tensor(prod, a[:, 0:4:2, :], a[:, 1:4:2, :], ALU.mult))
                v.tensor_reduce(lam_w[:, 0:2], prod, AX_X, ALU.add).then_inc(sm.lam_in, 1)
                v.tensor_scalar(lam_w[:, 5:6], col("diff_norm"), 1.0 - LAM_INIT[3], None, ALU.mult)
                dve.wait_ge(sm.lam_exp, 1)
                link(v.tensor_tensor(lam, lam_w[:, 3:4], lam_w[:, 2:3], ALU.subtract))
                link(v.tensor_scalar(lam, lam, -LAM_INIT[3], None, ALU.add))

            def ffn(ahead, layer):
                k, mt, p0, s0, a0, cg = n["slot"], n["mt"], n["part"], n["sil"], n["ada"], n["cg"]

                def ada_slot(a, kc, i):
                    dve.wait_ge(ada_loaded[a % ADA_RING], 16 * (a // ADA_RING + 1) + 64 * i)
                    if kc == 0:
                        op = v.tensor_scalar(ada_acc[:, :], ada_raw[a % ADA_RING][:, :], cond[:, 0:1], None, ALU.mult)
                    else:
                        dve.wait_ge(sm.ada_used, a + 8 * i)
                        op = v.scalar_tensor_tensor(ada_acc[:, :], ada_raw[a % ADA_RING][:, :], cond[:, kc:kc + 1],
                                                    ada_acc[:, :], ALU.mult, ALU.add)
                    op.then_inc(sm.ada_used, 1)

                def ada_out(g, i):
                    dve.wait_ge(sm.ada_sum, cg + g + 1 + i)
                    v.tensor_tensor(mod[ahead % 2][:, bass.ds(8 * g + 8 * i, 8)], bank[7][:, 0:8],
                                    co[:, bass.ds(COLS["ada_b"][0] + 48 * ahead + 8 * g + 8 * i, 8)],
                                    ALU.add).then_inc(sm.ada_mod, 1)

                def up(q, i):
                    dve.wait_ge(sm.sil_done, s0 + q + 1 + 4 * i)
                    dve.wait_ge(sm.slot_used, k + 2 * q + 2 + 8 * i)
                    v.tensor_tensor(sil[q % 2], bank[(mt + 2 * q + 1) % 4][:, :], sil[q % 2],
                                    ALU.mult).then_inc(sm.lin_free, 2)
                    dve.wait_ge(sm.part_hi, p0 + q + 1 + 4 * i)
                    v.tensor_tensor(hid_lo[:, q + 4 * i, :], sil[q % 2], hid_hi[:, q + 4 * i, :].bitcast(F32),
                                    ALU.subtract).then_inc(sm.part_lo, 1)

                if ahead is not None and a0 == 0:
                    dve.wait_ge(sm.cond_done, 1)
                with dve.Fori(0, 5) as i:
                    for q in range(4):
                        if ahead is not None:
                            ada_slot(a0 + 2 * q, 2 * q, i)
                            ada_slot(a0 + 2 * q + 1, 2 * q + 1, i)
                        up(q, i)
                    if ahead is not None:
                        ada_out(0, i)
                for q in range(20, 22):
                    if ahead is not None:
                        for kc in range(4 * (q - 20), 4 * (q - 20) + 4):
                            ada_slot(a0 + 40 + kc, kc, 0)
                    up(q, 0)
                if ahead is not None:
                    ada_out(5, 0)
                    n.add(ada=48, cg=6)
                    dve.wait_ge(sm.ada_mod, n["cg"])
                    more = mod[ahead % 2][:, :].rearrange("p (s k) -> p s k", s=2)[:, :, 8:24]
                    link(v.tensor_scalar(more, more, 1.0, None, ALU.add))
                n.add(slot=2 * FT, mt=2 * FT, part=FT, sil=FT)
                add_residual(3, layer, 1, sum_down)

            sil = [lc[:, r * S:(r + 1) * S] for r in range(2)]
            dve.wait_ge(sm.const_loaded, 48)
            for at, part in enumerate(parts):
                tiles, values = IN_PROJ[part]
                layer = None if part == "first" else part
                n.add(lc=2 if part == "first" else 1)
                if part == "first":
                    rms_input("g_mix")
                    dve.wait_ge(sm.gate_in, 1)
                    v.tensor_tensor(gates.rearrange("p (t g) -> p t g", t=TT),
                                    bank[6][:, 0:48].rearrange("p (t g) -> p t g", t=TT),
                                    col("b_gate", 0, 12).unsqueeze(1).to_broadcast([P, TT, 12]),
                                    ALU.add).then_inc(sm.gate_pre, 1)
                    keep(len(tiles), [], first_between)
                    first_values()
                else:
                    modulated_input(layer, 0, last_gain)
                    vals = {0: ml_v, 1: swa_v, 2: hg_v, 3: df_v}[part]
                    keep(len(tiles), [swa_v[:, :, :]] if part == 1 else
                         [vals[:, t, g * S:(g + 1) * S] for g in range(D // S) for t in range(TT)],
                         {0: mlstm_gates, 1: rope_between, 2: hgrn_gates, 3: rope_between}.get(part, lambda t: None), part == 3)
                dve.wait_ge(sm.layer_const_loaded, 16 * n["lc"])
                if part == "first":
                    first_mixer()
                elif part == 0:
                    mlstm()
                elif part == 1:
                    dve.wait_ge(sm.rope_out, n["rope"])
                    for g in range(2):
                        for b in (0, HD):
                            op = v.tensor_copy(swa_k[b:b + HD, g, :], proj[HD * g:HD * g + HD, 8, :])
                    op.then_inc(sm.mix_ready, 1)
                    attention(swa_jobs(), AT["late"])
                elif part == 2:
                    hgrn()
                else:
                    lambdas()
                    dve.wait_ge(sm.rope_out, n["rope"])
                    v.tensor_copy(lam_w[:, 4:5], eps6).then_inc(sm.mix_ready, 1)
                    attention(diff_jobs(), AT["late"])
                wait(dve, sm.att_out, n["att_g"])
                if out_norms(part):
                    group_norms(out_norms(part))
                else:
                    for c in range(DT):
                        low(c, proj[:, c, :])
                add_residual(1, layer, 0, sum_out)
                if part == "first":
                    rms_input("g_ffn")
                else:
                    centre(part, 1, 2 * part)
                    modulated_input(layer, 1, 2 * part)
                ffn(parts[at + 1] if at + 1 < len(parts) else None, layer)
                last_gain = None
                if part != "first":
                    last_gain = 2 * part + 1
                    if at + 1 < len(parts):
                        centre(parts[at + 1], 0, last_gain)
                    else:
                        centre()
            for c in range(DT if last_gain is not None else 0):
                normed_tile(c, last_gain)


def slot_rows(w, columns):
    rows = w.shape[0] // P
    slots = []
    for c in columns:
        t = w[:, c:c + P].reshape(rows, P, P).transpose(1, 0, 2)
        for r in range(0, rows, 8):
            s = np.zeros((P, 8, P), w.dtype)
            s[:, 0:min(8, rows - r), :] = t[:, r:r + 8, :]
            slots.append(s.reshape(P, SLOT))
    return slots


def weight_stream(a, parts):
    out = []
    every = [j * P for j in range(DT)]
    for part in parts:
        if part == "first":
            w_in, w_out, gate, up, down = (a[k][0] for k in ("w_in", "w_out", "w_gate", "w_up", "w_down"))
        else:
            name = ("mlstm", "swa", "hgrn", "diff")[part]
            w_in, w_out = a[f"{name}_w_in_2"][0], a[f"{name}_w_out_2"][0]
            both, down = a["ffn_w_in_2"][part], a["ffn_w_out_2"][part]
            gate, up = both[:, :FF], both[:, FF:]
        tiles, values = IN_PROJ[part]
        out += slot_rows(w_in, tiles)
        kinds = {"v": slot_rows(w_in, values) if len(values) < TT else []}
        if len(values) >= TT:
            for g in range(0, len(values), TT):
                w = np.concatenate([w_in[:, c:c + P] for c in values[g:g + TT]], 1)
                kinds["v"] += list(w.reshape(TT, 2, P, S).transpose(0, 2, 1, 3).reshape(TT, P, SLOT))
        if part == "first":
            kinds["b"] = [t for w in ("w1_k_cmp", "w1_v_cmp") for t in slot_rows(a[w][0], [0, P])]
            out += [kinds[kind].pop(0) for kind in VALUES_AND_BLOCKS]
        else:
            out += kinds["v"]
        out += slot_rows(w_out, every)
        hidden = [j * P for j in range(FT)]
        for g, u in zip(slot_rows(gate, hidden), slot_rows(up, hidden)):
            out += [g, u]
        out += slot_rows(down, every)
    return np.stack(out)


def ada_stream(w, parts):
    layers = [p for p in parts[1:]]
    if not layers:
        return np.zeros((1, P, SLOT), np.float32)
    return np.stack([w[p, s, c * P:(c + 1) * P, g * SLOT:(g + 1) * SLOT]
                     for p in layers for s in range(2) for g in range(3) for c in range(DT)])


def column_pack(a):
    def tiles(v):
        return v.reshape(-1, P).T

    def twice(v):
        return np.concatenate([v, v])[:, None]

    def spread(v):
        return np.broadcast_to(v.reshape(1, -1), (P, v.size))

    def by_tile(w):
        return w.reshape(-1, P, w.shape[1]).transpose(1, 0, 2).reshape(P, -1)

    pe = np.concatenate([a[k][0].reshape(16, 2, HD).transpose(2, 1, 0).reshape(HD, 32) for k in ("pe_k_cmp", "pe_v_cmp")])
    mb = np.zeros((P, 2), np.float32)
    mb[0:4, :] = a["mlstm_b_gate_2"][0].reshape(2, 4).T
    pack = {
        "g_mix": tiles(a["g_mix"][0]), "g_ffn": tiles(a["g_ffn"][0]), "g_out": tiles(a["g_out"][0]),
        "g_q_nsa": twice(a["g_q_nsa"][0]), "g_k_slc": twice(a["g_k_slc"][0]), "g_k_win": twice(a["g_k_win"][0]),
        "g_k_cmp": twice(a["g_k_cmp"][0]), "g_q_dil": twice(a["g_q_dil"][0]), "g_k_dil": twice(a["g_k_dil"][0]),
        "conv_w": a["conv_w"][0].T.reshape(2, P, 3).transpose(1, 0, 2).reshape(P, 6), "pe": pe,
        "gate_w": by_tile(a["w_in"][0][:, C_GT:C_GT + 12]), "b_gate": spread(a["b_gate"][0]),
        "w2": np.concatenate([by_tile(a["w2_k_cmp"][0]), by_tile(a["w2_v_cmp"][0])], 1),
        "c": tiles(a["c_2"]), "ada_b": tiles(a["ada_b_2"]), "ln_g": tiles(a["ln_g_2"]), "ln_b": tiles(a["ln_b_2"]),
        "mlstm_gw": by_tile(a["mlstm_w_in_2"][0][:, 3072:3080]), "mlstm_b": mb,
        "mlstm_norm": tiles(a["mlstm_norm_2"][0]), "sinks": spread(a["swa_sinks_2"][0]),
        "lower": tiles(a["hgrn_lower_bounds_2"]), "hgrn_norm": tiles(a["hgrn_norm_2"][0]),
        "diff_norm": a["diff_norm_2"][0][:, None], "diff_lambda": spread(a["diff_lambda_2"][0]),
    }
    return np.ascontiguousarray(np.concatenate([pack[name] for name in COLS], 1))


def kernel(**inputs):
    import concourse.bacc as bacc
    from concourse.bass_utils import run_bass_kernel_spmd

    a = {k: np.asarray(v) for k, v in inputs.items()}
    kept, big, layer = constants()
    arrays = {
        "x_t": np.ascontiguousarray(a["x"][0].T.reshape(DT, P, S).transpose(1, 0, 2)),
        "weights": weight_stream(a, PARTS), "ada": ada_stream(a["ada_w_2"], PARTS), "columns": column_pack(a),
        "kept_const": kept, "big_const": big, "layer_const": layer,
        "positions": np.ascontiguousarray(np.broadcast_to(a["positions_2"], (P, S))),
    }
    nc = bacc.Bacc("TRN2", target_bir_lowering=False, num_devices=1)
    args = [nc.dram_tensor(name, v.shape, mybir.dt.from_np(v.dtype), kind="ExternalInput").ap()
            for name, v in arrays.items()]
    out = nc.dram_tensor("y_t", (P, DT, S), F32, kind="ExternalOutput").ap()
    program(nc, *args, out, PARTS)
    r = run_bass_kernel_spmd(nc, [arrays], core_ids=[0])
    y = r.results[0]["y_t"]
    return np.ascontiguousarray(y.transpose(1, 0, 2).reshape(D, S).T)[None]
```
